# Optimizing a Trainium2 kernel written in Bass

```python
import math
import jax
import jax.numpy as jnp
from jax import lax

D_MODEL = 1024
BATCH = 1
SEQ = 256
DEPTH = 2

GRID_W = 64
CTX_LEN = 256
N_EVEN = (DEPTH + 1) // 2
N_ODD = DEPTH // 2

MLSTM_HEADS = 4
MLSTM_DQK = 64
MLSTM_DV = 128
MLSTM_CHUNK = 64
HGRN_HEADS = 4
HGRN_DK = 128
HGRN_DV = 128
HGRN_CHUNK = 32
HYENA_WIDTH = 512
HYENA_GROUPS = 8
HYENA_ORDER = 2
HYENA_EMB = 33
HYENA_FILTER_HIDDEN = 64
HYENA_SHORT = 3
HYENA_TARGET = 1e-2
HYENA_FAST_PCT = 0.3
HYENA_SLOW_PCT = 1.5
RET_HEADS = 4
RET_DQK = 128
RET_DV = 128
RET_CHUNK = 64
ROPE_BASE = 10000.0
N_EXPERTS = 64
TOP_K = 8
EXPERT_HIDDEN = 256
SHARED_HIDDEN = 256
ROUTED_SCALE = 2.5
MOE_BLOCK = 128
DEEPNORM_ALPHA = (2 * DEPTH) ** 0.25
DEEPNORM_BETA = (8 * DEPTH) ** -0.25
EPS = 1e-5
NEG_BIG = -1e30

MLSTM_SPLITS = (MLSTM_HEADS * MLSTM_DQK, MLSTM_HEADS * MLSTM_DQK, MLSTM_HEADS * MLSTM_DV, MLSTM_HEADS * MLSTM_DV, 4 * MLSTM_HEADS)
HGRN_SPLITS = (HGRN_HEADS * HGRN_DK, HGRN_HEADS * HGRN_DV, HGRN_HEADS * HGRN_DK, HGRN_HEADS * HGRN_DK, HGRN_HEADS * HGRN_DV)
EVEN_SPLITS = MLSTM_SPLITS + HGRN_SPLITS
EVEN_PROJ = sum(EVEN_SPLITS)
EVEN_MIX = MLSTM_HEADS * MLSTM_DV + HGRN_HEADS * HGRN_DV
RET_SPLITS = (RET_HEADS * RET_DQK, RET_HEADS * RET_DQK, RET_HEADS * RET_DV, RET_HEADS * RET_DV)
ODD_SPLITS = ((HYENA_ORDER + 1) * HYENA_WIDTH,) + RET_SPLITS
ODD_PROJ = sum(ODD_SPLITS)
ODD_MIX = HYENA_WIDTH + RET_HEADS * RET_DV

F32 = jnp.float32

kernel_name = 'hybrid_mlstm_hgrn2_hyena_retention_moe'

def split_cols(a, sizes):
    out, start = [], 0
    for s in sizes:
        out.append(a[..., start:start + s])
        start += s
    return out

def to_heads(a, n_heads):
    b, l, w = a.shape
    return a.reshape(b, l, n_heads, w // n_heads).transpose(0, 2, 1, 3)

def chunk(a, cs):
    b, h, l = a.shape[:3]
    return a.reshape((b, h, l // cs, cs) + a.shape[3:])

def layer_norm(x, w, b):
    xf = x.astype(F32)
    mu = jnp.mean(xf, -1, keepdims=True)
    var = jnp.mean(jnp.square(xf - mu), -1, keepdims=True)
    return ((xf - mu) * lax.rsqrt(var + EPS) * w + b).astype(x.dtype)

def head_norm(h, w, rms):
    h = h.transpose(0, 2, 1, 3)
    if not rms:
        h = h - jnp.mean(h, -1, keepdims=True)
    h = h * lax.rsqrt(jnp.mean(jnp.square(h), -1, keepdims=True) + EPS)
    b, l, nh, dh = h.shape
    return h.reshape(b, l, nh * dh) * w

def group_rms(z, w):
    b, l, wd = z.shape
    zg = z.reshape(b, l, HYENA_GROUPS, wd // HYENA_GROUPS)
    zg = zg * lax.rsqrt(jnp.mean(jnp.square(zg), -1, keepdims=True) + EPS)
    return zg.reshape(b, l, wd) * w

def run_direction(scan_fn, ctx_seq, lat_seq, const, state0, reverse):
    if reverse:
        ctx_seq = tuple(jnp.flip(a, axis=2) for a in ctx_seq)
        lat_seq = tuple(jnp.flip(a, axis=2) for a in lat_seq)
    y_ctx, state = scan_fn(ctx_seq, const, state0)
    y_lat, _ = scan_fn(lat_seq, const, state)
    if reverse:
        y_ctx = jnp.flip(y_ctx, axis=2)
        y_lat = jnp.flip(y_lat, axis=2)
    return y_lat, y_ctx

def mlstm_scan(seq, const, state):
    q, k, v, ig, lf = seq
    cs = MLSTM_CHUNK
    qc, kc, vc, igc, lfc = (chunk(a, cs) for a in seq)
    b = jnp.cumsum(lfc, axis=-1)
    g = b[..., -1]
    a = g[..., None] - b + igc
    m_loc = jnp.max(a, axis=-1)
    w = jnp.exp(a - m_loc[..., None])
    c_loc = jnp.einsum('bhcs,bhcsv,bhcsk->bhcvk', w, vc, kc)
    n_loc = jnp.einsum('bhcs,bhcsk->bhck', w, kc)

    def step(carry, inp):
        c_st, n_st, m_st = carry
        g_j, ml_j, cl_j, nl_j = inp
        m_new = jnp.maximum(g_j + m_st, ml_j)
        sp = jnp.exp(g_j + m_st - m_new)
        sl = jnp.exp(ml_j - m_new)
        new = (sp[..., None, None] * c_st + sl[..., None, None] * cl_j, sp[..., None] * n_st + sl[..., None] * nl_j, m_new)
        return new, carry

    final, (c_in, n_in, m_in) = lax.scan(step, state, tuple(jnp.moveaxis(t, 2, 0) for t in (g, m_loc, c_loc, n_loc)))
    c_in, n_in, m_in = jnp.moveaxis(c_in, 0, 2), jnp.moveaxis(n_in, 0, 2), jnp.moveaxis(m_in, 0, 2)
    tri = jnp.tril(jnp.ones((cs, cs), bool))
    log_d = jnp.where(tri, b[..., :, None] - b[..., None, :] + igc[..., None, :], -jnp.inf)
    inter = b + m_in[..., None]
    m_out = jnp.maximum(inter, jnp.max(log_d, -1))
    s = jnp.einsum('bhctk,bhcsk->bhcts', qc, kc) * jnp.exp(log_d - m_out[..., None])
    e_int = jnp.exp(inter - m_out)
    num = jnp.einsum('bhcts,bhcsv->bhctv', s, vc) + e_int[..., None] * jnp.einsum('bhctk,bhcvk->bhctv', qc, c_in)
    den = jnp.sum(s, -1) + e_int * jnp.einsum('bhctk,bhck->bhct', qc, n_in)
    h = num / jnp.maximum(jnp.abs(den), jnp.exp(-m_out))[..., None]
    return h.reshape(v.shape), final

def hgrn2_scan(seq, const, state):
    q, k, v, lf = seq
    cs = HGRN_CHUNK
    qc, kc, vc, lfc = (chunk(a, cs) for a in seq)
    a_cum = jnp.cumsum(lfc, axis=3)
    a_end = a_cum[:, :, :, -1]
    s_loc = jnp.einsum('bhcsk,bhcsv->bhckv', kc * jnp.exp(a_end[:, :, :, None] - a_cum), vc)

    def step(s_st, inp):
        a_j, sl_j = inp
        return jnp.exp(a_j)[..., None] * s_st + sl_j, s_st

    final, s_in = lax.scan(step, state, (jnp.moveaxis(a_end, 2, 0), jnp.moveaxis(s_loc, 2, 0)))
    s_in = jnp.moveaxis(s_in, 0, 2)
    inter = jnp.einsum('bhctk,bhckv->bhctv', qc * jnp.exp(a_cum), s_in)
    a_mid = a_cum[:, :, :, cs // 2 - 1:cs // 2]
    tri = jnp.tril(jnp.ones((cs, cs), bool))
    sc = jnp.einsum('bhctk,bhcsk->bhcts', qc * jnp.exp(a_cum - a_mid), kc * jnp.exp(a_mid - a_cum))
    sc = jnp.where(tri, sc, 0.0)
    out = inter + jnp.einsum('bhcts,bhcsv->bhctv', sc, vc)
    return out.reshape(v.shape), final

def retention_scan(seq, log_gamma, state):
    q, k, v = seq
    cs = RET_CHUNK
    qc, kc, vc = (chunk(a, cs) for a in seq)
    pos = jnp.arange(cs, dtype=F32)
    tri = jnp.tril(jnp.ones((cs, cs), bool))
    delta = pos[:, None] - pos[None, :]
    decay = jnp.exp(jnp.where(tri, delta[None] * log_gamma[:, None, None], -jnp.inf))
    sc = jnp.einsum('bhctk,bhcsk->bhcts', qc, kc) * decay[:, None]
    intra = jnp.einsum('bhcts,bhcsv->bhctv', sc, vc)
    q_dec = jnp.exp((pos + 1.0)[None, :] * log_gamma[:, None])
    k_dec = jnp.exp((cs - 1.0 - pos)[None, :] * log_gamma[:, None])
    s_loc = jnp.einsum('bhcsk,hs,bhcsv->bhckv', kc, k_dec, vc)
    chunk_decay = jnp.exp(cs * log_gamma)[None, :, None, None]

    def step(s_st, sl_j):
        return chunk_decay * s_st + sl_j, s_st

    final, s_in = lax.scan(step, state, jnp.moveaxis(s_loc, 2, 0))
    s_in = jnp.moveaxis(s_in, 0, 2)
    inter = jnp.einsum('bhctk,ht,bhckv->bhctv', qc, q_dec, s_in)
    return (inter + intra).reshape(v.shape), final

def rope_1d(x, pos):
    d = x.shape[-1]
    inv = ROPE_BASE ** (-jnp.arange(0, d, 2, dtype=F32) / d)
    ang = pos[:, None] * inv[None, :]
    cos = jnp.cos(ang)[None, :, None, :]
    sin = jnp.sin(ang)[None, :, None, :]
    x1, x2 = x[..., :d // 2], x[..., d // 2:]
    return jnp.concatenate([x1 * cos - x2 * sin, x1 * sin + x2 * cos], -1)

def axial_rope(x, row, col):
    half = x.shape[-1] // 2
    return jnp.concatenate([rope_1d(x[..., :half], row), rope_1d(x[..., half:], col)], -1)

def mlstm_group(cols_lat, cols_ctx, gate_b, norm_w):
    def prep(cols):
        q, k, v, o, gates = cols
        b, l, _ = q.shape
        q = to_heads(q, MLSTM_HEADS) * MLSTM_DQK ** -0.5
        k = to_heads(k, MLSTM_HEADS)
        v = to_heads(v, MLSTM_HEADS)
        gates = (gates.reshape(b, l, 4, MLSTM_HEADS) + gate_b).transpose(2, 0, 3, 1)
        fwd = (q, k, v, gates[0], jax.nn.log_sigmoid(gates[1]))
        bwd = (q, k, v, gates[2], jax.nn.log_sigmoid(gates[3]))
        return fwd, bwd, o

    fwd_l, bwd_l, o_l = prep(cols_lat)
    fwd_c, bwd_c, o_c = prep(cols_ctx)
    batch = o_l.shape[0]
    state0 = (jnp.zeros((batch, MLSTM_HEADS, MLSTM_DV, MLSTM_DQK), F32),
              jnp.zeros((batch, MLSTM_HEADS, MLSTM_DQK), F32),
              jnp.full((batch, MLSTM_HEADS), NEG_BIG, F32))
    hf_lat, hf_ctx = run_direction(mlstm_scan, fwd_c, fwd_l, None, state0, False)
    hb_lat, hb_ctx = run_direction(mlstm_scan, bwd_c, bwd_l, None, state0, True)
    y_lat = head_norm(hf_lat + hb_lat, norm_w, False) * jax.nn.sigmoid(o_l)
    y_ctx = head_norm(hf_ctx + hb_ctx, norm_w, False) * jax.nn.sigmoid(o_c)
    return y_lat, y_ctx

def hgrn_group(cols_lat, cols_ctx, lb, norm_w):
    def prep(cols):
        q, i, f_fwd, f_bwd, g = cols
        q = to_heads(jax.nn.silu(q), HGRN_HEADS)
        v = to_heads(i, HGRN_HEADS)

        def gate(fp):
            f = lb + (1.0 - lb) * jax.nn.sigmoid(fp)
            return to_heads(1.0 - f, HGRN_HEADS), to_heads(jnp.log(f), HGRN_HEADS)

        k_f, lf_f = gate(f_fwd)
        k_b, lf_b = gate(f_bwd)
        return (q, k_f, v, lf_f), (q, k_b, v, lf_b), g

    fwd_l, bwd_l, g_l = prep(cols_lat)
    fwd_c, bwd_c, g_c = prep(cols_ctx)
    state0 = jnp.zeros((g_l.shape[0], HGRN_HEADS, HGRN_DK, HGRN_DV), F32)
    yf_lat, yf_ctx = run_direction(hgrn2_scan, fwd_c, fwd_l, None, state0, False)
    yb_lat, yb_ctx = run_direction(hgrn2_scan, bwd_c, bwd_l, None, state0, True)
    y_lat = head_norm(yf_lat + yb_lat, norm_w, True) * jax.nn.silu(g_l)
    y_ctx = head_norm(yf_ctx + yb_ctx, norm_w, True) * jax.nn.silu(g_c)
    return y_lat, y_ctx

def hyena_filters(length, fw1, fb1, fw2, fb2, fw3, fb3, freq, wout):
    pos = jnp.arange(length, dtype=F32)
    t = (pos / max(length - 1, 1))[:, None]
    bands = (HYENA_EMB - 1) // 2
    w = 2.0 * math.pi * pos[:, None] / length * jnp.linspace(1e-4, bands - 1, bands)[None, :]
    z = jnp.concatenate([t, jnp.cos(w), jnp.sin(w)], -1)
    hid = jnp.sin(freq * (z @ fw1 + fb1))
    hid = jnp.sin(freq * (hid @ fw2 + fb2))
    hid = jnp.sin(freq * (hid @ fw3 + fb3))
    h = (hid @ wout).reshape(length, HYENA_ORDER, 2, HYENA_WIDTH)
    deltas = jnp.abs(jnp.linspace(math.log(HYENA_TARGET) / HYENA_SLOW_PCT, math.log(HYENA_TARGET) / HYENA_FAST_PCT, HYENA_WIDTH))
    decay = jnp.exp(-t * deltas[None, :])
    return (h * decay[:, None, None, :]).transpose(1, 2, 0, 3)

def bidir_fftconv(u, h_fwd, h_bwd, d_skip):
    length, width = h_fwd.shape
    kern = jnp.concatenate([h_fwd, jnp.zeros((1, width), F32), jnp.flip(h_bwd[1:], axis=0)], axis=0)
    spec = jnp.fft.rfft(u, n=2 * length, axis=1) * jnp.fft.rfft(kern, axis=0)[None]
    y = jnp.fft.irfft(spec, n=2 * length, axis=1)[:, :length]
    return y + u * d_skip

def hyena_group(u_lat, u_ctx, conv_w, conv_b, fw1, fb1, fw2, fb2, fw3, fb3, freq, wout, skip, norm_w):
    def run(u):
        length = u.shape[1]
        up = jnp.pad(u, ((0, 0), (1, 1), (0, 0)))
        u = up[:, :-2] * conv_w[0] + up[:, 1:-1] * conv_w[1] + up[:, 2:] * conv_w[2] + conv_b
        streams = jnp.split(u, HYENA_ORDER + 1, axis=-1)
        gates, z = streams[:-1], streams[-1]
        h = hyena_filters(length, fw1, fb1, fw2, fb2, fw3, fb3, freq, wout)
        for n in range(HYENA_ORDER):
            z = gates[n] * bidir_fftconv(z, h[n, 0], h[n, 1], skip[n])
        return group_rms(z, norm_w)

    return run(u_lat), run(u_ctx)

def retention_group(cols_lat, cols_ctx, log_decay, norm_w, row, col):
    def prep(cols, rotary):
        q, k, v, g = cols
        b, l, _ = q.shape
        q = q.reshape(b, l, RET_HEADS, RET_DQK)
        k = k.reshape(b, l, RET_HEADS, RET_DQK)
        if rotary:
            q = axial_rope(q, row, col)
            k = axial_rope(k, row, col)
        q = q.transpose(0, 2, 1, 3)
        k = k.transpose(0, 2, 1, 3) * RET_DQK ** -0.5
        return (q, k, to_heads(v, RET_HEADS)), g

    lat, g_l = prep(cols_lat, True)
    ctx, g_c = prep(cols_ctx, False)
    state0 = jnp.zeros((g_l.shape[0], RET_HEADS, RET_DQK, RET_DV), F32)
    yf_lat, yf_ctx = run_direction(retention_scan, ctx, lat, log_decay[0], state0, False)
    yb_lat, yb_ctx = run_direction(retention_scan, ctx, lat, log_decay[1], state0, True)
    y_lat = head_norm(yf_lat + yb_lat, norm_w, False) * jax.nn.silu(g_l)
    y_ctx = head_norm(yf_ctx + yb_ctx, norm_w, False) * jax.nn.silu(g_c)
    return y_lat, y_ctx

def even_mixer(u_lat, u_ctx, w_in, gate_b, mlstm_norm_w, lb, hgrn_norm_w, w_out):
    w_in = w_in.astype(F32)
    w_out = w_out.astype(F32)
    p_lat = split_cols(u_lat.astype(F32) @ w_in, EVEN_SPLITS)
    p_ctx = split_cols(u_ctx.astype(F32) @ w_in, EVEN_SPLITS)
    n_a = len(MLSTM_SPLITS)
    a_lat, a_ctx = mlstm_group(p_lat[:n_a], p_ctx[:n_a], gate_b.astype(F32), mlstm_norm_w.astype(F32))
    b_lat, b_ctx = hgrn_group(p_lat[n_a:], p_ctx[n_a:], lb, hgrn_norm_w.astype(F32))
    return jnp.concatenate([a_lat, b_lat], -1) @ w_out, jnp.concatenate([a_ctx, b_ctx], -1) @ w_out

def odd_mixer(u_lat, u_ctx, w_in, hyena_p, log_decay, ret_norm_w, w_out, row, col):
    w_in = w_in.astype(F32)
    w_out = w_out.astype(F32)
    p_lat = split_cols(u_lat.astype(F32) @ w_in, ODD_SPLITS)
    p_ctx = split_cols(u_ctx.astype(F32) @ w_in, ODD_SPLITS)
    hy_lat, hy_ctx = hyena_group(p_lat[0], p_ctx[0], *[p.astype(F32) for p in hyena_p])
    r_lat, r_ctx = retention_group(p_lat[1:], p_ctx[1:], log_decay.astype(F32), ret_norm_w.astype(F32), row, col)
    return jnp.concatenate([hy_lat, r_lat], -1) @ w_out, jnp.concatenate([hy_ctx, r_ctx], -1) @ w_out

def moe_ffn(t, router_w, router_bias, w1, w3, w2, sw1, sw3, sw2):
    n_tok, d = t.shape
    tf = t.astype(F32)
    scores = jax.nn.sigmoid(tf @ router_w.astype(F32))
    _, idx = lax.top_k(scores + router_bias.astype(F32), TOP_K)
    gate = jnp.take_along_axis(scores, idx, axis=1)
    gate = ROUTED_SCALE * gate / jnp.sum(gate, -1, keepdims=True)
    n_assign = n_tok * TOP_K
    e_flat = idx.reshape(-1)
    g_flat = gate.reshape(-1)
    tok_flat = jnp.arange(n_assign, dtype=jnp.int32) // TOP_K
    order = jnp.argsort(e_flat)
    e_s, tok_s, g_s = e_flat[order], tok_flat[order], g_flat[order]
    counts = jnp.bincount(e_flat, length=N_EXPERTS)
    padded = (counts + MOE_BLOCK - 1) // MOE_BLOCK * MOE_BLOCK
    start = jnp.cumsum(counts) - counts
    pend = jnp.cumsum(padded)
    pstart = pend - padded
    dest = pstart[e_s] + jnp.arange(n_assign, dtype=jnp.int32) - start[e_s]
    n_blocks = -(-(n_assign + N_EXPERTS * (MOE_BLOCK - 1)) // MOE_BLOCK)
    slot_tok = jnp.full((n_blocks * MOE_BLOCK,), n_tok, jnp.int32).at[dest].set(tok_s)
    slot_gate = jnp.zeros((n_blocks * MOE_BLOCK,), F32).at[dest].set(g_s)
    block_e = jnp.minimum(jnp.searchsorted(pend, jnp.arange(n_blocks, dtype=jnp.int32) * MOE_BLOCK, side='right'), N_EXPERTS - 1)
    t_ext = jnp.concatenate([tf, jnp.zeros((1, d), F32)], 0)

    def expert_block(acc, blk):
        tok, g, e = blk
        xb = t_ext[tok]
        hb = jax.nn.silu(xb @ w1[e]) * (xb @ w3[e])
        return acc.at[tok].add((hb @ w2[e]) * g[:, None]), None

    acc, _ = lax.scan(expert_block, jnp.zeros((n_tok + 1, d), F32),
                      (slot_tok.reshape(n_blocks, MOE_BLOCK), slot_gate.reshape(n_blocks, MOE_BLOCK), block_e))
    shared = (jax.nn.silu(tf @ sw1) * (tf @ sw3)) @ sw2
    return acc[:n_tok] + shared

def setup_inputs(seed: int = 0) -> dict:
    key = jax.random.key(seed)
    keys = iter(jax.random.split(key, 48))

    def nrm(shape, scale=1.0):
        return scale * jax.random.normal(next(keys), shape, F32)

    d = D_MODEL
    hfh = HYENA_FILTER_HIDDEN
    hyw = (HYENA_ORDER + 1) * HYENA_WIDTH
    f_bias = jnp.linspace(3.0, 6.0, MLSTM_HEADS)
    gate_base = jnp.stack([jnp.zeros(MLSTM_HEADS), f_bias, jnp.zeros(MLSTM_HEADS), f_bias])
    ret_base = jnp.log(1.0 - 2.0 ** (-5.0 - jnp.arange(RET_HEADS, dtype=F32)))
    return {
        'x': nrm((BATCH, SEQ, d)),
        'c': nrm((BATCH, d)),
        'ctx': nrm((BATCH, CTX_LEN, d)),
        'c_ctx': nrm((d,)),
        'ada_w': nrm((DEPTH, d, 6 * d), d ** -0.5),
        'ada_b': nrm((DEPTH, 6 * d), 0.02),
        'ln_w': 1.0 + nrm((DEPTH, 2, d), 0.02),
        'ln_b': nrm((DEPTH, 2, d), 0.02),
        'even_w_in': nrm((N_EVEN, d, EVEN_PROJ), d ** -0.5),
        'mlstm_gate_b': gate_base + nrm((N_EVEN, 4, MLSTM_HEADS), 0.1),
        'mlstm_norm_w': 1.0 + nrm((N_EVEN, MLSTM_HEADS * MLSTM_DV), 0.02),
        'hgrn_lb': nrm((N_EVEN, HGRN_HEADS * HGRN_DK), 1.0),
        'hgrn_norm_w': 1.0 + nrm((N_EVEN, HGRN_HEADS * HGRN_DV), 0.02),
        'even_w_out': nrm((N_EVEN, EVEN_MIX, d), DEEPNORM_BETA * EVEN_MIX ** -0.5),
        'odd_w_in': nrm((N_ODD, d, ODD_PROJ), d ** -0.5),
        'hy_conv_w': nrm((N_ODD, HYENA_SHORT, hyw), HYENA_SHORT ** -0.5),
        'hy_conv_b': nrm((N_ODD, hyw), 0.02),
        'hy_f_w1': nrm((N_ODD, HYENA_EMB, hfh), HYENA_EMB ** -0.5),
        'hy_f_b1': nrm((N_ODD, hfh), 0.1),
        'hy_f_w2': nrm((N_ODD, hfh, hfh), hfh ** -0.5),
        'hy_f_b2': nrm((N_ODD, hfh), 0.1),
        'hy_f_w3': nrm((N_ODD, hfh, hfh), hfh ** -0.5),
        'hy_f_b3': nrm((N_ODD, hfh), 0.1),
        'hy_f_freq': 1.0 + nrm((N_ODD, hfh), 0.02),
        'hy_f_wout': nrm((N_ODD, hfh, HYENA_ORDER * 2 * HYENA_WIDTH), hfh ** -0.5),
        'hy_skip': nrm((N_ODD, HYENA_ORDER, HYENA_WIDTH), 1.0),
        'hy_norm_w': 1.0 + nrm((N_ODD, HYENA_WIDTH), 0.02),
        'ret_log_decay': ret_base * (1.0 + nrm((N_ODD, 2, RET_HEADS), 0.05)),
        'ret_norm_w': 1.0 + nrm((N_ODD, RET_HEADS * RET_DV), 0.02),
        'odd_w_out': nrm((N_ODD, ODD_MIX, d), DEEPNORM_BETA * ODD_MIX ** -0.5),
        'router_w': nrm((DEPTH, d, N_EXPERTS), d ** -0.5),
        'router_bias': nrm((DEPTH, N_EXPERTS), 0.01),
        'exp_w1': nrm((DEPTH, N_EXPERTS, d, EXPERT_HIDDEN), d ** -0.5),
        'exp_w3': nrm((DEPTH, N_EXPERTS, d, EXPERT_HIDDEN), d ** -0.5),
        'exp_w2': nrm((DEPTH, N_EXPERTS, EXPERT_HIDDEN, d), DEEPNORM_BETA * EXPERT_HIDDEN ** -0.5),
        'sh_w1': nrm((DEPTH, d, SHARED_HIDDEN), d ** -0.5),
        'sh_w3': nrm((DEPTH, d, SHARED_HIDDEN), d ** -0.5),
        'sh_w2': nrm((DEPTH, SHARED_HIDDEN, d), DEEPNORM_BETA * SHARED_HIDDEN ** -0.5),
    }

def reference(x, c, ctx, c_ctx, ada_w, ada_b, ln_w, ln_b, even_w_in, mlstm_gate_b, mlstm_norm_w, hgrn_lb, hgrn_norm_w, even_w_out, odd_w_in, hy_conv_w, hy_conv_b, hy_f_w1, hy_f_b1, hy_f_w2, hy_f_b2, hy_f_w3, hy_f_b3, hy_f_freq, hy_f_wout, hy_skip, hy_norm_w, ret_log_decay, ret_norm_w, odd_w_out, router_w, router_bias, exp_w1, exp_w3, exp_w2, sh_w1, sh_w3, sh_w2):
    batch, n_lat, d = x.shape
    n_ctx = ctx.shape[1]
    rows = n_lat // GRID_W
    row = jnp.repeat(jnp.arange(rows, dtype=F32), GRID_W)
    col = jnp.tile(jnp.arange(GRID_W, dtype=F32), rows)
    sm = jax.nn.softmax(hgrn_lb.astype(F32), axis=0)
    lower_bounds = jnp.cumsum(sm, axis=0) - sm[0]
    c_act = jax.nn.silu(c.astype(F32))
    cc_act = jax.nn.silu(c_ctx.astype(F32))
    h_lat, h_ctx = x, ctx
    for l in range(DEPTH):
        last = l == DEPTH - 1
        ada_wl = ada_w[l].astype(F32)
        mod_lat = jnp.split((c_act @ ada_wl + ada_b[l])[:, None, :], 6, axis=-1)
        mod_ctx = jnp.split((cc_act @ ada_wl + ada_b[l])[None, None, :], 6, axis=-1)
        u_lat = h_lat * (1.0 + mod_lat[1]) + mod_lat[0]
        u_ctx = h_ctx * (1.0 + mod_ctx[1]) + mod_ctx[0]
        if l % 2 == 0:
            e = l // 2
            y_lat, y_ctx = even_mixer(u_lat, u_ctx, even_w_in[e], mlstm_gate_b[e], mlstm_norm_w[e], lower_bounds[e], hgrn_norm_w[e], even_w_out[e])
        else:
            o = l // 2
            hyena_p = (hy_conv_w[o], hy_conv_b[o], hy_f_w1[o], hy_f_b1[o], hy_f_w2[o], hy_f_b2[o], hy_f_w3[o], hy_f_b3[o], hy_f_freq[o], hy_f_wout[o], hy_skip[o], hy_norm_w[o])
            y_lat, y_ctx = odd_mixer(u_lat, u_ctx, odd_w_in[o], hyena_p, ret_log_decay[o], ret_norm_w[o], odd_w_out[o], row, col)
        h_lat = layer_norm(DEEPNORM_ALPHA * h_lat + (mod_lat[2] * y_lat).astype(h_lat.dtype), ln_w[l, 0], ln_b[l, 0])
        v_lat = (h_lat * (1.0 + mod_lat[4]) + mod_lat[3]).reshape(batch * n_lat, d)
        if last:
            f_lat = moe_ffn(v_lat, router_w[l], router_bias[l], exp_w1[l], exp_w3[l], exp_w2[l], sh_w1[l], sh_w3[l], sh_w2[l])
        else:
            h_ctx = layer_norm(DEEPNORM_ALPHA * h_ctx + (mod_ctx[2] * y_ctx).astype(h_ctx.dtype), ln_w[l, 0], ln_b[l, 0])
            v_ctx = (h_ctx * (1.0 + mod_ctx[4]) + mod_ctx[3]).reshape(batch * n_ctx, d)
            f_all = moe_ffn(jnp.concatenate([v_lat, v_ctx], 0), router_w[l], router_bias[l], exp_w1[l], exp_w3[l], exp_w2[l], sh_w1[l], sh_w3[l], sh_w2[l])
            f_lat = f_all[:batch * n_lat]
            f_ctx = f_all[batch * n_lat:].reshape(batch, n_ctx, d)
            h_ctx = layer_norm(DEEPNORM_ALPHA * h_ctx + (mod_ctx[5] * f_ctx).astype(h_ctx.dtype), ln_w[l, 1], ln_b[l, 1])
        h_lat = layer_norm(DEEPNORM_ALPHA * h_lat + (mod_lat[5] * f_lat.reshape(batch, n_lat, d)).astype(h_lat.dtype), ln_w[l, 1], ln_b[l, 1])
    return h_lat


_drawn_inputs = setup_inputs


def setup_inputs(seed=0):
    import zlib

    import numpy as np

    out = dict(_drawn_inputs(seed))
    spreads = {}
    factors = {'mlstm_norm_w': 3.916,
     'hgrn_norm_w': 3.216,
     'hy_conv_b': 2.806,
     'hy_f_freq': 3.25,
     'hy_norm_w': 11.99,
     'ret_norm_w': 20.515}
    for name, (base, spread) in spreads.items():
        noise = np.random.default_rng([zlib.crc32(name.encode()), seed]).standard_normal(out[name].shape)
        drawn = base * np.exp(spread * noise) if base else spread * noise
        out[name] = jnp.asarray(drawn.astype(out[name].dtype))
    for name, factor in factors.items():
        out[name] = (out[name] * factor).astype(out[name].dtype)
    return out
```

```python
import math
from contextlib import ExitStack

import numpy as np
import concourse.bass as bass
from concourse import mybir

P = 128
D = 1024
KT = D // P
T = 512
NT = T // P
CTX = 256
LAT = 256
TW = 512
HEADS = 4
CHUNK = 32
NCH = T // CHUNK
MODS = 6
EXPERTS = 64
TOPK = 8
HID = 256
ROUTED_SCALE = 2.5
ALPHA = 4.0 ** 0.25
EPS = 1e-5
NEG_BIG = -1e30
TINY = 2.0 ** -63
HYW = 512
HYHID = 64
HYEMB = 33
NFREQ = 256
GROUP = 64
W13 = 2 * KT * HID
WEXP = W13 + 2 * D
EVEN_GROUPS = ("qk", "v", "o", "hq", "hi", "ff", "fb", "hg")
ODD_GROUPS = ("gate0", "gate1", "z", "rq", "rk", "rv", "rg")

F32 = mybir.dt.float32
U32 = mybir.dt.uint32
ALU = mybir.AluOpType
ACT = mybir.ActivationFunctionType
AX = mybir.AxisListType


def shape_tables():
    i = np.arange(P)
    ident = np.eye(P, dtype=np.float32)
    upper = (i[:, None] <= i[None, :]).astype(np.float32)
    lower = (i[:, None] >= i[None, :]).astype(np.float32)
    same = (i[:, None] // CHUNK) == (i[None, :] // CHUNK)
    chunk_of = (i[:, None] // CHUNK == np.arange(P // CHUNK)[None, :]).astype(np.float32)
    base = np.concatenate([ident, upper, lower, upper * same, lower * same, chunk_of], axis=1)
    negsel = np.zeros((HEADS, HEADS, P), np.float32)
    for h in range(HEADS):
        negsel[h, h] = -1.0

    pos = np.arange(LAT, dtype=np.float32)
    inv = (np.float32(10000.0) ** (-np.arange(0, 64, 2, dtype=np.float32) / np.float32(64))).astype(np.float32)
    parts_c, parts_s = [], []
    for p in (np.floor(pos / 64), np.mod(pos, 64)):
        ang = (p[:, None].astype(np.float32) * inv[None, :]).astype(np.float32)
        c, s = np.cos(ang).astype(np.float32), np.sin(ang).astype(np.float32)
        parts_c += [c, c]
        parts_s += [-s, s]
    rope = np.stack([np.concatenate(parts_c, 1), np.concatenate(parts_s, 1)])
    rope = rope.reshape(2, 2, P, P).transpose(2, 0, 1, 3).reshape(P, -1)

    s = np.arange(T)[:, None]
    t = np.arange(LAT)[None, :]
    is_ctx = s < CTX
    d_fwd = np.where(is_ctx, CTX + t - s, t - (s - CTX))
    d_bwd = np.where(is_ctx, CTX - t + s, (s - CTX) - t)
    delta = np.stack([np.maximum(d_fwd, 0), np.maximum(d_bwd, 0)]).astype(np.float32)
    keep = np.stack([d_fwd >= 0, d_bwd >= 0]).astype(np.float32)[:, CTX:]
    delta = delta.reshape(2, NT, P, LAT).transpose(2, 0, 1, 3).reshape(P, -1)
    keep = keep.reshape(2, 2, P, LAT).transpose(2, 0, 1, 3).reshape(P, -1)

    lags = np.arange(LAT, dtype=np.float64)
    omega = 2.0 * np.pi * (np.arange(NFREQ) + 0.5) / (2 * LAT)
    cos = np.cos(lags[:, None] * omega[None, :]).astype(np.float32)
    sin = np.sin(lags[:, None] * omega[None, :]).astype(np.float32)
    fwd = np.stack([cos, sin]).reshape(2, 2, P, NFREQ).transpose(2, 0, 1, 3).reshape(P, -1)
    inv_t = np.stack([cos.T, -sin.T]).astype(np.float64) / NFREQ
    inv_t = inv_t.astype(np.float32).reshape(2, 2, P, LAT).transpose(2, 0, 1, 3).reshape(P, -1)
    dft = np.concatenate([fwd, inv_t], axis=1)

    tt = (pos / np.float32(LAT - 1))[:, None]
    bands = (HYEMB - 1) // 2
    w = (np.float32(2.0 * math.pi) * pos[:, None] / np.float32(LAT)
         * np.linspace(1e-4, bands - 1, bands, dtype=np.float32)[None, :]).astype(np.float32)
    z = np.concatenate([tt, np.cos(w), np.sin(w)], -1).astype(np.float32)
    deltas = np.abs(np.linspace(math.log(1e-2) / 1.5, math.log(1e-2) / 0.3, HYW, dtype=np.float32))
    decay = np.exp(-tt * deltas[None, :]).astype(np.float32)
    decay_b = decay.copy()
    decay_b[0] = 0.0
    decay = np.stack([decay, decay_b]).reshape(2, 2, P, HYW).transpose(2, 0, 1, 3).reshape(P, -1)
    return {
        "t_base": base, "t_negsel": negsel.reshape(HEADS, -1), "t_rope": rope, "t_delta": delta,
        "t_keep": keep, "t_dft": dft, "t_z": np.ascontiguousarray(z.T), "t_decay": decay,
    }


class Net:
    pass


def new_sem(g, name):
    g.n_sems += 1
    sem = g.nc.alloc_semaphore(f"{name}_{g.n_sems}")
    g.sems.append(sem)
    return sem


def recycle_sems(g):
    g.nc.clear_and_free_semaphores(g.sems)
    g.sems = []
    g.nc.all_engine_barrier()


class Chain:

    def __init__(self, eng, sem):
        self.eng, self.sem, self.n = eng, sem, 0

    def __call__(self, ins):
        self.n += 1
        ins.then_inc(self.sem, 1)
        self.eng.wait_ge(self.sem, self.n)


def load_stage(g):
    nc = g.nc
    loaded = new_sem(g, "const_loaded")
    act_done = new_sem(g, "silu_done")
    loads = [(g.h[:], g.dram["x_all"]), (g.base[:], g.dram["t_base"]), (g.c_cols[:], g.dram["c_cols"])]
    with nc.Block() as block:
        @block.sync
        def _(sp):
            for dst, src in loads:
                sp.dma_start(dst, src).then_inc(loaded, 16)

        @block.scalar
        def _(act):
            act.wait_ge(loaded, 16 * len(loads))
            nc.scalar.activation(g.c_act[:], g.c_cols[:], ACT.Silu).then_inc(act_done, 1)
            act.wait_ge(act_done, 1)


def ada_stage(g, l):
    nc = g.nc
    NCH_A, SLOTS = MODS * D // 512, 4
    loaded = [new_sem(g, "ada_w_loaded") for _ in range(SLOTS)]
    bias_loaded, used, summed, added = (new_sem(g, n) for n in ("ada_b_loaded", "ada_w_used", "ada_summed", "ada_added"))
    with ExitStack() as ctx:
        ring = ctx.enter_context(nc.sbuf_tensor(f"ada_ring{l}", [P, SLOTS, KT, 512], F32))
        bias = ctx.enter_context(nc.sbuf_tensor(f"ada_bias{l}", [P, MODS * KT], F32))
        ps = g.bank[0][:, 0:MODS * KT * 2]
        with nc.Block() as block:
            @block.sync
            def _(sp):
                sp.dma_start(bias[:], g.dram["ada_b"][l]).then_inc(bias_loaded, 16)
                for c in range(NCH_A):
                    if c >= SLOTS:
                        sp.wait_ge(used, c - SLOTS + 1)
                    sp.dma_start(ring[:, c % SLOTS], g.dram["ada_w"][l, c]).then_inc(loaded[c % SLOTS], 16)

            @block.tensor
            def _(pe):
                for c in range(NCH_A):
                    pe.wait_ge(loaded[c % SLOTS], 16 * (c // SLOTS + 1))
                    for j in range(4):
                        m = 4 * c + j
                        for k in range(KT):
                            last = nc.tensor.matmul(ps[:, 2 * m:2 * m + 2], ring[:, c % SLOTS, k, j * P:(j + 1) * P],
                                                    g.c_act[:, k, :], start=k == 0, stop=k == KT - 1)
                    last.then_inc(used, 1)

            @block.vector
            def _(dve):
                link = Chain(dve, added)
                dve.wait_ge(used, NCH_A)
                dve.wait_ge(bias_loaded, 16)
                mods = g.mods[:, l]
                link(nc.vector.tensor_tensor(mods, ps.rearrange("p (m v) -> p m v", v=2),
                                             bias[:].unsqueeze(2).broadcast_to([P, MODS * KT, 2]), ALU.add))
                for which in (1, 4):
                    part = mods[:, which * KT:(which + 1) * KT, :]
                    link(nc.vector.tensor_scalar(part, part, 1.0, None, ALU.add))


def modulate_stage(g, l, shift, scale, tiles, rows):
    nc = g.nc
    t0, n = tiles[0] * P, len(tiles) * P
    streams = [(1, 0, CTX), (0, CTX, T)] if tiles[0] == 0 else [(0, CTX, T)]
    turned, modulated, row_ready, row_copied = (new_sem(g, x) for x in ("turned", "modulated", "row_ready", "row_copied"))
    mods = g.mods[:, l]
    with nc.Block() as block:
        @block.tensor
        def _(pe):
            for k in range(KT):
                if k >= 4:
                    pe.wait_ge(modulated, len(streams) * (k - 3))
                for i in tiles:
                    last = nc.tensor.transpose(g.bank[k % 4][:, i * P:(i + 1) * P], g.h[:, i, k * P:(k + 1) * P], g.ident)
                last.then_inc(turned, 1)
            for v in range(2):
                for k in range(KT):
                    col = mods[:, rows * KT + k, v:v + 1].broadcast_to([P, P])
                    last = nc.tensor.matmul(g.bank[4 + 2 * v + k // 4][:, (k % 4) * P:(k % 4 + 1) * P], col, g.ident,
                                            start=True, stop=True)
            last.then_inc(row_ready, 1)

        @block.scalar
        def _(act):
            for k in range(KT):
                act.wait_ge(turned, k + 1)
                for v, a, b in streams:
                    nc.scalar.activation(g.xt[:, k, a:b], g.bank[k % 4][:, a:b], ACT.Identity,
                                         bias=mods[:, shift * KT + k, v:v + 1],
                                         scale=mods[:, scale * KT + k, v:v + 1]).then_inc(modulated, 1)

        @block.vector
        def _(dve):
            dve.wait_ge(row_ready, 1)
            for v in range(2):
                for half in range(2):
                    nc.vector.tensor_copy(g.mod_row[:, v, half * 512:(half + 1) * 512],
                                          g.bank[4 + 2 * v + half][:]).then_inc(row_copied, 1)


def projection_stage(g, weights, jobs):
    nc = g.nc
    SLOTS = 3
    loaded = [new_sem(g, "w_in_loaded") for _ in range(SLOTS)]
    produced, squashed, act_evac, dve_evac = (new_sem(g, x) for x in ("proj_produced", "proj_sigmoid", "proj_act_evac", "proj_dve_evac"))
    outs = []
    for gi, (_, kind, tiles, dst, fn) in enumerate(jobs):
        for j in (range(4) if kind == "T" else range(len(tiles))):
            outs.append((gi, kind, tiles, j, dst, fn))
    last_of = {gi: n for n, (gi, *_) in enumerate(outs)}
    emptied, counts = [], {"act": 0, "dve": 0}
    for *_, fn in outs:
        who = "act" if fn == "sigmoid" else "dve"
        counts[who] += 1
        emptied.append((act_evac if who == "act" else dve_evac, counts[who]))
    silus = [n for n, o in enumerate(outs) if o[-1] == "silu"]
    with ExitStack() as ctx:
        ring = ctx.enter_context(nc.sbuf_tensor(f"w_in_ring{g.n_sems}", [P, SLOTS, KT, 512], F32))
        sig = ctx.enter_context(nc.sbuf_tensor(f"sig{g.n_sems}", [P, 2, 512], F32))
        with nc.Block() as block:
            @block.sync
            def _(sp):
                for gi, (w, *_) in enumerate(jobs):
                    if gi >= SLOTS:
                        sp.wait_ge(produced, last_of[gi - SLOTS] + 1)
                    sp.dma_start(ring[:, gi % SLOTS], weights[w]).then_inc(loaded[gi % SLOTS], 16)

            @block.tensor
            def _(pe):
                for n, (gi, kind, tiles, j, dst, fn) in enumerate(outs):
                    w = ring[:, gi % SLOTS]
                    if j == 0:
                        pe.wait_ge(loaded[gi % SLOTS], 16 * (gi // SLOTS + 1))
                    if n >= 8:
                        pe.wait_ge(*emptied[n - 8])
                    a, b = tiles[0] * P, (tiles[-1] + 1) * P
                    for k in range(KT):
                        if kind == "T":
                            last = nc.tensor.matmul(g.bank[n % 8][:, 0:b - a], w[:, k, j * P:(j + 1) * P], g.xt[:, k, a:b],
                                                    start=k == 0, stop=k == KT - 1)
                        else:
                            i = tiles[j]
                            last = nc.tensor.matmul(g.bank[n % 8][:], g.xt[:, k, i * P:(i + 1) * P], w[:, k, :],
                                                    start=k == 0, stop=k == KT - 1)
                    last.then_inc(produced, 1)

            @block.scalar
            def _(act):
                for n, (gi, kind, tiles, j, dst, fn) in enumerate(outs):
                    wd = (tiles[-1] + 1 - tiles[0]) * P if kind == "T" else 512
                    src = g.bank[n % 8][:, 0:wd]
                    if fn == "sigmoid":
                        act.wait_ge(produced, n + 1)
                        nc.scalar.activation(dst(j), src, ACT.Sigmoid).then_inc(act_evac, 1)
                    elif fn == "silu":
                        m = silus.index(n)
                        act.wait_ge(produced, n + 1)
                        if m >= 2:
                            act.wait_ge(*emptied[silus[m - 2]])
                        nc.scalar.activation(sig[:, m % 2, 0:wd], src, ACT.Sigmoid).then_inc(squashed, 1)

            @block.vector
            def _(dve):
                for n, (gi, kind, tiles, j, dst, fn) in enumerate(outs):
                    wd = (tiles[-1] + 1 - tiles[0]) * P if kind == "T" else 512
                    src = g.bank[n % 8][:, 0:wd]
                    if fn == "sigmoid":
                        continue
                    if fn == "silu":
                        m = silus.index(n)
                        dve.wait_ge(squashed, m + 1)
                        nc.vector.tensor_tensor(dst(j), src, sig[:, m % 2, 0:wd], ALU.mult).then_inc(dve_evac, 1)
                        continue
                    dve.wait_ge(produced, n + 1)
                    if fn == "heads":
                        src = src.rearrange("p (h d) -> p h d", h=HEADS)
                    if fn == "q_scale" and j < 2:
                        nc.vector.tensor_scalar(dst(j), src, 64.0 ** -0.5, None, ALU.mult).then_inc(dve_evac, 1)
                    else:
                        nc.vector.tensor_copy(dst(j), src).then_inc(dve_evac, 1)


def mlstm_tiles(d, j):
    if d == 0:
        return [(j, j + 1)] + ([(j + 1, NT)] if j + 1 < NT else [])
    if j >= 2:
        return [(j, j + 1)] + ([(2, j)] if j > 2 else [])
    return [(j, j + 1)] + ([(0, j)] if j > 0 else []) + [(2, NT)]


def key_tiles(d, i):
    return [j for j in range(NT) if any(a <= i < b for a, b in mlstm_tiles(d, j))]


def gates_stage(g, s):
    nc = g.nc
    loaded, made, activated, step, turned = (new_sem(g, x) for x in ("gate_w_loaded", "gates_made", "gate_act", "gate_step", "gate_turned"))
    act_step = new_sem(g, "gate_act_step")
    with ExitStack() as ctx:
        wg = ctx.enter_context(nc.sbuf_tensor("w_gates", [P, KT, 4 * HEADS], F32))
        gb = ctx.enter_context(nc.sbuf_tensor("gate_b", [HEADS, 4], F32))
        tmp = {n: ctx.enter_context(nc.sbuf_tensor(f"gate_{n}", [HEADS, 2, T], F32)) for n in ("x", "e", "lf", "B", "a", "m", "ones")}
        with nc.Block() as block:
            @block.sync
            def _(sp):
                sp.dma_start(wg[:], g.dram["w_gates"]).then_inc(loaded, 16)
                sp.dma_start(gb[:], g.dram["gate_b"]).then_inc(loaded, 16)

            @block.tensor
            def _(pe):
                pe.wait_ge(loaded, 32)
                for q in range(4):
                    for k in range(KT):
                        last = nc.tensor.matmul(g.bank[q][0:HEADS, :], wg[:, k, q * HEADS:(q + 1) * HEADS], g.xt[:, k, :],
                                                start=k == 0, stop=k == KT - 1)
                last.then_inc(made, 1)
                pe.wait_ge(step, s["n_rows"])
                for d in range(2):
                    for c, src in enumerate((tmp["a"], tmp["m"])):
                        for i in range(NT):
                            at = ((d * 2 + c) * NT + i) * HEADS
                            last = nc.tensor.transpose(g.bank[4][:, at:at + HEADS], src[:, d, i * P:(i + 1) * P],
                                                       g.ident[0:HEADS, 0:HEADS])
                last.then_inc(turned, 1)

            @block.scalar
            def _(act):
                act.wait_ge(step, s["n_abs"])
                nc.scalar.activation(tmp["e"][:], tmp["e"][:], ACT.Exp, scale=-1.0).then_inc(act_step, 1)
                act.wait_ge(act_step, 1)
                nc.scalar.activation(tmp["e"][:], tmp["e"][:], ACT.Ln, bias=1.0).then_inc(activated, 1)
                act.wait_ge(turned, 1)
                cols = g.bank[4][:, 0:2 * 2 * NT * HEADS].rearrange("p (d c i) -> p d c i", d=2, c=2)
                nc.scalar.activation(s["a_col"][:], cols[:, :, 0, :], ACT.Copy).then_inc(activated, 1)
                nc.scalar.activation(s["floor_col"][:], cols[:, :, 1, :], ACT.Exp, scale=-1.0).then_inc(activated, 1)

            @block.vector
            def _(dve):
                link = Chain(dve, step)
                link(nc.vector.memset(tmp["ones"][:], 1.0))
                dve.wait_ge(made, 1)
                for d in range(2):
                    link(nc.vector.tensor_scalar(tmp["x"][:, d], g.bank[2 * d + 1][0:HEADS, :], gb[:, 2 * d + 1:2 * d + 2], None, ALU.add))
                    link(nc.vector.tensor_scalar(tmp["a"][:, d], g.bank[2 * d][0:HEADS, :], gb[:, 2 * d:2 * d + 1], None, ALU.add))
                link(nc.vector.scalar_tensor_tensor(tmp["e"][:], tmp["x"][:], -1.0, tmp["x"][:], ALU.mult, ALU.max))
                s["n_abs"] = link.n
                dve.wait_ge(activated, 1)
                link(nc.vector.scalar_tensor_tensor(tmp["lf"][:], tmp["x"][:], 0.0, tmp["e"][:], ALU.min, ALU.subtract))
                ones, lf, B, a, M = tmp["ones"], tmp["lf"], tmp["B"], tmp["a"], s["max_row"]
                link(nc.vector.tensor_tensor_scan(B[:, 0, :], ones[:, 0, :], lf[:, 0, :], 0.0, ALU.mult, ALU.add))
                link(nc.vector.tensor_tensor_scan(B[:, 1, 0:CTX][:, ::-1], ones[:, 0, 0:CTX], lf[:, 1, 0:CTX][:, ::-1], 0.0, ALU.mult, ALU.add))
                link(nc.vector.tensor_tensor_scan(B[:, 1, CTX:T][:, ::-1], ones[:, 0, 0:LAT], lf[:, 1, CTX:T][:, ::-1], B[:, 1, 0:1], ALU.mult, ALU.add))
                link(nc.vector.tensor_tensor(a[:], a[:], B[:], ALU.subtract))
                link(nc.vector.tensor_tensor_scan(M[:, 0, :], a[:, 0, :], a[:, 0, :], NEG_BIG, ALU.max, ALU.max))
                ac, al = a[:, 1, 0:CTX][:, ::-1], a[:, 1, CTX:T][:, ::-1]
                link(nc.vector.tensor_tensor_scan(M[:, 1, 0:CTX][:, ::-1], ac, ac, NEG_BIG, ALU.max, ALU.max))
                link(nc.vector.tensor_tensor_scan(M[:, 1, CTX:T][:, ::-1], al, al, M[:, 1, 0:1], ALU.max, ALU.max))
                link(nc.vector.tensor_tensor(tmp["m"][:], B[:], M[:], ALU.add))
                s["n_rows"] = link.n


def mlstm_stage(g, s):
    nc = g.nc
    scored, row_max_ready, clamped, exped, weighted, read, summed, step = (
        new_sem(g, x) for x in ("scores_ready", "max_rows_ready", "clamped", "exp_ready", "weights_ready",
                                "scores_used", "values_summed", "dve_step"))
    pool_masked = new_sem(g, "diag_masked")
    units = [(h, d) for h in range(HEADS) for d in range(2)]
    pieces = [(u, j, n, rng) for u, (h, d) in enumerate(units) for j in range(NT)
              for n, rng in enumerate(mlstm_tiles(d, j))]
    tri = {0: g.upper, 1: g.lower}
    with ExitStack() as ctx:
        e = ctx.enter_context(nc.sbuf_tensor("mlstm_e", [P, 2, NT, T], F32))
        sm = ctx.enter_context(nc.sbuf_tensor("mlstm_small", [P, 2, 3, NT], F32))
        loaded = new_sem(g, "negsel_loaded")
        negsel = ctx.enter_context(nc.sbuf_tensor("negsel", [HEADS, HEADS, P], F32))
        S = g.bank[0:4]
        ndone = {u: sum(1 for p in pieces if p[0] <= u) for u in range(len(units))}
        ndone[-1] = 0
        with nc.Block() as block:
            @block.sync
            def _(sp):
                sp.dma_start(negsel[:], g.dram["t_negsel"].rearrange("h (a b) -> h a b", a=HEADS)).then_inc(loaded, 16)

            @block.tensor
            def _(pe):
                pe.wait_ge(loaded, 16)

                def scores(u):
                    h, d = units[u]
                    if u >= 2:
                        pe.wait_ge(clamped, ndone[u - 2])
                    nc.tensor.matmul(g.bank[4 + d][:], negsel[:, h, :], s["max_row"][:, d, :], start=True, stop=True).then_inc(row_max_ready, 1)
                    if d == 0:
                        if u >= 1:
                            pe.wait_ge(weighted, ndone[u - 1])
                        r = slice(64 * (h % 2), 64 * (h % 2) + 64)
                        for j in range(NT):
                            nc.tensor.matmul(S[j][:], s["kT"][r, h // 2, j * P:(j + 1) * P], s["qT"][r, h // 2, :],
                                             start=True, stop=True).then_inc(scored, 1)

                def values(u):
                    h, d = units[u]
                    pe.wait_ge(weighted, ndone[u])
                    if u >= 1:
                        pe.wait_ge(read, u)
                    for i in range(NT):
                        keys = key_tiles(d, i)
                        for j in keys:
                            last = nc.tensor.matmul(g.bank[6 + i // 2][:, (i % 2) * 256:(i % 2) * 256 + P + 1],
                                                    e[:, u % 2, j, i * P:(i + 1) * P], s["v1"][:, j, h, :],
                                                    start=j == keys[0], stop=j == keys[-1])
                    last.then_inc(summed, 1)

                scores(0)
                for u in range(len(units)):
                    if u + 1 < len(units) and units[u + 1][1] == 1:
                        scores(u + 1)
                        values(u)
                    elif u + 1 < len(units):
                        scores(u + 1)
                        values(u)
                    else:
                        values(u)

            @block.scalar
            def _(act):
                for n, (u, j, k, (a, b)) in enumerate(pieces):
                    act.wait_ge(clamped, n + 1)
                    w = e[:, u % 2, j, a * P:b * P]
                    nc.scalar.activation(w, w, ACT.Exp).then_inc(exped, 1)

            @block.vector
            def _(dve):
                link = Chain(dve, step)
                dve_n = 0

                def clamp(u):
                    h, d = units[u]
                    dve.wait_ge(row_max_ready, u + 1)
                    if u >= 2:
                        dve.wait_ge(summed, u - 1)
                    for (uu, j, k, (a, b)) in pieces:
                        if uu == u:
                            nc.vector.tensor_scalar(e[:, u % 2, j, a * P:b * P], g.bank[4 + d][:, a * P:b * P],
                                                    s["a_col"][:, d, j * HEADS + h:j * HEADS + h + 1], 0.0,
                                                    ALU.add, ALU.min).then_inc(clamped, 1)

                def weigh(u):
                    h, d = units[u]
                    for n, (uu, j, k, (a, b)) in enumerate(pieces):
                        if uu != u:
                            continue
                        dve.wait_ge(exped, n + 1)
                        w = e[:, u % 2, j, a * P:b * P]
                        if k == 0:
                            if d == 0:
                                dve.wait_ge(scored, h * NT + j + 1)
                            link(nc.vector.tensor_tensor(w, w, tri[d], ALU.mult))
                        nc.vector.tensor_tensor(w, w, S[j][:, a * P:b * P], ALU.mult).then_inc(weighted, 1)

                def finish(u):
                    h, d = units[u]
                    dve.wait_ge(summed, u + 1)
                    x = sm[:, u % 2]
                    den, neg, inv = x[:, 0], x[:, 1], x[:, 2]
                    for half in range(2):
                        b = g.bank[6 + half][:].rearrange("p (i w) -> p i w", i=2)[:, :, P]
                        link(nc.vector.tensor_copy(den[:, 2 * half:2 * half + 2], b))
                    link(nc.vector.scalar_tensor_tensor(neg, den, -1.0, den, ALU.mult, ALU.max))
                    fl = s["floor_col"][:, d].rearrange("p (i h) -> p i h", h=HEADS)[:, :, h]
                    link(nc.vector.tensor_tensor(neg, neg, fl, ALU.max))
                    link(nc.vector.reciprocal(inv, neg))
                    for i in range(NT):
                        src = g.bank[6 + i // 2][:, (i % 2) * 256:(i % 2) * 256 + P]
                        dst = s["y"][:, i, h * P:(h + 1) * P]
                        if d == 0:
                            ins = nc.vector.tensor_scalar(dst, src, inv[:, i:i + 1], None, ALU.mult)
                        else:
                            ins = nc.vector.scalar_tensor_tensor(dst, src, inv[:, i:i + 1], dst, ALU.mult, ALU.add)
                        link(ins)
                    dve.sem_inc(read, 1)

                clamp(0)
                for u in range(len(units)):
                    if u + 1 < len(units):
                        clamp(u + 1)
                    weigh(u)
                    finish(u)


def norm_stage(g, y, tiles, groups, center, gate, w_name, mix_base, tag):
    nc = g.nc
    nt = len(tiles)
    width = 512 // groups
    loaded, step, rooted, turned, copied = (new_sem(g, x) for x in ("norm_w_loaded", "norm_step", "norm_root", "mix_turned", "mix_copied"))
    with ExitStack() as ctx:
        sq = ctx.enter_context(nc.sbuf_tensor(f"norm_sq_{tag}", [P, nt, 512], F32))
        st = ctx.enter_context(nc.sbuf_tensor(f"norm_st_{tag}", [P, 2, nt, groups], F32))
        w = ctx.enter_context(nc.sbuf_tensor(f"norm_w_{tag}", [P, 512], F32))
        marks = {}
        flat = y.rearrange("p i (n w) -> p i n w", w=width)
        sqf = sq[:].rearrange("p i (n w) -> p i n w", w=width)
        with nc.Block() as block:
            @block.sync
            def _(sp):
                sp.dma_start(w[:], g.dram[w_name]).then_inc(loaded, 16)

            @block.vector
            def _(dve):
                link = Chain(dve, step)
                if center:
                    link(nc.vector.tensor_reduce(st[:, 0], flat, AX.X, ALU.add))
                    link(nc.vector.tensor_scalar(st[:, 0], st[:, 0], 1.0 / width, None, ALU.mult))
                    link(nc.vector.tensor_tensor(flat, flat, st[:, 0].unsqueeze(3).broadcast_to([P, nt, groups, width]), ALU.subtract))
                link(nc.vector.tensor_tensor(sq[:], y, y, ALU.mult))
                link(nc.vector.tensor_reduce(st[:, 1], sqf, AX.X, ALU.add))
                link(nc.vector.tensor_scalar(st[:, 1], st[:, 1], 1.0 / width, EPS, ALU.mult, ALU.add))
                marks["var"] = link.n
                dve.wait_ge(rooted, 1)
                link(nc.vector.reciprocal(st[:, 1], st[:, 1]))
                link(nc.vector.tensor_tensor(flat, flat, st[:, 1].unsqueeze(3).broadcast_to([P, nt, groups, width]), ALU.mult))
                dve.wait_ge(loaded, 16)
                link(nc.vector.tensor_tensor(y, y, w[:].unsqueeze(1).broadcast_to([P, nt, 512]), ALU.mult))
                if gate is not None:
                    link(nc.vector.tensor_tensor(y, y, gate, ALU.mult))
                marks["gated"] = link.n

            @block.scalar
            def _(act):
                act.wait_ge(step, marks["var"])
                nc.scalar.activation(st[:, 1], st[:, 1], ACT.Sqrt).then_inc(rooted, 1)
                for c in range(4):
                    act.wait_ge(turned, c + 1)
                    nc.scalar.activation(g.mix[:, mix_base + c, tiles[0] * P:(tiles[-1] + 1) * P],
                                         g.bank[c][:, 0:nt * P], ACT.Copy).then_inc(copied, 1)

            @block.tensor
            def _(pe):
                pe.wait_ge(step, marks["gated"])
                for c in range(4):
                    for n in range(nt):
                        last = nc.tensor.transpose(g.bank[c][:, n * P:(n + 1) * P], y[:, n, c * P:(c + 1) * P], g.ident)
                    last.then_inc(turned, 1)


def hgrn_stage(g, s):
    nc = g.nc
    TILE_CH = P // CHUNK
    SR = TILE_CH + 1
    (lb_loaded, prep, act_prep, vmasked, zeroed, turned, k1_ready, scored, masked, located, stated, out_ready,
     added) = (new_sem(g, x) for x in (
        "lb_loaded", "hgrn_prep", "hgrn_act", "v_masked", "sc_zeroed", "k1_turned", "k1_ready", "hgrn_scored",
        "hgrn_masked", "s_loc_ready", "state_ready", "hgrn_out_ready", "hgrn_added"))
    lb_step = new_sem(g, "lb_step")
    lb_act = new_sem(g, "lb_act")
    with ExitStack() as ctx:
        sb = lambda n, shape: ctx.enter_context(nc.sbuf_tensor(f"hgrn_{n}", shape, F32))
        lbw = sb("lb", [P, 4, HEADS])
        k, A, E, D1, Q1, K1 = (sb(n, [P, HEADS * T]) for n in ("k", "A", "E", "D1", "Q1", "K1"))
        reset = sb("reset", [P, HEADS * T])
        dend = sb("dend", [P, HEADS * NCH])
        vmask = sb("vmask", [P, 2, HEADS, TILE_CH * P])
        k1t = sb("k1t", [P, 2, HEADS, P])
        sc = sb("sc", [P, 2, 2, HEADS, P])
        st = sb("state", [P, HEADS, SR, P])

        def per_chunk(x):
            return x.rearrange("p (c t) -> p c t", t=CHUNK)

        with nc.Block() as block:
            @block.sync
            def _(sp):
                sp.dma_start(lbw[:, 0], g.dram["lb_cols"]).then_inc(lb_loaded, 16)

            @block.scalar
            def _(act):
                act.wait_ge(lb_step, 1)
                nc.scalar.activation(lbw[:, 1], lbw[:, 1], ACT.Exp).then_inc(lb_act, 1)

            @block.vector
            def _(dve):
                link = Chain(dve, lb_step)
                dve.wait_ge(lb_loaded, 16)
                link(nc.vector.tensor_tensor(lbw[:, 1], lbw[:, 0], lbw[:, 0], ALU.subtract))
                dve.wait_ge(lb_act, 1)
                link(nc.vector.reciprocal(lbw[:, 2], lbw[:, 1]))
                link(nc.vector.tensor_tensor(lbw[:, 1], lbw[:, 1], lbw[:, 2], ALU.mult))
                link(nc.vector.tensor_tensor(lbw[:, 2], lbw[:, 1], lbw[:, 1], ALU.subtract))
                link(nc.vector.tensor_scalar(lbw[:, 3], lbw[:, 2], -1.0, 1.0, ALU.mult, ALU.add))

            @block.gpsimd
            def _(pool):
                pool.memset(reset[:], 1.0).then_inc(zeroed, 1)
                pool.wait_ge(zeroed, 1)
                pool.memset(per_chunk(reset[:])[:, :, 0:1], 0.0).then_inc(zeroed, 1)
                pool.memset(sc[:], 0.0).then_inc(zeroed, 1)
                pool.wait_ge(zeroed, 3)

        for d in range(2):
            f = s["f"][d]
            Q2 = f.rearrange("p h t -> p (h t)")
            rev = slice(None, None, -1) if d else slice(None)
            last_t, mid_t = (CHUNK - 1, CHUNK // 2 - 1) if d == 0 else (0, CHUNK // 2)
            tiles = [0, 1, 2, 3] if d == 0 else [1, 0, 3, 2]
            chunk_order = list(range(TILE_CH)) if d == 0 else list(range(TILE_CH))[::-1]
            marks = {}
            prep, act_prep = new_sem(g, "hgrn_prep"), new_sem(g, "hgrn_act")
            with nc.Block() as block:
                @block.vector
                def _(dve):
                    link = Chain(dve, prep)
                    for h in range(HEADS):
                        link(nc.vector.tensor_scalar(f[:, h], f[:, h], lbw[:, 3, h:h + 1], lbw[:, 2, h:h + 1], ALU.mult, ALU.add))
                    ff = f.rearrange("p h t -> p (h t)")
                    q = s["q"].rearrange("p h t -> p (h t)")
                    marks["f"] = link.n
                    link(nc.vector.tensor_scalar(k[:], ff, -1.0, 1.0, ALU.mult, ALU.add))
                    link(nc.vector.tensor_scalar(ff, ff, TINY, None, ALU.max))
                    marks["floor"] = link.n
                    dve.wait_ge(act_prep, 1)
                    link(nc.vector.tensor_tensor_scan(A[:, rev], reset[:], E[:, rev], 0.0, ALU.mult, ALU.add))
                    marks["A"] = link.n
                    Ac = per_chunk(A[:])
                    mid = Ac[:, :, mid_t:mid_t + 1].broadcast_to([P, HEADS * NCH, CHUNK])
                    end = Ac[:, :, last_t:last_t + 1].broadcast_to([P, HEADS * NCH, CHUNK])
                    link(nc.vector.tensor_tensor(per_chunk(D1[:]), Ac, mid, ALU.subtract))
                    marks["D1"] = link.n
                    dve.wait_ge(act_prep, 3)
                    link(nc.vector.tensor_tensor(Q1[:], E[:], q, ALU.mult))
                    marks["Q1"] = link.n
                    dve.wait_ge(act_prep, 4)
                    link(nc.vector.tensor_tensor(Q2, E[:], q, ALU.mult))
                    link(nc.vector.tensor_tensor(per_chunk(K1[:]), end, Ac, ALU.subtract))
                    marks["K1"] = link.n
                    dve.wait_ge(act_prep, 6)
                    link(nc.vector.tensor_tensor(K1[:], K1[:], k[:], ALU.mult))
                    link(nc.vector.tensor_tensor(D1[:], D1[:], k[:], ALU.mult))

                @block.scalar
                def _(act):
                    act.wait_ge(prep, marks["floor"])
                    nc.scalar.activation(E[:], f.rearrange("p h t -> p (h t)"), ACT.Ln).then_inc(act_prep, 1)
                    act.wait_ge(prep, marks["A"])
                    ends = per_chunk(A[:])[:, :, last_t]
                    nc.scalar.activation(dend[:], ends, ACT.Exp).then_inc(act_prep, 1)
                    nc.scalar.activation(E[:], A[:], ACT.Exp).then_inc(act_prep, 1)
                    act.wait_ge(prep, marks["Q1"])
                    nc.scalar.activation(E[:], D1[:], ACT.Exp).then_inc(act_prep, 1)
                    act.wait_ge(act_prep, 4)
                    nc.scalar.activation(D1[:], D1[:], ACT.Exp, scale=-1.0).then_inc(act_prep, 1)
                    act.wait_ge(prep, marks["K1"])
                    nc.scalar.activation(K1[:], K1[:], ACT.Exp).then_inc(act_prep, 1)

            (vmasked, turned, k1_ready, scored, masked, located, stated, out_ready, added) = (new_sem(g, x) for x in (
                "v_masked", "k1_turned", "k1_ready", "hgrn_scored", "hgrn_masked", "s_loc_ready", "state_ready",
                "hgrn_out_ready", "hgrn_added"))
            keep = g.tri_chunk[d]
            state_zeroed = new_sem(g, "state_zeroed")
            with nc.Block() as block:
                @block.tensor
                def _(pe):
                    for n, i in enumerate(tiles):
                        if n >= 1:
                            pe.wait_ge(k1_ready, n)
                        for h in range(HEADS):
                            at = h * T + i * P
                            last = nc.tensor.transpose(g.bank[0][:, h * P:(h + 1) * P], K1[:, at:at + P], g.ident)
                        last.then_inc(turned, 1)
                        if n >= 1:
                            pe.wait_ge(masked, n * HEADS)
                        for h in range(HEADS):
                            at = h * T + i * P
                            last = nc.tensor.matmul(g.bank[1][:, h * P:(h + 1) * P], D1[:, at:at + P], Q2[:, at:at + P],
                                                    start=True, stop=True)
                        last.then_inc(scored, 1)
                        pe.wait_ge(k1_ready, n + 1)
                        pe.wait_ge(vmasked, n + 1)
                        if n >= 1:
                            pe.wait_ge(stated, HEADS * TILE_CH * n)
                        for h in range(HEADS):
                            nc.tensor.matmul(g.bank[2 + h][:], k1t[:, n % 2, h], vmask[:, n % 2, h], start=True, stop=True).then_inc(located, 1)
                        if n >= 2:
                            pe.wait_ge(added, n - 1)
                        for h in range(HEADS):
                            pe.wait_ge(masked, n * HEADS + h + 1)
                            out = g.bank[6 + n % 2][:, h * P:(h + 1) * P]
                            first = n == 0
                            nc.tensor.matmul(out, sc[:, d, n % 2, h], s["v"][:, i, h * P:(h + 1) * P], start=True, stop=False, skip_group_check=True)
                            for m, c in enumerate(chunk_order):
                                pe.wait_ge(stated, HEADS * (n * TILE_CH + m)) if n or m else pe.wait_ge(state_zeroed, 1)
                                at = h * T + i * P + c * CHUNK
                                slot = (n * TILE_CH + m) % SR
                                last = nc.tensor.matmul(out[c * CHUNK:(c + 1) * CHUNK, :], Q1[:, at:at + CHUNK], st[:, h, slot],
                                                        start=False, stop=m == TILE_CH - 1, skip_group_check=True)
                        last.then_inc(out_ready, 1)

                @block.scalar
                def _(act):
                    for n, i in enumerate(tiles):
                        act.wait_ge(turned, n + 1)
                        if n >= 2:
                            act.wait_ge(located, HEADS * (n - 1))
                        nc.scalar.activation(k1t[:, n % 2], g.bank[0][:].rearrange("p (h t) -> p h t", h=HEADS), ACT.Copy).then_inc(k1_ready, 1)

                @block.gpsimd
                def _(pool):
                    for n, i in enumerate(tiles):
                        if n >= 2:
                            pool.wait_ge(located, HEADS * (n - 1))
                        for h in range(HEADS):
                            src = s["v"][:, i, h * P:(h + 1) * P].unsqueeze(1).broadcast_to([P, TILE_CH, P])
                            last = pool.tensor_tensor(vmask[:, n % 2, h].rearrange("p (c v) -> p c v", v=P), src,
                                                      g.chunk_of.unsqueeze(2).broadcast_to([P, TILE_CH, P]), ALU.mult)
                        last.then_inc(vmasked, 1)

                @block.vector
                def _(dve):
                    nc.vector.memset(st[:, :, 0], 0.0).then_inc(state_zeroed, 1)
                    dve.wait_ge(state_zeroed, 1)
                    for n, i in enumerate(tiles):
                        if n >= 2:
                            dve.wait_ge(out_ready, n - 1)
                        dve.wait_ge(scored, n + 1)
                        for h in range(HEADS):
                            nc.vector.copy_predicated(sc[:, d, n % 2, h], keep.bitcast(U32), g.bank[1][:, h * P:(h + 1) * P]).then_inc(masked, 1)
                        for m, c in enumerate(chunk_order):
                            gc = n * TILE_CH + m
                            for h in range(HEADS):
                                if m == 0:
                                    dve.wait_ge(located, n * HEADS + h + 1)
                                if gc >= 1:
                                    dve.wait_ge(stated, HEADS * (gc - 1) + h + 1)
                                at = h * NCH + i * TILE_CH + c
                                nc.vector.scalar_tensor_tensor(st[:, h, (gc + 1) % SR], st[:, h, gc % SR], dend[:, at:at + 1],
                                                               g.bank[2 + h][:, c * P:(c + 1) * P], ALU.mult, ALU.add).then_inc(stated, 1)
                        dve.wait_ge(out_ready, n + 1)
                        src = g.bank[6 + n % 2][:]
                        if d == 0:
                            nc.vector.tensor_copy(s["y"][:, i], src).then_inc(added, 1)
                        else:
                            nc.vector.tensor_tensor(s["y"][:, i], s["y"][:, i], src, ALU.add).then_inc(added, 1)


def residual_stage(g, l, which, tiles, source, w_out=None):
    nc = g.nc
    (w_loaded, ln_loaded, produced, freed, step, rooted) = (new_sem(g, x) for x in (
        "w_out_loaded", "ln_loaded", "y_produced", "y_freed", "ln_step", "ln_root"))
    tag = f"{l}{which}"
    with ExitStack() as ctx:
        if w_out is not None:
            w = ctx.enter_context(nc.sbuf_tensor(f"w_out{tag}", [P, KT, D], F32))
        ln = ctx.enter_context(nc.sbuf_tensor(f"ln{tag}", [P, 2, D], F32))
        z = ctx.enter_context(nc.sbuf_tensor(f"ln_z{tag}", [P, 2, D], F32))
        stats = ctx.enter_context(nc.sbuf_tensor(f"ln_stats{tag}", [P, 2, 2, 6], F32))
        mv = ctx.enter_context(nc.sbuf_tensor(f"ln_mv{tag}", [P, 4, 4], F32))
        marks = {}
        with nc.Block() as block:
            @block.sync
            def _(sp):
                if w_out is not None:
                    sp.dma_start(w[:], w_out).then_inc(w_loaded, 16)
                sp.dma_start(ln[:], g.dram["ln_rows"][l, which]).then_inc(ln_loaded, 16)

            if w_out is not None:
                @block.tensor
                def _(pe):
                    pe.wait_ge(w_loaded, 16)
                    for n, i in enumerate(tiles):
                        for half in range(2):
                            u = 2 * n + half
                            for k in range(KT):
                                last = nc.tensor.matmul(g.bank[u % 8][:], g.mix[:, k, i * P:(i + 1) * P], w[:, k, half * 512:(half + 1) * 512],
                                                        start=k == 0, stop=k == KT - 1)
                            last.then_inc(produced, 1)

            @block.vector
            def _(dve):
                link = Chain(dve, step)
                for n, i in enumerate(tiles):
                    v = 1 if i < 2 else 0
                    zz = z[:, n % 2]
                    for half in range(2):
                        cols = slice(half * 512, (half + 1) * 512)
                        if w_out is not None:
                            dve.wait_ge(produced, 2 * n + half + 1)
                            y = g.bank[2 * n + half][:]
                        else:
                            y = source[:, n, cols]
                        link(nc.vector.tensor_tensor(zz[:, cols], y, g.mod_row[:, v, cols], ALU.mult))
                    link(nc.vector.scalar_tensor_tensor(zz, g.h[:, i], ALPHA, zz, ALU.mult, ALU.add))
                    for half in range(2):
                        link(nc.vector.bn_stats(stats[:, n % 2, half], zz[:, half * 512:(half + 1) * 512]))
                    link(nc.vector.bn_aggr(mv[:, n, 0:2], stats[:, n % 2]))
                    link(nc.vector.tensor_scalar(mv[:, n, 2:3], mv[:, n, 1:2], EPS, None, ALU.add))
                    marks[n] = link.n
                    dve.wait_ge(rooted, n + 1)
                    link(nc.vector.reciprocal(mv[:, n, 2:3], mv[:, n, 3:4]))
                    link(nc.vector.tensor_scalar(zz, zz, mv[:, n, 0:1], mv[:, n, 2:3], ALU.subtract, ALU.mult))
                    if n == 0:
                        dve.wait_ge(ln_loaded, 16)
                    link(nc.vector.tensor_tensor(zz, zz, ln[:, 0], ALU.mult))
                    link(nc.vector.tensor_tensor(g.h[:, i], zz, ln[:, 1], ALU.add))

            @block.scalar
            def _(act):
                for n, i in enumerate(tiles):
                    act.wait_ge(step, marks[n])
                    nc.scalar.activation(mv[:, n, 3:4], mv[:, n, 2:3], ACT.Sqrt).then_inc(rooted, 1)


def router_stage(g, l, tiles, gates):
    nc = g.nc
    loaded, scored, squashed, step = (new_sem(g, x) for x in ("router_loaded", "router_scored", "router_sigmoid", "router_step"))
    with ExitStack() as ctx:
        sb = lambda n, shape: ctx.enter_context(nc.sbuf_tensor(f"router_{n}{l}", shape, F32))
        rw, rb = sb("w", [P, KT, EXPERTS]), sb("b", [P, EXPERTS])
        sig, pick, rest, top, tot = (sb(n, [P, 4, w]) for n, w in (("sig", EXPERTS), ("pick", EXPERTS), ("rest", EXPERTS), ("top", TOPK), ("tot", 2)))
        with nc.Block() as block:
            @block.sync
            def _(sp):
                sp.dma_start(rw[:], g.dram["router_w"][l]).then_inc(loaded, 16)
                sp.dma_start(rb[:], g.dram["router_b"][l]).then_inc(loaded, 16)

            @block.tensor
            def _(pe):
                pe.wait_ge(loaded, 32)
                for n, i in enumerate(tiles):
                    for k in range(KT):
                        last = nc.tensor.matmul(g.bank[n][:, 0:EXPERTS], g.xt[:, k, i * P:(i + 1) * P], rw[:, k], start=k == 0, stop=k == KT - 1)
                    last.then_inc(scored, 1)

            @block.scalar
            def _(act):
                for n, i in enumerate(tiles):
                    act.wait_ge(scored, n + 1)
                    nc.scalar.activation(sig[:, n], g.bank[n][:, 0:EXPERTS], ACT.Sigmoid).then_inc(squashed, 1)

            @block.vector
            def _(dve):
                link = Chain(dve, step)
                dve.wait_ge(loaded, 32)
                for n, i in enumerate(tiles):
                    dve.wait_ge(squashed, n + 1)
                    link(nc.vector.tensor_tensor(pick[:, n], sig[:, n], rb[:], ALU.add))
                    link(nc.vector.max(top[:, n], pick[:, n]))
                    link(nc.vector.match_replace(rest[:, n], top[:, n], pick[:, n], NEG_BIG))
                    link(nc.vector.tensor_tensor(rest[:, n], rest[:, n], pick[:, n], ALU.not_equal))
                    link(nc.vector.tensor_tensor(rest[:, n], rest[:, n], sig[:, n], ALU.mult))
                    link(nc.vector.tensor_reduce(tot[:, n, 0:1], rest[:, n], AX.X, ALU.add))
                    link(nc.vector.reciprocal(tot[:, n, 1:2], tot[:, n, 0:1]))
                    link(nc.vector.tensor_scalar(gates[:, n, 0:EXPERTS], rest[:, n], tot[:, n, 1:2], ROUTED_SCALE, ALU.mult, ALU.mult))


def experts_stage(g, l, tiles, gates, acc):
    nc = g.nc
    nt = len(tiles)
    a0, n_tok = tiles[0] * P, nt * P
    PAIRS = EXPERTS // 2
    up_loaded = [new_sem(g, f"up_loaded{s}") for s in range(2)]
    down_loaded = [new_sem(g, f"down_loaded{s}") for s in range(2)]
    up_ready, silu_ready, hidden_ready, y_ready, y_added, zeroed = (new_sem(g, x) for x in (
        "up_ready", "silu_ready", "hidden_ready", "y_ready", "y_added", "acc_zeroed"))
    YP = 2 * nt
    with ExitStack() as ctx:
        up = ctx.enter_context(nc.sbuf_tensor(f"exp_up{l}", [P, 2, 2, KT, HID], F32))
        down = ctx.enter_context(nc.sbuf_tensor(f"exp_down{l}", [P, 2, 2, D], F32))
        silu = ctx.enter_context(nc.sbuf_tensor(f"exp_silu{l}", [P, 2, n_tok], F32))
        hidden = ctx.enter_context(nc.sbuf_tensor(f"exp_hidden{l}", [P, 2, 2, n_tok], F32))
        wd = g.dram["experts"]

        def load_up(sp, slot, n):
            src = wd[base + n, :, 0:W13].rearrange("p (a k c) -> p a k c", a=2, k=KT)
            sp.dma_start(up[:, slot], src).then_inc(up_loaded[slot], 16)

        def load_down(sp, slot, n):
            src = wd[base + n, :, W13:WEXP].rearrange("p (a c) -> p a c", a=2)
            sp.dma_start(down[:, slot], src).then_inc(down_loaded[slot], 16)

        def reload(sp, slot, n):
            sp.wait_ge(up_ready, 2 * n - 2)
            load_up(sp, slot, n)
            sp.wait_ge(y_ready, (n - 1) * YP)
            load_down(sp, slot, n)

        base = l * (EXPERTS + 1)
        with nc.Block() as block:
            @block.sync
            def _(sp):
                load_up(sp, 0, 0)
                load_down(sp, 0, 0)
                load_up(sp, 1, 1)
                load_down(sp, 1, 1)
                with sp.Fori(0, PAIRS - 1) as i:
                    reload(sp, 0, 2 * i + 2)
                    reload(sp, 1, 2 * i + 3)
                reload(sp, 0, 2 * PAIRS)

            def up_project(pe, slot, loads, n, first):
                pe.wait_ge(up_loaded[slot], 16 * loads)
                if not first:
                    pe.wait_ge(hidden_ready, 2 * n)
                for m in range(2):
                    for a in range(2):
                        for k in range(KT):
                            last = nc.tensor.matmul(g.bank[2 * m + a][:, 0:n_tok], up[:, slot, a, k, m * P:(m + 1) * P],
                                                    g.xt[:, k, a0:a0 + n_tok], start=k == 0, stop=k == KT - 1)
                    last.then_inc(up_ready, 1)

            def down_project(pe, slot, loads, n, first):
                pe.wait_ge(down_loaded[slot], 16 * loads)
                pe.wait_ge(hidden_ready, 2 * n + 2)
                for u in range(YP):
                    i, half = u // 2, u % 2
                    if not (first and u < 4):
                        pe.wait_ge(y_added, n * YP + u - 3)
                    for m in range(2):
                        last = nc.tensor.matmul(g.bank[4 + u % 4][:], hidden[:, slot, m, i * P:(i + 1) * P],
                                                down[:, slot, m, half * 512:(half + 1) * 512], start=m == 0, stop=m == 1)
                    last.then_inc(y_ready, 1)

            @block.tensor
            def _(pe):
                up_project(pe, 0, 1, 0, True)
                up_project(pe, 1, 1, 1, False)
                down_project(pe, 0, 1, 0, True)
                up_project(pe, 0, 2, 2, False)
                down_project(pe, 1, 1, 1, False)
                with pe.Fori(1, PAIRS) as i:
                    up_project(pe, 1, i + 1, 2 * i + 1, False)
                    down_project(pe, 0, i + 1, 2 * i, False)
                    up_project(pe, 0, i + 2, 2 * i + 2, False)
                    down_project(pe, 1, i + 1, 2 * i + 1, False)
                down_project(pe, 0, PAIRS + 1, 2 * PAIRS, False)

            def activate(act, slot, n):
                for m in range(2):
                    act.wait_ge(up_ready, 2 * n + m + 1)
                    nc.scalar.activation(silu[:, m], g.bank[2 * m][:, 0:n_tok], ACT.Silu).then_inc(silu_ready, 1)

            @block.scalar
            def _(act):
                activate(act, 0, 0)
                with act.Fori(0, PAIRS) as i:
                    activate(act, 1, 2 * i + 1)
                    activate(act, 0, 2 * i + 2)

            def gate_up(dve, slot, n):
                for m in range(2):
                    dve.wait_ge(silu_ready, 2 * n + m + 1)
                    nc.vector.tensor_tensor(hidden[:, slot, m], silu[:, m], g.bank[2 * m + 1][:, 0:n_tok], ALU.mult).then_inc(hidden_ready, 1)

            def accumulate(dve, n, gate_col):
                for u in range(YP):
                    i, half = u // 2, u % 2
                    dve.wait_ge(y_ready, n * YP + u + 1)
                    part = acc[:, i, half * 512:(half + 1) * 512]
                    nc.vector.scalar_tensor_tensor(part, g.bank[4 + u % 4][:], gate_col(i), part, ALU.mult, ALU.add).then_inc(y_added, 1)

            @block.vector
            def _(dve):
                nc.vector.memset(acc, 0.0).then_inc(zeroed, 1)
                nc.vector.memset(gates[:, :, EXPERTS:EXPERTS + 1], 1.0).then_inc(zeroed, 1)
                dve.wait_ge(zeroed, 2)
                gate_up(dve, 0, 0)
                gate_up(dve, 1, 1)
                accumulate(dve, 0, lambda i: gates[:, i, EXPERTS:EXPERTS + 1])
                gate_up(dve, 0, 2)
                dve.wait_ge(y_added, YP)
                accumulate(dve, 1, lambda i: gates[:, i, 0:1])
                with dve.Fori(1, PAIRS) as p:
                    gate_up(dve, 1, 2 * p + 1)
                    dve.wait_ge(y_added, 2 * p * YP)
                    accumulate(dve, 2 * p, lambda i: gates[:, i, bass.ds(2 * p - 1, 1)])
                    gate_up(dve, 0, 2 * p + 2)
                    dve.wait_ge(y_added, (2 * p + 1) * YP)
                    accumulate(dve, 2 * p + 1, lambda i: gates[:, i, bass.ds(2 * p, 1)])
                dve.wait_ge(y_added, 2 * PAIRS * YP)
                accumulate(dve, 2 * PAIRS, lambda i: gates[:, i, EXPERTS - 1:EXPERTS])


def moe(g, l, tiles):
    nc = g.nc
    modulate_stage(g, l, 3, 4, tiles, 5)
    with ExitStack() as ctx:
        gates = ctx.enter_context(nc.sbuf_tensor(f"gates{l}", [P, 4, EXPERTS + 1], F32))
        acc = ctx.enter_context(nc.sbuf_tensor(f"acc{l}", [P, len(tiles), D], F32))
        router_stage(g, l, tiles, gates)
        experts_stage(g, l, tiles, gates, acc[:])
        residual_stage(g, l, 1, tiles, acc[:])


def even_layer(g):
    nc = g.nc
    modulate_stage(g, 0, 0, 1, list(range(NT)), 2)
    with ExitStack() as ctx:
        g.mix = ctx.enter_context(nc.sbuf_tensor("mix0", [P, KT, T], F32))
        with ExitStack() as c2:
            sb = lambda n, shape: c2.enter_context(nc.sbuf_tensor(n, shape, F32))
            qT, kT = sb("m_qT", [P, 2, T]), sb("m_kT", [P, 2, T])
            v1, o, y = sb("m_v1", [P, NT, HEADS, P + 1]), sb("m_o", [P, NT, 512]), sb("m_y", [P, NT, 512])
            s = {"qT": qT, "kT": kT, "v1": v1, "y": y, "a_col": sb("a_col", [P, 2, NT * HEADS]),
                 "floor_col": sb("floor_col", [P, 2, NT * HEADS]), "max_row": sb("max_row", [HEADS, 2, T])}
            ones = new_sem(g, "v_ones")
            with nc.Block() as block:
                @block.gpsimd
                def _(pool):
                    pool.memset(v1[:, :, :, P:P + 1], 1.0).then_inc(ones, 1)
                    pool.wait_ge(ones, 1)
            allt = list(range(NT))
            projection_stage(g, g.dram["even_w_in"], [
                (0, "T", allt, lambda j: (qT if j < 2 else kT)[:, j % 2], "q_scale"),
                (1, "N", allt, lambda j: v1[:, j, :, 0:P], "heads"),
                (2, "N", allt, lambda j: o[:, j], "sigmoid")])
            gates_wrapped(g, s)
            mlstm_stage(g, s)
            norm_stage(g, y[:], allt, HEADS, True, o[:], "mlstm_norm_w", 0, "m")
        with ExitStack() as c2:
            sb = lambda n, shape: c2.enter_context(nc.sbuf_tensor(n, shape, F32))
            q, v, hg, ff, fb, y = (sb(n, [P, HEADS, T]) for n in ("h_q", "h_v", "h_g", "h_ff", "h_fb", "h_y"))
            projection_stage(g, g.dram["even_w_in"], [
                (3, "T", allt, lambda j: q[:, j], "silu"),
                (4, "N", allt, lambda j: v[:, j], "copy"),
                (5, "T", allt, lambda j: ff[:, j], "sigmoid"),
                (6, "T", allt, lambda j: fb[:, j], "sigmoid"),
                (7, "N", allt, lambda j: hg[:, j], "silu")])
            hgrn_stage(g, {"q": q[:], "v": v, "f": (ff[:], fb[:]), "y": y})
            norm_stage(g, y[:], allt, HEADS, False, hg[:], "hgrn_norm_w", 4, "h")
        residual_stage(g, 0, 0, allt, None, g.dram["even_w_out"])


def gates_wrapped(g, s):
    s["n_abs"] = 1 + 4 + 1
    s["n_rows"] = s["n_abs"] + 1 + 3 + 1 + 3 + 1
    gates_stage(g, s)


def hyena_filter_stage(g, filt):
    nc = g.nc
    loaded, mm, step, act_s, hsem = (new_sem(g, x) for x in ("hyf_loaded", "hyf_mm", "hyf_step", "hyf_sin", "hyf_h"))
    TWO_PI = 2.0 * math.pi
    HI = float(np.float32(TWO_PI))
    LO = float(TWO_PI - np.float64(np.float32(TWO_PI)))
    MAGIC = 1.5 * 2.0 ** 23
    PI_F = float(np.float32(3.1415925))
    with ExitStack() as ctx:
        sb = lambda n, shape: ctx.enter_context(nc.sbuf_tensor(f"hyf_{n}", shape, F32))
        z = sb("z", [HYEMB, LAT])
        w1, w23 = sb("w1", [HYEMB, HYHID]), sb("w23", [HYHID, 2, HYHID])
        cols = sb("cols", [HYHID, 4])
        wout = sb("wout", [HYHID, 4, HYW])
        dec = sb("dec", [P, 2, 2, HYW])
        hid, x, r = sb("hid", [HYHID, LAT]), sb("x", [HYHID, LAT]), sb("r", [HYHID, LAT])
        loads = [(z[:], g.dram["t_z"]), (w1[:], g.dram["hy_w1"]), (w23[:], g.dram["hy_w23"]), (cols[:], g.dram["hy_cols"]),
                 (wout[:], g.dram["hy_wout"]), (dec[:], g.dram["t_decay"].rearrange("p (a b c) -> p a b c", a=2, b=2))]
        PER = 7
        with nc.Block() as block:
            @block.sync
            def _(sp):
                for dst, src in loads:
                    sp.dma_start(dst, src).then_inc(loaded, 16)

            @block.tensor
            def _(pe):
                pe.wait_ge(loaded, 16 * len(loads))
                for n in range(3):
                    if n:
                        pe.wait_ge(act_s, n)
                    nc.tensor.matmul(g.bank[n][0:HYHID, 0:LAT], w1[:] if n == 0 else w23[:, n - 1], z[:] if n == 0 else hid[:],
                                     start=True, stop=True).then_inc(mm, 1)
                pe.wait_ge(act_s, 3)
                for u in range(8):
                    q, i = u // 2, u % 2
                    if u >= 5:
                        pe.wait_ge(hsem, u - 4)
                    nc.tensor.matmul(g.bank[3 + u % 5][:], hid[:, i * P:(i + 1) * P], wout[:, q], start=True, stop=True).then_inc(mm, 1)

            @block.scalar
            def _(act):
                for n in range(3):
                    act.wait_ge(step, PER * (n + 1))
                    nc.scalar.activation(hid[:], x[:], ACT.Sin).then_inc(act_s, 1)

            @block.vector
            def _(dve):
                link = Chain(dve, step)
                dve.wait_ge(loaded, 16 * len(loads))
                for n in range(3):
                    dve.wait_ge(mm, n + 1)
                    link(nc.vector.tensor_scalar(x[:], g.bank[n][0:HYHID, 0:LAT], cols[:, n:n + 1], cols[:, 3:4], ALU.add, ALU.mult))
                    link(nc.vector.tensor_scalar(r[:], x[:], 1.0 / TWO_PI, MAGIC, ALU.mult, ALU.add))
                    link(nc.vector.tensor_scalar(r[:], r[:], -MAGIC, None, ALU.add))
                    link(nc.vector.scalar_tensor_tensor(x[:], r[:], -HI, x[:], ALU.mult, ALU.add))
                    link(nc.vector.scalar_tensor_tensor(x[:], r[:], -LO, x[:], ALU.mult, ALU.add))
                    link(nc.vector.tensor_scalar(x[:], x[:], PI_F, None, ALU.min))
                    link(nc.vector.tensor_scalar(x[:], x[:], -PI_F, None, ALU.max))
                for u in range(8):
                    q, i = u // 2, u % 2
                    dve.wait_ge(mm, 3 + u + 1)
                    nc.vector.tensor_tensor(filt[:, q // 2, q % 2, i], g.bank[3 + u % 5][:], dec[:, q % 2, i], ALU.mult).then_inc(hsem, 1)
                dve.wait_ge(hsem, 8)
                for order in range(2):
                    fwd, bwd = filt[:, order, 0], filt[:, order, 1]
                    link(nc.vector.tensor_tensor(fwd, fwd, bwd, ALU.add))
                    link(nc.vector.scalar_tensor_tensor(bwd, bwd, -2.0, fwd, ALU.mult, ALU.add))


def hyena_stage(g, u, filt):
    nc = g.nc
    loaded, shifted, zeroed, step = (new_sem(g, x) for x in ("hy_loaded", "hy_shifted", "hy_zeroed", "hy_step"))
    with ExitStack() as ctx:
        sb = lambda n, shape: ctx.enter_context(nc.sbuf_tensor(f"hy_{n}", shape, F32))
        HW = 3 * HYW
        with ExitStack() as c2:
            prev = c2.enter_context(nc.sbuf_tensor("hy_prev", [P, 2, HW], F32))
            nxt = c2.enter_context(nc.sbuf_tensor("hy_next", [P, 2, HW], F32))
            cw = c2.enter_context(nc.sbuf_tensor("hy_cw", [P, 4, HW], F32))
            uf = u.rearrange("p i s c -> p i (s c)")
            with nc.Block() as block:
                @block.gpsimd
                def _(pool):
                    pool.memset(prev[:, 0], 0.0).then_inc(zeroed, 1)
                    pool.memset(nxt[:, 1], 0.0).then_inc(zeroed, 1)

                @block.sync
                def _(sp):
                    sp.dma_start(cw[:], g.dram["hy_conv"]).then_inc(loaded, 16)
                    sp.wait_ge(zeroed, 2)
                    sp.dma_start(prev[1:P, 0], uf[0:P - 1, 0]).then_inc(shifted, 16)
                    sp.dma_start(prev[0:1, 1], uf[P - 1:P, 0]).then_inc(shifted, 16)
                    sp.dma_start(prev[1:P, 1], uf[0:P - 1, 1]).then_inc(shifted, 16)
                    sp.dma_start(nxt[0:P - 1, 0], uf[1:P, 0]).then_inc(shifted, 16)
                    sp.dma_start(nxt[P - 1:P, 0], uf[0:1, 1]).then_inc(shifted, 16)
                    sp.dma_start(nxt[0:P - 1, 1], uf[1:P, 1]).then_inc(shifted, 16)

                @block.vector
                def _(dve):
                    link = Chain(dve, step)
                    dve.wait_ge(loaded, 16)
                    dve.wait_ge(shifted, 96)
                    for i in range(2):
                        link(nc.vector.tensor_tensor(uf[:, i], uf[:, i], cw[:, 1], ALU.mult))
                        link(nc.vector.tensor_tensor(prev[:, i], prev[:, i], cw[:, 0], ALU.mult))
                        link(nc.vector.tensor_tensor(nxt[:, i], nxt[:, i], cw[:, 2], ALU.mult))
                        link(nc.vector.tensor_tensor(uf[:, i], uf[:, i], prev[:, i], ALU.add))
                        link(nc.vector.tensor_tensor(uf[:, i], uf[:, i], nxt[:, i], ALU.add))
                        link(nc.vector.tensor_tensor(uf[:, i], uf[:, i], cw[:, 3], ALU.add))

        dft = sb("dft", [P, 2, 2, 2, LAT])
        skip = sb("skip", [P, 2, HYW])
        ker = sb("ker", [P, 2, 2, HYW])
        spec = sb("spec", [P, 2, 2, HYW])
        tmp = sb("tmp", [P, 2, HYW])
        t_loaded, uspec, kspec, kcopied, pointed, inv, step2 = (new_sem(g, x) for x in (
            "dft_loaded", "u_spectrum", "k_spectrum", "k_copied", "spec_ready", "conv_ready", "hy_step2"))
        STEPS = 2 * 6 + 2 * 3
        z = u[:, :, 2]
        with nc.Block() as block:
            @block.sync
            def _(sp):
                sp.dma_start(dft[:], g.dram["t_dft"].rearrange("p (d c i f) -> p d c i f", d=2, c=2, i=2)).then_inc(t_loaded, 16)
                sp.dma_start(skip[:], g.dram["hy_skip"]).then_inc(t_loaded, 16)

            @block.tensor
            def _(pe):
                pe.wait_ge(t_loaded, 32)
                for order in range(2):
                    if order:
                        pe.wait_ge(step2, STEPS * order)
                    for c in range(2):
                        for f in range(2):
                            for i in range(2):
                                last = nc.tensor.matmul(g.bank[2 * c + f][:], dft[:, 0, c, i, f * P:(f + 1) * P], filt[:, order, c, i],
                                                        start=i == 0, stop=i == 1)
                    last.then_inc(kspec, 1)
                    for c in range(2):
                        for f in range(2):
                            for i in range(2):
                                last = nc.tensor.matmul(g.bank[4 + 2 * c + f][:], dft[:, 0, c, i, f * P:(f + 1) * P], z[:, i],
                                                        start=i == 0, stop=i == 1)
                    last.then_inc(uspec, 1)
                    pe.wait_ge(pointed, order + 1)
                    for i in range(2):
                        n = 0
                        for c in range(2):
                            for f in range(2):
                                last = nc.tensor.matmul(g.bank[i][:], dft[:, 1, c, f, i * P:(i + 1) * P], spec[:, c, f], start=n == 0, stop=n == 3)
                                n += 1
                    last.then_inc(inv, 1)

            @block.scalar
            def _(act):
                for order in range(2):
                    act.wait_ge(kspec, order + 1)
                    if order:
                        act.wait_ge(pointed, order)
                    for c in range(2):
                        for f in range(2):
                            nc.scalar.activation(ker[:, c, f], g.bank[2 * c + f][:], ACT.Copy).then_inc(kcopied, 1)

            @block.vector
            def _(dve):
                link = Chain(dve, step2)
                for order in range(2):
                    dve.wait_ge(uspec, order + 1)
                    dve.wait_ge(kcopied, 4 * (order + 1))
                    for f in range(2):
                        uc, us = g.bank[4 + f][:], g.bank[6 + f][:]
                        kc, ks = ker[:, 0, f], ker[:, 1, f]
                        link(nc.vector.tensor_tensor(spec[:, 0, f], uc, kc, ALU.mult))
                        link(nc.vector.tensor_tensor(tmp[:, 0], us, ks, ALU.mult))
                        link(nc.vector.tensor_tensor(spec[:, 0, f], spec[:, 0, f], tmp[:, 0], ALU.subtract))
                        link(nc.vector.tensor_tensor(spec[:, 1, f], uc, ks, ALU.mult))
                        link(nc.vector.tensor_tensor(tmp[:, 1], us, kc, ALU.mult))
                        link(nc.vector.scalar_tensor_tensor(spec[:, 1, f], spec[:, 1, f], -1.0, tmp[:, 1], ALU.mult, ALU.subtract))
                    dve.sem_inc(pointed, 1)
                    dve.wait_ge(inv, order + 1)
                    for i in range(2):
                        link(nc.vector.tensor_tensor(z[:, i], z[:, i], skip[:, order], ALU.mult))
                        link(nc.vector.tensor_tensor(z[:, i], z[:, i], g.bank[i][:], ALU.add))
                        link(nc.vector.tensor_tensor(z[:, i], z[:, i], u[:, i, order], ALU.mult))


def rope_stage(g, q, k):
    nc = g.nc
    loaded, step = new_sem(g, "rope_loaded"), new_sem(g, "rope_step")
    with ExitStack() as ctx:
        tab = ctx.enter_context(nc.sbuf_tensor("rope_tab", [P, 2, 2, P], F32))
        rot = ctx.enter_context(nc.sbuf_tensor("rope_rot", [P, 512], F32))
        with nc.Block() as block:
            @block.sync
            def _(sp):
                sp.dma_start(tab[:], g.dram["t_rope"].rearrange("p (c i d) -> p c i d", c=2, i=2)).then_inc(loaded, 16)

            @block.vector
            def _(dve):
                link = Chain(dve, step)
                dve.wait_ge(loaded, 16)
                for x, off in ((q, 0), (k, 2)):
                    for i in range(2):
                        src = x[:, i + off]
                        for h in range(HEADS):
                            xs = src[:, h * P:(h + 1) * P].rearrange("p (a b c) -> p a b c", a=2, b=2)
                            rs = rot[:, h * P:(h + 1) * P].rearrange("p (a b c) -> p a b c", a=2, b=2)
                            sn = tab[:, 1, i].rearrange("p (a b c) -> p a b c", a=2, b=2)
                            for b in range(2):
                                link(nc.vector.tensor_tensor(rs[:, :, b], xs[:, :, 1 - b], sn[:, :, b], ALU.mult))
                        cos = tab[:, 0, i].unsqueeze(1).broadcast_to([P, HEADS, P])
                        s3 = src.rearrange("p (h d) -> p h d", h=HEADS)
                        link(nc.vector.tensor_tensor(s3, s3, cos, ALU.mult))
                        link(nc.vector.tensor_tensor(src, src, rot[:], ALU.add))


def retention_stage(g, q, k, v, y):
    nc = g.nc
    loaded, turned, copied, scored, exped, weighted, summed, ycopied, step = (new_sem(g, x) for x in (
        "ret_loaded", "qk_turned", "qk_copied", "ret_scored", "ret_exp", "ret_weighted", "ret_summed", "ret_copied", "ret_step"))
    with ExitStack() as ctx:
        sb = lambda n, shape: ctx.enter_context(nc.sbuf_tensor(f"ret_{n}", shape, F32))
        delta, keep, lg = sb("delta", [P, 2, NT, LAT]), sb("keep", [P, 2, 2, LAT]), sb("lg", [P, 2, HEADS])
        qT, kT = sb("qT", [P, HEADS, LAT]), sb("kT", [P, HEADS, T])
        e = sb("e", [P, 2, 2, NT, LAT])
        with nc.Block() as block:
            @block.sync
            def _(sp):
                sp.dma_start(delta[:], g.dram["t_delta"].rearrange("p (d j t) -> p d j t", d=2, j=NT)).then_inc(loaded, 16)
                sp.dma_start(keep[:], g.dram["t_keep"].rearrange("p (d j t) -> p d j t", d=2, j=2)).then_inc(loaded, 16)
                sp.dma_start(lg[:], g.dram["ret_lg"]).then_inc(loaded, 16)

            def values(pe, h):
                pe.wait_ge(weighted, NT * (h + 1))
                if h >= 2:
                    pe.wait_ge(ycopied, h - 1)
                for i in range(2):
                    for j in range(NT):
                        last = nc.tensor.matmul(g.bank[4 + h % 2][:, i * P:(i + 1) * P], e[:, h % 2, 0, j, i * P:(i + 1) * P],
                                                v[:, j, h * P:(h + 1) * P], start=j == 0, stop=j == NT - 1)
                last.then_inc(summed, 1)

            def finish(dve, h):
                dve.wait_ge(summed, h + 1)
                nc.vector.tensor_copy(y[:, :, h * P:(h + 1) * P], g.bank[4 + h % 2][:, 0:LAT].rearrange("p (i d) -> p i d", i=2)).then_inc(ycopied, 1)

            @block.tensor
            def _(pe):
                for h in range(HEADS):
                    if h >= 2:
                        pe.wait_ge(copied, 2 * (h - 1))
                    b = g.bank[2 * (h % 2)]
                    for i in range(2):
                        last = nc.tensor.transpose(b[:, i * P:(i + 1) * P], q[:, i, h * P:(h + 1) * P], g.ident)
                    last.then_inc(turned, 1)
                    b = g.bank[2 * (h % 2) + 1]
                    for i in range(NT):
                        last = nc.tensor.transpose(b[:, i * P:(i + 1) * P], k[:, i, h * P:(h + 1) * P], g.ident)
                    last.then_inc(turned, 1)
                pe.wait_ge(copied, 2 * HEADS)
                for h in range(HEADS):
                    if h >= 2:
                        pe.wait_ge(weighted, NT * (h - 1))
                    for j in range(NT):
                        nc.tensor.matmul(g.bank[2 * (h % 2) + j // 2][:, (j % 2) * LAT:(j % 2 + 1) * LAT], kT[:, h, j * P:(j + 1) * P], qT[:, h],
                                         start=True, stop=True).then_inc(scored, 1)
                    if h >= 1:
                        values(pe, h - 1)
                values(pe, HEADS - 1)

            @block.scalar
            def _(act):
                for h in range(HEADS):
                    act.wait_ge(turned, 2 * h + 1)
                    nc.scalar.activation(qT[:, h], g.bank[2 * (h % 2)][:, 0:LAT], ACT.Copy, scale=float(P) ** -0.5).then_inc(copied, 1)
                    act.wait_ge(turned, 2 * h + 2)
                    nc.scalar.activation(kT[:, h], g.bank[2 * (h % 2) + 1][:], ACT.Copy).then_inc(copied, 1)
                act.wait_ge(loaded, 48)
                for h in range(HEADS):
                    if h >= 2:
                        act.wait_ge(summed, h - 1)
                    for d in range(2):
                        nc.scalar.activation(e[:, h % 2, d], delta[:, d], ACT.Exp, scale=lg[:, d, h:h + 1]).then_inc(exped, 1)

            @block.vector
            def _(dve):
                link = Chain(dve, step)
                dve.wait_ge(loaded, 48)
                for h in range(HEADS):
                    dve.wait_ge(exped, 2 * (h + 1))
                    ef, eb = e[:, h % 2, 0], e[:, h % 2, 1]
                    link(nc.vector.tensor_tensor(ef[:, 2:4], ef[:, 2:4], keep[:, 0], ALU.mult))
                    link(nc.vector.tensor_tensor(eb[:, 2:4], eb[:, 2:4], keep[:, 1], ALU.mult))
                    link(nc.vector.tensor_tensor(ef, ef, eb, ALU.add))
                    for j in range(NT):
                        dve.wait_ge(scored, h * NT + j // 2 * 2 + 2)
                        nc.vector.tensor_tensor(ef[:, j], ef[:, j], g.bank[2 * (h % 2) + j // 2][:, (j % 2) * LAT:(j % 2 + 1) * LAT], ALU.mult).then_inc(weighted, 1)
                    if h >= 1:
                        finish(dve, h - 1)
                finish(dve, HEADS - 1)


def odd_layer(g):
    nc = g.nc
    allt, lat = list(range(NT)), [2, 3]
    modulate_stage(g, 1, 0, 1, allt, 2)
    with ExitStack() as ctx:
        g.mix = ctx.enter_context(nc.sbuf_tensor("mix1", [P, KT, T], F32))
        with ExitStack() as c2:
            sb = lambda n, shape: c2.enter_context(nc.sbuf_tensor(n, shape, F32))
            u, filt = sb("hy_u", [P, 2, 3, HYW]), sb("hy_filt", [P, 2, 2, 2, HYW])
            hyena_filter_stage(g, filt)
            projection_stage(g, g.dram["odd_w_in"], [
                (i, "N", lat, (lambda i: lambda j: u[:, j, i])(i), "copy") for i in range(3)])
            hyena_stage(g, u[:], filt)
            norm_stage(g, u[:, :, 2], lat, HYW // GROUP, False, None, "hy_norm_w", 0, "y")
        with ExitStack() as c2:
            sb = lambda n, shape: c2.enter_context(nc.sbuf_tensor(n, shape, F32))
            q, k, v, rg, y = (sb(n, [P, w, 512]) for n, w in (("r_q", 2), ("r_k", 4), ("r_v", 4), ("r_g", 2), ("r_y", 2)))
            projection_stage(g, g.dram["odd_w_in"], [
                (3, "N", lat, lambda j: q[:, j], "copy"),
                (4, "N", allt, lambda j: k[:, j], "copy"),
                (5, "N", allt, lambda j: v[:, j], "copy"),
                (6, "N", lat, lambda j: rg[:, j], "silu")])
            rope_stage(g, q, k)
            retention_stage(g, q, k, v, y)
            norm_stage(g, y[:], lat, HEADS, True, rg[:], "ret_norm_w", 4, "r")
        residual_stage(g, 1, 0, lat, None, g.dram["odd_w_out"])


def build(nc, dram, out):
    g = Net()
    g.nc, g.dram, g.n_sems, g.sems = nc, dram, 0, []
    with ExitStack() as ctx:
        sb = lambda n, shape: ctx.enter_context(nc.sbuf_tensor(n, shape, F32))
        g.h = sb("h", [P, NT, D])
        g.xt = sb("xt", [P, KT, T])
        g.base = sb("base", [P, 5 * P + P // CHUNK])
        g.c_cols, g.c_act = sb("c_cols", [P, KT, 2]), sb("c_act", [P, KT, 2])
        g.mods = sb("mods", [P, 2, MODS * KT, 2])
        g.mod_row = sb("mod_row", [P, 2, D])
        g.ident, g.upper, g.lower = (g.base[:, i * P:(i + 1) * P] for i in range(3))
        g.tri_chunk = [g.base[:, (3 + i) * P:(4 + i) * P] for i in range(2)]
        g.chunk_of = g.base[:, 5 * P:]
        g.bank = [ctx.enter_context(nc.psum_tensor(f"bank{i}", [P, 512], F32)) for i in range(8)]
        load_stage(g)
        ada_stage(g, 0)
        ada_stage(g, 1)
        even_layer(g)
        recycle_sems(g)
        moe(g, 0, list(range(NT)))
        recycle_sems(g)
        odd_layer(g)
        recycle_sems(g)
        moe(g, 1, [2, 3])
        stored = new_sem(g, "out_stored")
        with nc.Block() as block:
            @block.sync
            def _(sp):
                sp.dma_start(out.rearrange("b (i p) d -> p (b i) d", p=P), g.h[:, 2:4]).then_inc(stored, 16)
                sp.wait_ge(stored, 16)


def on_rows(a):
    return np.ascontiguousarray(np.broadcast_to(a[..., None, :, :] if a.ndim > 1 else a[None, None, :], a.shape[:-2] + (P,) + a.shape[-2:] if a.ndim > 1 else (P, 1) + a.shape))


def layout(i):
    i = {k: np.asarray(v) for k, v in i.items()}
    L = 2
    a = dict(shape_tables())
    tok = np.concatenate([i["ctx"][0], i["x"][0]], 0)
    a["x_all"] = tok.reshape(NT, P, D).transpose(1, 0, 2)
    a["c_cols"] = np.stack([i["c"][0], i["c_ctx"]]).reshape(2, KT, P).transpose(2, 1, 0)
    a["ada_w"] = i["ada_w"].reshape(L, KT, P, MODS * D // 512, 512).transpose(0, 3, 2, 1, 4)
    a["ada_b"] = i["ada_b"].reshape(L, MODS * KT, P).transpose(0, 2, 1)
    ln = np.stack([i["ln_w"], i["ln_b"]], 2)
    a["ln_rows"] = np.broadcast_to(ln[:, :, None], (L, 2, P, 2, D))
    we = i["even_w_in"][0]
    groups, gates = np.concatenate([we[:, :1536], we[:, 1552:]], 1), we[:, 1536:1552]
    a["even_w_in"] = groups.reshape(KT, P, 8, 512).transpose(2, 1, 0, 3)
    a["w_gates"] = gates.reshape(KT, P, 16).transpose(1, 0, 2)
    a["gate_b"] = i["mlstm_gate_b"][0].T
    a["odd_w_in"] = i["odd_w_in"][0].reshape(KT, P, 7, 512).transpose(2, 1, 0, 3)
    for n in ("even_w_out", "odd_w_out"):
        a[n] = i[n][0].reshape(KT, P, D).transpose(1, 0, 2)
    for n in ("mlstm_norm_w", "hgrn_norm_w", "ret_norm_w", "hy_norm_w"):
        a[n] = np.broadcast_to(i[n][0][None], (P, 512))
    a["lb_cols"] = i["hgrn_lb"][0].reshape(HEADS, P).T
    a["hy_conv"] = np.broadcast_to(np.concatenate([i["hy_conv_w"][0], i["hy_conv_b"]], 0)[None], (P, 4, 3 * HYW))
    a["hy_w1"] = i["hy_f_w1"][0]
    a["hy_w23"] = np.stack([i["hy_f_w2"][0], i["hy_f_w3"][0]], 1)
    a["hy_cols"] = np.stack([i["hy_f_b1"][0], i["hy_f_b2"][0], i["hy_f_b3"][0], i["hy_f_freq"][0]], 1)
    a["hy_wout"] = i["hy_f_wout"][0].reshape(HYHID, 4, HYW)
    a["hy_skip"] = np.broadcast_to(i["hy_skip"][0][None], (P, 2, HYW))
    a["ret_lg"] = np.broadcast_to(i["ret_log_decay"][0][None], (P, 2, HEADS))
    a["router_w"] = i["router_w"].reshape(L, KT, P, EXPERTS).transpose(0, 2, 1, 3)
    a["router_b"] = np.broadcast_to(i["router_bias"][:, None], (L, P, EXPERTS))

    def expert_rows(w1, w3, w2):
        n = w1.shape[:-2]
        up = [w.reshape(*n, KT, P, HID).swapaxes(-3, -2).reshape(*n, P, KT * HID) for w in (w1, w3)]
        down = w2.reshape(*n, 2, P, D).swapaxes(-3, -2).reshape(*n, P, 2 * D)
        return np.concatenate([*up, down], -1)
    routed = expert_rows(i["exp_w1"], i["exp_w3"], i["exp_w2"])
    shared = expert_rows(i["sh_w1"], i["sh_w3"], i["sh_w2"])[:, None]
    a["experts"] = np.concatenate([shared, routed, ], 1).reshape(L * (EXPERTS + 1), P, WEXP)
    return {k: np.ascontiguousarray(v) for k, v in a.items()}


def kernel(**inputs):
    import concourse.bacc as bacc
    from concourse.bass_utils import run_bass_kernel_spmd

    nc = bacc.Bacc("TRN2", target_bir_lowering=False, num_devices=1)
    arrays = {f"in_{k}": v for k, v in layout(inputs).items()}
    dram = {k[3:]: nc.dram_tensor(k, v.shape, F32, kind="ExternalInput").ap() for k, v in arrays.items()}
    out = nc.dram_tensor("out", (1, LAT, D), F32, kind="ExternalOutput").ap()
    build(nc, dram, out)
    return run_bass_kernel_spmd(nc, [arrays], core_ids=[0]).results[0]["out"]
```

```python
import math
from contextlib import ExitStack

import numpy as np
import concourse.bass as bass
from concourse import mybir

P = 128
D = 1024
KT = D // P
T = 512
NT = T // P
CTX = 256
LAT = 256
TW = 512
HEADS = 4
CHUNK = 32
NCH = T // CHUNK
MODS = 6
EXPERTS = 64
TOPK = 8
HID = 256
ROUTED_SCALE = 2.5
ALPHA = 4.0 ** 0.25
EPS = 1e-5
NEG_BIG = -1e30
TINY = 2.0 ** -63
SKIP = 4095
MAX_BLOCKS = (EXPERTS + (T * TOPK - EXPERTS) // P + 1) // 2 * 2
MIN_BLOCKS = T * TOPK // P
CLEAR = 8
MIN_PAIRS = TOPK // 2
HYW = 512
HYHID = 64
HYEMB = 33
NFREQ = 256
GROUP = 64
W13 = 2 * KT * HID
WEXP = W13 + 2 * D
EVEN_GROUPS = ("qk", "v", "o", "hq", "hi", "ff", "fb", "hg")
ODD_GROUPS = ("gate0", "gate1", "z", "rq", "rk", "rv", "rg")

F32 = mybir.dt.float32
U32 = mybir.dt.uint32
ALU = mybir.AluOpType
ACT = mybir.ActivationFunctionType
AX = mybir.AxisListType


def shape_tables():
    i = np.arange(P)
    ident = np.eye(P, dtype=np.float32)
    upper = (i[:, None] <= i[None, :]).astype(np.float32)
    lower = (i[:, None] >= i[None, :]).astype(np.float32)
    same = (i[:, None] // CHUNK) == (i[None, :] // CHUNK)
    chunk_of = (i[:, None] // CHUNK == np.arange(P // CHUNK)[None, :]).astype(np.float32)
    iota_e = np.broadcast_to(np.arange(EXPERTS, dtype=np.float32), (P, EXPERTS))
    base = np.concatenate([ident, upper, lower, upper * same, lower * same, chunk_of, iota_e,
                           i[:, None].astype(np.float32), np.ones((P, P), np.float32)], axis=1)
    negsel = np.zeros((HEADS, HEADS, P), np.float32)
    for h in range(HEADS):
        negsel[h, h] = -1.0

    pos = np.arange(LAT, dtype=np.float32)
    inv = (np.float32(10000.0) ** (-np.arange(0, 64, 2, dtype=np.float32) / np.float32(64))).astype(np.float32)
    parts_c, parts_s = [], []
    for p in (np.floor(pos / 64), np.mod(pos, 64)):
        ang = (p[:, None].astype(np.float32) * inv[None, :]).astype(np.float32)
        c, s = np.cos(ang).astype(np.float32), np.sin(ang).astype(np.float32)
        parts_c += [c, c]
        parts_s += [-s, s]
    rope = np.stack([np.concatenate(parts_c, 1), np.concatenate(parts_s, 1)])
    rope = rope.reshape(2, 2, P, P).transpose(2, 0, 1, 3).reshape(P, -1)

    s = np.arange(T)[:, None]
    t = np.arange(LAT)[None, :]
    is_ctx = s < CTX
    d_fwd = np.where(is_ctx, CTX + t - s, t - (s - CTX))
    d_bwd = np.where(is_ctx, CTX - t + s, (s - CTX) - t)
    delta = np.stack([np.maximum(d_fwd, 0), np.maximum(d_bwd, 0)]).astype(np.float32)
    keep = np.stack([d_fwd >= 0, d_bwd >= 0]).astype(np.float32)[:, CTX:]
    delta = delta.reshape(2, NT, P, LAT).transpose(2, 0, 1, 3).reshape(P, -1)
    keep = keep.reshape(2, 2, P, LAT).transpose(2, 0, 1, 3).reshape(P, -1)

    lags = np.arange(LAT, dtype=np.float64)
    omega = 2.0 * np.pi * (np.arange(NFREQ) + 0.5) / (2 * LAT)
    cos = np.cos(lags[:, None] * omega[None, :]).astype(np.float32)
    sin = np.sin(lags[:, None] * omega[None, :]).astype(np.float32)
    fwd = np.stack([cos, sin]).reshape(2, 2, P, NFREQ).transpose(2, 0, 1, 3).reshape(P, -1)
    inv_t = np.stack([cos.T, -sin.T]).astype(np.float64) / NFREQ
    inv_t = inv_t.astype(np.float32).reshape(2, 2, P, LAT).transpose(2, 0, 1, 3).reshape(P, -1)
    dft = np.concatenate([fwd, inv_t], axis=1)

    tt = (pos / np.float32(LAT - 1))[:, None]
    bands = (HYEMB - 1) // 2
    w = (np.float32(2.0 * math.pi) * pos[:, None] / np.float32(LAT)
         * np.linspace(1e-4, bands - 1, bands, dtype=np.float32)[None, :]).astype(np.float32)
    z = np.concatenate([tt, np.cos(w), np.sin(w)], -1).astype(np.float32)
    deltas = np.abs(np.linspace(math.log(1e-2) / 1.5, math.log(1e-2) / 0.3, HYW, dtype=np.float32))
    decay = np.exp(-tt * deltas[None, :]).astype(np.float32)
    decay_b = decay.copy()
    decay_b[0] = 0.0
    decay = np.stack([decay, decay_b]).reshape(2, 2, P, HYW).transpose(2, 0, 1, 3).reshape(P, -1)
    return {
        "t_base": base, "t_negsel": negsel.reshape(HEADS, -1), "t_rope": rope, "t_delta": delta,
        "t_keep": keep, "t_dft": dft, "t_z": np.ascontiguousarray(z.T), "t_decay": decay,
    }


class Net:
    pass


def new_sem(g, name):
    g.n_sems += 1
    sem = g.nc.alloc_semaphore(f"{name}_{g.n_sems}")
    g.sems.append(sem)
    return sem


def recycle_sems(g):
    g.nc.clear_and_free_semaphores(g.sems)
    g.sems = []
    g.nc.all_engine_barrier()


class Chain:

    def __init__(self, eng, sem):
        self.eng, self.sem, self.n = eng, sem, 0

    def __call__(self, ins):
        self.n += 1
        ins.then_inc(self.sem, 1)
        self.eng.wait_ge(self.sem, self.n)


def load_stage(g):
    nc = g.nc
    loaded = new_sem(g, "const_loaded")
    act_done = new_sem(g, "silu_done")
    zeroed = new_sem(g, "zero_row_ready")
    loads = [(g.h[:], g.dram["x_all"]), (g.base[:], g.dram["t_base"]), (g.c_cols[:], g.dram["c_cols"])]
    with nc.Block() as block:
        @block.sync
        def _(sp):
            for dst, src in loads:
                sp.dma_start(dst, src).then_inc(loaded, 16)

        @block.gpsimd
        def _(pool):
            pool.memset(g.zero_row[:], 0.0).then_inc(zeroed, 1)
            pool.wait_ge(zeroed, 1)

        @block.scalar
        def _(act):
            act.wait_ge(loaded, 16 * len(loads))
            nc.scalar.activation(g.c_act[:], g.c_cols[:], ACT.Silu).then_inc(act_done, 1)
            act.wait_ge(act_done, 1)


def ada_stage(g, l):
    nc = g.nc
    NCH_A, SLOTS = MODS * D // 512, 4
    loaded = [new_sem(g, "ada_w_loaded") for _ in range(SLOTS)]
    bias_loaded, used, summed, added = (new_sem(g, n) for n in ("ada_b_loaded", "ada_w_used", "ada_summed", "ada_added"))
    with ExitStack() as ctx:
        ring = ctx.enter_context(nc.sbuf_tensor(f"ada_ring{l}", [P, SLOTS, KT, 512], F32))
        bias = ctx.enter_context(nc.sbuf_tensor(f"ada_bias{l}", [P, MODS * KT], F32))
        ps = g.bank[0][:, 0:MODS * KT * 2]
        with nc.Block() as block:
            @block.sync
            def _(sp):
                sp.dma_start(bias[:], g.dram["ada_b"][l]).then_inc(bias_loaded, 16)
                for c in range(NCH_A):
                    if c >= SLOTS:
                        sp.wait_ge(used, c - SLOTS + 1)
                    sp.dma_start(ring[:, c % SLOTS], g.dram["ada_w"][l, c]).then_inc(loaded[c % SLOTS], 16)

            @block.tensor
            def _(pe):
                for c in range(NCH_A):
                    pe.wait_ge(loaded[c % SLOTS], 16 * (c // SLOTS + 1))
                    for j in range(4):
                        m = 4 * c + j
                        for k in range(KT):
                            last = nc.tensor.matmul(ps[:, 2 * m:2 * m + 2], ring[:, c % SLOTS, k, j * P:(j + 1) * P],
                                                    g.c_act[:, k, :], start=k == 0, stop=k == KT - 1)
                    last.then_inc(used, 1)

            @block.vector
            def _(dve):
                link = Chain(dve, added)
                dve.wait_ge(used, NCH_A)
                dve.wait_ge(bias_loaded, 16)
                mods = g.mods[:, l]
                link(nc.vector.tensor_tensor(mods, ps.rearrange("p (m v) -> p m v", v=2),
                                             bias[:].unsqueeze(2).broadcast_to([P, MODS * KT, 2]), ALU.add))
                for which in (1, 4):
                    part = mods[:, which * KT:(which + 1) * KT, :]
                    link(nc.vector.tensor_scalar(part, part, 1.0, None, ALU.add))


def modulate_stage(g, l, shift, scale, tiles, rows):
    nc = g.nc
    t0, n = tiles[0] * P, len(tiles) * P
    streams = [(1, 0, CTX), (0, CTX, T)] if tiles[0] == 0 else [(0, CTX, T)]
    turned, modulated, row_ready, row_copied = (new_sem(g, x) for x in ("turned", "modulated", "row_ready", "row_copied"))
    mods = g.mods[:, l]
    with nc.Block() as block:
        @block.tensor
        def _(pe):
            for k in range(KT):
                if k >= 4:
                    pe.wait_ge(modulated, len(streams) * (k - 3))
                for i in tiles:
                    last = nc.tensor.transpose(g.bank[k % 4][:, i * P:(i + 1) * P], g.h[:, i, k * P:(k + 1) * P], g.ident)
                last.then_inc(turned, 1)
            for v in range(2):
                for k in range(KT):
                    col = mods[:, rows * KT + k, v:v + 1].broadcast_to([P, P])
                    last = nc.tensor.matmul(g.bank[4 + 2 * v + k // 4][:, (k % 4) * P:(k % 4 + 1) * P], col, g.ident,
                                            start=True, stop=True)
            last.then_inc(row_ready, 1)

        @block.scalar
        def _(act):
            for k in range(KT):
                act.wait_ge(turned, k + 1)
                for v, a, b in streams:
                    nc.scalar.activation(g.xt[:, k, a:b], g.bank[k % 4][:, a:b], ACT.Identity,
                                         bias=mods[:, shift * KT + k, v:v + 1],
                                         scale=mods[:, scale * KT + k, v:v + 1]).then_inc(modulated, 1)

        @block.vector
        def _(dve):
            dve.wait_ge(row_ready, 1)
            for v in range(2):
                for half in range(2):
                    nc.vector.tensor_copy(g.mod_row[:, v, half * 512:(half + 1) * 512],
                                          g.bank[4 + 2 * v + half][:]).then_inc(row_copied, 1)


def projection_stage(g, weights, jobs):
    nc = g.nc
    SLOTS = 3
    loaded = [new_sem(g, "w_in_loaded") for _ in range(SLOTS)]
    produced, squashed, act_evac, dve_evac = (new_sem(g, x) for x in ("proj_produced", "proj_sigmoid", "proj_act_evac", "proj_dve_evac"))
    outs = []
    for gi, (_, kind, tiles, dst, fn) in enumerate(jobs):
        for j in (range(4) if kind == "T" else range(len(tiles))):
            outs.append((gi, kind, tiles, j, dst, fn))
    last_of = {gi: n for n, (gi, *_) in enumerate(outs)}
    emptied, counts = [], {"act": 0, "dve": 0}
    for *_, fn in outs:
        who = "act" if fn == "sigmoid" else "dve"
        counts[who] += 1
        emptied.append((act_evac if who == "act" else dve_evac, counts[who]))
    silus = [n for n, o in enumerate(outs) if o[-1] == "silu"]
    with ExitStack() as ctx:
        ring = ctx.enter_context(nc.sbuf_tensor(f"w_in_ring{g.n_sems}", [P, SLOTS, KT, 512], F32))
        sig = ctx.enter_context(nc.sbuf_tensor(f"sig{g.n_sems}", [P, 2, 512], F32))
        with nc.Block() as block:
            @block.sync
            def _(sp):
                for gi, (w, *_) in enumerate(jobs):
                    if gi >= SLOTS:
                        sp.wait_ge(produced, last_of[gi - SLOTS] + 1)
                    sp.dma_start(ring[:, gi % SLOTS], weights[w]).then_inc(loaded[gi % SLOTS], 16)

            @block.tensor
            def _(pe):
                for n, (gi, kind, tiles, j, dst, fn) in enumerate(outs):
                    w = ring[:, gi % SLOTS]
                    if j == 0:
                        pe.wait_ge(loaded[gi % SLOTS], 16 * (gi // SLOTS + 1))
                    if n >= 8:
                        pe.wait_ge(*emptied[n - 8])
                    a, b = tiles[0] * P, (tiles[-1] + 1) * P
                    for k in range(KT):
                        if kind == "T":
                            last = nc.tensor.matmul(g.bank[n % 8][:, 0:b - a], w[:, k, j * P:(j + 1) * P], g.xt[:, k, a:b],
                                                    start=k == 0, stop=k == KT - 1)
                        else:
                            i = tiles[j]
                            last = nc.tensor.matmul(g.bank[n % 8][:], g.xt[:, k, i * P:(i + 1) * P], w[:, k, :],
                                                    start=k == 0, stop=k == KT - 1)
                    last.then_inc(produced, 1)

            @block.scalar
            def _(act):
                for n, (gi, kind, tiles, j, dst, fn) in enumerate(outs):
                    wd = (tiles[-1] + 1 - tiles[0]) * P if kind == "T" else 512
                    src = g.bank[n % 8][:, 0:wd]
                    if fn == "sigmoid":
                        act.wait_ge(produced, n + 1)
                        nc.scalar.activation(dst(j), src, ACT.Sigmoid).then_inc(act_evac, 1)
                    elif fn == "silu":
                        m = silus.index(n)
                        act.wait_ge(produced, n + 1)
                        if m >= 2:
                            act.wait_ge(*emptied[silus[m - 2]])
                        nc.scalar.activation(sig[:, m % 2, 0:wd], src, ACT.Sigmoid).then_inc(squashed, 1)

            @block.vector
            def _(dve):
                for n, (gi, kind, tiles, j, dst, fn) in enumerate(outs):
                    wd = (tiles[-1] + 1 - tiles[0]) * P if kind == "T" else 512
                    src = g.bank[n % 8][:, 0:wd]
                    if fn == "sigmoid":
                        continue
                    if fn == "silu":
                        m = silus.index(n)
                        dve.wait_ge(squashed, m + 1)
                        nc.vector.tensor_tensor(dst(j), src, sig[:, m % 2, 0:wd], ALU.mult).then_inc(dve_evac, 1)
                        continue
                    dve.wait_ge(produced, n + 1)
                    if fn == "heads":
                        src = src.rearrange("p (h d) -> p h d", h=HEADS)
                    if fn == "q_scale" and j < 2:
                        nc.vector.tensor_scalar(dst(j), src, 64.0 ** -0.5, None, ALU.mult).then_inc(dve_evac, 1)
                    else:
                        nc.vector.tensor_copy(dst(j), src).then_inc(dve_evac, 1)


def mlstm_tiles(d, j):
    if d == 0:
        return [(j, j + 1)] + ([(j + 1, NT)] if j + 1 < NT else [])
    if j >= 2:
        return [(j, j + 1)] + ([(2, j)] if j > 2 else [])
    return [(j, j + 1)] + ([(0, j)] if j > 0 else []) + [(2, NT)]


def key_tiles(d, i):
    return [j for j in range(NT) if any(a <= i < b for a, b in mlstm_tiles(d, j))]


def gates_stage(g, s):
    nc = g.nc
    loaded, made, activated, step, turned = (new_sem(g, x) for x in ("gate_w_loaded", "gates_made", "gate_act", "gate_step", "gate_turned"))
    act_step = new_sem(g, "gate_act_step")
    with ExitStack() as ctx:
        wg = ctx.enter_context(nc.sbuf_tensor("w_gates", [P, KT, 4 * HEADS], F32))
        gb = ctx.enter_context(nc.sbuf_tensor("gate_b", [HEADS, 4], F32))
        tmp = {n: ctx.enter_context(nc.sbuf_tensor(f"gate_{n}", [HEADS, 2, T], F32)) for n in ("x", "e", "lf", "B", "a", "m", "ones")}
        with nc.Block() as block:
            @block.sync
            def _(sp):
                sp.dma_start(wg[:], g.dram["w_gates"]).then_inc(loaded, 16)
                sp.dma_start(gb[:], g.dram["gate_b"]).then_inc(loaded, 16)

            @block.tensor
            def _(pe):
                pe.wait_ge(loaded, 32)
                for q in range(4):
                    for k in range(KT):
                        last = nc.tensor.matmul(g.bank[q][0:HEADS, :], wg[:, k, q * HEADS:(q + 1) * HEADS], g.xt[:, k, :],
                                                start=k == 0, stop=k == KT - 1)
                last.then_inc(made, 1)
                pe.wait_ge(step, s["n_rows"])
                for d in range(2):
                    for c, src in enumerate((tmp["a"], tmp["m"])):
                        for i in range(NT):
                            at = ((d * 2 + c) * NT + i) * HEADS
                            last = nc.tensor.transpose(g.bank[4][:, at:at + HEADS], src[:, d, i * P:(i + 1) * P],
                                                       g.ident[0:HEADS, 0:HEADS])
                last.then_inc(turned, 1)

            @block.scalar
            def _(act):
                act.wait_ge(step, s["n_abs"])
                nc.scalar.activation(tmp["e"][:], tmp["e"][:], ACT.Exp, scale=-1.0).then_inc(act_step, 1)
                act.wait_ge(act_step, 1)
                nc.scalar.activation(tmp["e"][:], tmp["e"][:], ACT.Ln, bias=1.0).then_inc(activated, 1)
                act.wait_ge(turned, 1)
                cols = g.bank[4][:, 0:2 * 2 * NT * HEADS].rearrange("p (d c i) -> p d c i", d=2, c=2)
                nc.scalar.activation(s["a_col"][:], cols[:, :, 0, :], ACT.Copy).then_inc(activated, 1)
                nc.scalar.activation(s["floor_col"][:], cols[:, :, 1, :], ACT.Exp, scale=-1.0).then_inc(activated, 1)

            @block.vector
            def _(dve):
                link = Chain(dve, step)
                link(nc.vector.memset(tmp["ones"][:], 1.0))
                dve.wait_ge(made, 1)
                for d in range(2):
                    link(nc.vector.tensor_scalar(tmp["x"][:, d], g.bank[2 * d + 1][0:HEADS, :], gb[:, 2 * d + 1:2 * d + 2], None, ALU.add))
                    link(nc.vector.tensor_scalar(tmp["a"][:, d], g.bank[2 * d][0:HEADS, :], gb[:, 2 * d:2 * d + 1], None, ALU.add))
                link(nc.vector.scalar_tensor_tensor(tmp["e"][:], tmp["x"][:], -1.0, tmp["x"][:], ALU.mult, ALU.max))
                s["n_abs"] = link.n
                dve.wait_ge(activated, 1)
                link(nc.vector.scalar_tensor_tensor(tmp["lf"][:], tmp["x"][:], 0.0, tmp["e"][:], ALU.min, ALU.subtract))
                ones, lf, B, a, M = tmp["ones"], tmp["lf"], tmp["B"], tmp["a"], s["max_row"]
                link(nc.vector.tensor_tensor_scan(B[:, 0, :], ones[:, 0, :], lf[:, 0, :], 0.0, ALU.mult, ALU.add))
                link(nc.vector.tensor_tensor_scan(B[:, 1, 0:CTX][:, ::-1], ones[:, 0, 0:CTX], lf[:, 1, 0:CTX][:, ::-1], 0.0, ALU.mult, ALU.add))
                link(nc.vector.tensor_tensor_scan(B[:, 1, CTX:T][:, ::-1], ones[:, 0, 0:LAT], lf[:, 1, CTX:T][:, ::-1], B[:, 1, 0:1], ALU.mult, ALU.add))
                link(nc.vector.tensor_tensor(a[:], a[:], B[:], ALU.subtract))
                link(nc.vector.tensor_tensor_scan(M[:, 0, :], a[:, 0, :], a[:, 0, :], NEG_BIG, ALU.max, ALU.max))
                ac, al = a[:, 1, 0:CTX][:, ::-1], a[:, 1, CTX:T][:, ::-1]
                link(nc.vector.tensor_tensor_scan(M[:, 1, 0:CTX][:, ::-1], ac, ac, NEG_BIG, ALU.max, ALU.max))
                link(nc.vector.tensor_tensor_scan(M[:, 1, CTX:T][:, ::-1], al, al, M[:, 1, 0:1], ALU.max, ALU.max))
                link(nc.vector.tensor_tensor(tmp["m"][:], B[:], M[:], ALU.add))
                s["n_rows"] = link.n


def mlstm_stage(g, s):
    nc = g.nc
    scored, row_max_ready, clamped, exped, weighted, read, summed, step = (
        new_sem(g, x) for x in ("scores_ready", "max_rows_ready", "clamped", "exp_ready", "weights_ready",
                                "scores_used", "values_summed", "dve_step"))
    pool_masked = new_sem(g, "diag_masked")
    units = [(h, d) for h in range(HEADS) for d in range(2)]
    pieces = [(u, j, n, rng) for u, (h, d) in enumerate(units) for j in range(NT)
              for n, rng in enumerate(mlstm_tiles(d, j))]
    tri = {0: g.upper, 1: g.lower}
    with ExitStack() as ctx:
        e = ctx.enter_context(nc.sbuf_tensor("mlstm_e", [P, 2, NT, T], F32))
        sm = ctx.enter_context(nc.sbuf_tensor("mlstm_small", [P, 2, 3, NT], F32))
        loaded = new_sem(g, "negsel_loaded")
        negsel = ctx.enter_context(nc.sbuf_tensor("negsel", [HEADS, HEADS, P], F32))
        S = g.bank[0:4]
        ndone = {u: sum(1 for p in pieces if p[0] <= u) for u in range(len(units))}
        ndone[-1] = 0
        with nc.Block() as block:
            @block.sync
            def _(sp):
                sp.dma_start(negsel[:], g.dram["t_negsel"].rearrange("h (a b) -> h a b", a=HEADS)).then_inc(loaded, 16)
                src = g.zero_row[:].unsqueeze(1).broadcast_to([P, CLEAR, D])
                for b in range(MIN_BLOCKS, MAX_BLOCKS, CLEAR):
                    sp.dma_start(g.y_dram[b:b + CLEAR].rearrange("b p d -> p b d"), src).then_inc(g.y_cleared, 16)

            @block.tensor
            def _(pe):
                pe.wait_ge(loaded, 16)

                def scores(u):
                    h, d = units[u]
                    if u >= 2:
                        pe.wait_ge(clamped, ndone[u - 2])
                    nc.tensor.matmul(g.bank[4 + d][:], negsel[:, h, :], s["max_row"][:, d, :], start=True, stop=True).then_inc(row_max_ready, 1)
                    if d == 0:
                        if u >= 1:
                            pe.wait_ge(weighted, ndone[u - 1])
                        r = slice(64 * (h % 2), 64 * (h % 2) + 64)
                        for j in range(NT):
                            nc.tensor.matmul(S[j][:], s["kT"][r, h // 2, j * P:(j + 1) * P], s["qT"][r, h // 2, :],
                                             start=True, stop=True).then_inc(scored, 1)

                def values(u):
                    h, d = units[u]
                    pe.wait_ge(weighted, ndone[u])
                    if u >= 1:
                        pe.wait_ge(read, u)
                    for i in range(NT):
                        keys = key_tiles(d, i)
                        for j in keys:
                            last = nc.tensor.matmul(g.bank[6 + i // 2][:, (i % 2) * 256:(i % 2) * 256 + P + 1],
                                                    e[:, u % 2, j, i * P:(i + 1) * P], s["v1"][:, j, h, :],
                                                    start=j == keys[0], stop=j == keys[-1])
                    last.then_inc(summed, 1)

                scores(0)
                for u in range(len(units)):
                    if u + 1 < len(units) and units[u + 1][1] == 1:
                        scores(u + 1)
                        values(u)
                    elif u + 1 < len(units):
                        scores(u + 1)
                        values(u)
                    else:
                        values(u)

            @block.scalar
            def _(act):
                for n, (u, j, k, (a, b)) in enumerate(pieces):
                    act.wait_ge(clamped, n + 1)
                    w = e[:, u % 2, j, a * P:b * P]
                    nc.scalar.activation(w, w, ACT.Exp).then_inc(exped, 1)

            @block.vector
            def _(dve):
                link = Chain(dve, step)
                dve_n = 0

                def clamp(u):
                    h, d = units[u]
                    dve.wait_ge(row_max_ready, u + 1)
                    if u >= 2:
                        dve.wait_ge(summed, u - 1)
                    for (uu, j, k, (a, b)) in pieces:
                        if uu == u:
                            nc.vector.tensor_scalar(e[:, u % 2, j, a * P:b * P], g.bank[4 + d][:, a * P:b * P],
                                                    s["a_col"][:, d, j * HEADS + h:j * HEADS + h + 1], 0.0,
                                                    ALU.add, ALU.min).then_inc(clamped, 1)

                def weigh(u):
                    h, d = units[u]
                    for n, (uu, j, k, (a, b)) in enumerate(pieces):
                        if uu != u:
                            continue
                        dve.wait_ge(exped, n + 1)
                        w = e[:, u % 2, j, a * P:b * P]
                        if k == 0:
                            if d == 0:
                                dve.wait_ge(scored, h * NT + j + 1)
                            link(nc.vector.tensor_tensor(w, w, tri[d], ALU.mult))
                        nc.vector.tensor_tensor(w, w, S[j][:, a * P:b * P], ALU.mult).then_inc(weighted, 1)

                def finish(u):
                    h, d = units[u]
                    dve.wait_ge(summed, u + 1)
                    x = sm[:, u % 2]
                    den, neg, inv = x[:, 0], x[:, 1], x[:, 2]
                    for half in range(2):
                        b = g.bank[6 + half][:].rearrange("p (i w) -> p i w", i=2)[:, :, P]
                        link(nc.vector.tensor_copy(den[:, 2 * half:2 * half + 2], b))
                    link(nc.vector.scalar_tensor_tensor(neg, den, -1.0, den, ALU.mult, ALU.max))
                    fl = s["floor_col"][:, d].rearrange("p (i h) -> p i h", h=HEADS)[:, :, h]
                    link(nc.vector.tensor_tensor(neg, neg, fl, ALU.max))
                    link(nc.vector.reciprocal(inv, neg))
                    for i in range(NT):
                        src = g.bank[6 + i // 2][:, (i % 2) * 256:(i % 2) * 256 + P]
                        dst = s["y"][:, i, h * P:(h + 1) * P]
                        if d == 0:
                            ins = nc.vector.tensor_scalar(dst, src, inv[:, i:i + 1], None, ALU.mult)
                        else:
                            ins = nc.vector.scalar_tensor_tensor(dst, src, inv[:, i:i + 1], dst, ALU.mult, ALU.add)
                        link(ins)
                    dve.sem_inc(read, 1)

                clamp(0)
                for u in range(len(units)):
                    if u + 1 < len(units):
                        clamp(u + 1)
                    weigh(u)
                    finish(u)


def norm_stage(g, y, tiles, groups, center, gate, w_name, mix_base, tag):
    nc = g.nc
    nt = len(tiles)
    width = 512 // groups
    loaded, step, rooted, turned, copied = (new_sem(g, x) for x in ("norm_w_loaded", "norm_step", "norm_root", "mix_turned", "mix_copied"))
    with ExitStack() as ctx:
        sq = ctx.enter_context(nc.sbuf_tensor(f"norm_sq_{tag}", [P, nt, 512], F32))
        st = ctx.enter_context(nc.sbuf_tensor(f"norm_st_{tag}", [P, 2, nt, groups], F32))
        w = ctx.enter_context(nc.sbuf_tensor(f"norm_w_{tag}", [P, 512], F32))
        marks = {}
        flat = y.rearrange("p i (n w) -> p i n w", w=width)
        sqf = sq[:].rearrange("p i (n w) -> p i n w", w=width)
        with nc.Block() as block:
            @block.sync
            def _(sp):
                sp.dma_start(w[:], g.dram[w_name]).then_inc(loaded, 16)

            @block.vector
            def _(dve):
                link = Chain(dve, step)
                if center:
                    link(nc.vector.tensor_reduce(st[:, 0], flat, AX.X, ALU.add))
                    link(nc.vector.tensor_scalar(st[:, 0], st[:, 0], 1.0 / width, None, ALU.mult))
                    link(nc.vector.tensor_tensor(flat, flat, st[:, 0].unsqueeze(3).broadcast_to([P, nt, groups, width]), ALU.subtract))
                link(nc.vector.tensor_tensor(sq[:], y, y, ALU.mult))
                link(nc.vector.tensor_reduce(st[:, 1], sqf, AX.X, ALU.add))
                link(nc.vector.tensor_scalar(st[:, 1], st[:, 1], 1.0 / width, EPS, ALU.mult, ALU.add))
                marks["var"] = link.n
                dve.wait_ge(rooted, 1)
                link(nc.vector.reciprocal(st[:, 1], st[:, 1]))
                link(nc.vector.tensor_tensor(flat, flat, st[:, 1].unsqueeze(3).broadcast_to([P, nt, groups, width]), ALU.mult))
                dve.wait_ge(loaded, 16)
                link(nc.vector.tensor_tensor(y, y, w[:].unsqueeze(1).broadcast_to([P, nt, 512]), ALU.mult))
                if gate is not None:
                    link(nc.vector.tensor_tensor(y, y, gate, ALU.mult))
                marks["gated"] = link.n

            @block.scalar
            def _(act):
                act.wait_ge(step, marks["var"])
                nc.scalar.activation(st[:, 1], st[:, 1], ACT.Sqrt).then_inc(rooted, 1)
                for c in range(4):
                    act.wait_ge(turned, c + 1)
                    nc.scalar.activation(g.mix[:, mix_base + c, tiles[0] * P:(tiles[-1] + 1) * P],
                                         g.bank[c][:, 0:nt * P], ACT.Copy).then_inc(copied, 1)

            @block.tensor
            def _(pe):
                pe.wait_ge(step, marks["gated"])
                for c in range(4):
                    for n in range(nt):
                        last = nc.tensor.transpose(g.bank[c][:, n * P:(n + 1) * P], y[:, n, c * P:(c + 1) * P], g.ident)
                    last.then_inc(turned, 1)


def hgrn_stage(g, s):
    nc = g.nc
    TILE_CH = P // CHUNK
    SR = TILE_CH + 1
    (lb_loaded, prep, act_prep, vmasked, zeroed, turned, k1_ready, scored, masked, located, stated, out_ready,
     added) = (new_sem(g, x) for x in (
        "lb_loaded", "hgrn_prep", "hgrn_act", "v_masked", "sc_zeroed", "k1_turned", "k1_ready", "hgrn_scored",
        "hgrn_masked", "s_loc_ready", "state_ready", "hgrn_out_ready", "hgrn_added"))
    lb_step = new_sem(g, "lb_step")
    lb_act = new_sem(g, "lb_act")
    with ExitStack() as ctx:
        sb = lambda n, shape: ctx.enter_context(nc.sbuf_tensor(f"hgrn_{n}", shape, F32))
        lbw = sb("lb", [P, 4, HEADS])
        k, A, E, D1, Q1, K1 = (sb(n, [P, HEADS * T]) for n in ("k", "A", "E", "D1", "Q1", "K1"))
        reset = sb("reset", [P, HEADS * T])
        dend = sb("dend", [P, HEADS * NCH])
        vmask = sb("vmask", [P, 2, HEADS, TILE_CH * P])
        k1t = sb("k1t", [P, 2, HEADS, P])
        sc = sb("sc", [P, 2, 2, HEADS, P])
        st = sb("state", [P, HEADS, SR, P])

        def per_chunk(x):
            return x.rearrange("p (c t) -> p c t", t=CHUNK)

        with nc.Block() as block:
            @block.sync
            def _(sp):
                sp.dma_start(lbw[:, 0], g.dram["lb_cols"]).then_inc(lb_loaded, 16)

            @block.scalar
            def _(act):
                act.wait_ge(lb_step, 1)
                nc.scalar.activation(lbw[:, 1], lbw[:, 1], ACT.Exp).then_inc(lb_act, 1)

            @block.vector
            def _(dve):
                link = Chain(dve, lb_step)
                dve.wait_ge(lb_loaded, 16)
                link(nc.vector.tensor_tensor(lbw[:, 1], lbw[:, 0], lbw[:, 0], ALU.subtract))
                dve.wait_ge(lb_act, 1)
                link(nc.vector.reciprocal(lbw[:, 2], lbw[:, 1]))
                link(nc.vector.tensor_tensor(lbw[:, 1], lbw[:, 1], lbw[:, 2], ALU.mult))
                link(nc.vector.tensor_tensor(lbw[:, 2], lbw[:, 1], lbw[:, 1], ALU.subtract))
                link(nc.vector.tensor_scalar(lbw[:, 3], lbw[:, 2], -1.0, 1.0, ALU.mult, ALU.add))

            @block.gpsimd
            def _(pool):
                pool.memset(reset[:], 1.0).then_inc(zeroed, 1)
                pool.wait_ge(zeroed, 1)
                pool.memset(per_chunk(reset[:])[:, :, 0:1], 0.0).then_inc(zeroed, 1)
                pool.memset(sc[:], 0.0).then_inc(zeroed, 1)
                pool.wait_ge(zeroed, 3)

        for d in range(2):
            f = s["f"][d]
            Q2 = f.rearrange("p h t -> p (h t)")
            rev = slice(None, None, -1) if d else slice(None)
            last_t, mid_t = (CHUNK - 1, CHUNK // 2 - 1) if d == 0 else (0, CHUNK // 2)
            tiles = [0, 1, 2, 3] if d == 0 else [1, 0, 3, 2]
            chunk_order = list(range(TILE_CH)) if d == 0 else list(range(TILE_CH))[::-1]
            marks = {}
            prep, act_prep = new_sem(g, "hgrn_prep"), new_sem(g, "hgrn_act")
            with nc.Block() as block:
                @block.vector
                def _(dve):
                    link = Chain(dve, prep)
                    for h in range(HEADS):
                        link(nc.vector.tensor_scalar(f[:, h], f[:, h], lbw[:, 3, h:h + 1], lbw[:, 2, h:h + 1], ALU.mult, ALU.add))
                    ff = f.rearrange("p h t -> p (h t)")
                    q = s["q"].rearrange("p h t -> p (h t)")
                    marks["f"] = link.n
                    link(nc.vector.tensor_scalar(k[:], ff, -1.0, 1.0, ALU.mult, ALU.add))
                    link(nc.vector.tensor_scalar(ff, ff, TINY, None, ALU.max))
                    marks["floor"] = link.n
                    dve.wait_ge(act_prep, 1)
                    link(nc.vector.tensor_tensor_scan(A[:, rev], reset[:], E[:, rev], 0.0, ALU.mult, ALU.add))
                    marks["A"] = link.n
                    Ac = per_chunk(A[:])
                    mid = Ac[:, :, mid_t:mid_t + 1].broadcast_to([P, HEADS * NCH, CHUNK])
                    end = Ac[:, :, last_t:last_t + 1].broadcast_to([P, HEADS * NCH, CHUNK])
                    link(nc.vector.tensor_tensor(per_chunk(D1[:]), Ac, mid, ALU.subtract))
                    marks["D1"] = link.n
                    dve.wait_ge(act_prep, 3)
                    link(nc.vector.tensor_tensor(Q1[:], E[:], q, ALU.mult))
                    marks["Q1"] = link.n
                    dve.wait_ge(act_prep, 4)
                    link(nc.vector.tensor_tensor(Q2, E[:], q, ALU.mult))
                    link(nc.vector.tensor_tensor(per_chunk(K1[:]), end, Ac, ALU.subtract))
                    marks["K1"] = link.n
                    dve.wait_ge(act_prep, 6)
                    link(nc.vector.tensor_tensor(K1[:], K1[:], k[:], ALU.mult))
                    link(nc.vector.tensor_tensor(D1[:], D1[:], k[:], ALU.mult))

                @block.scalar
                def _(act):
                    act.wait_ge(prep, marks["floor"])
                    nc.scalar.activation(E[:], f.rearrange("p h t -> p (h t)"), ACT.Ln).then_inc(act_prep, 1)
                    act.wait_ge(prep, marks["A"])
                    ends = per_chunk(A[:])[:, :, last_t]
                    nc.scalar.activation(dend[:], ends, ACT.Exp).then_inc(act_prep, 1)
                    nc.scalar.activation(E[:], A[:], ACT.Exp).then_inc(act_prep, 1)
                    act.wait_ge(prep, marks["Q1"])
                    nc.scalar.activation(E[:], D1[:], ACT.Exp).then_inc(act_prep, 1)
                    act.wait_ge(act_prep, 4)
                    nc.scalar.activation(D1[:], D1[:], ACT.Exp, scale=-1.0).then_inc(act_prep, 1)
                    act.wait_ge(prep, marks["K1"])
                    nc.scalar.activation(K1[:], K1[:], ACT.Exp).then_inc(act_prep, 1)

            (vmasked, turned, k1_ready, scored, masked, located, stated, out_ready, added) = (new_sem(g, x) for x in (
                "v_masked", "k1_turned", "k1_ready", "hgrn_scored", "hgrn_masked", "s_loc_ready", "state_ready",
                "hgrn_out_ready", "hgrn_added"))
            keep = g.tri_chunk[d]
            state_zeroed = new_sem(g, "state_zeroed")
            with nc.Block() as block:
                @block.tensor
                def _(pe):
                    for n, i in enumerate(tiles):
                        if n >= 1:
                            pe.wait_ge(k1_ready, n)
                        for h in range(HEADS):
                            at = h * T + i * P
                            last = nc.tensor.transpose(g.bank[0][:, h * P:(h + 1) * P], K1[:, at:at + P], g.ident)
                        last.then_inc(turned, 1)
                        if n >= 1:
                            pe.wait_ge(masked, n * HEADS)
                        for h in range(HEADS):
                            at = h * T + i * P
                            last = nc.tensor.matmul(g.bank[1][:, h * P:(h + 1) * P], D1[:, at:at + P], Q2[:, at:at + P],
                                                    start=True, stop=True)
                        last.then_inc(scored, 1)
                        pe.wait_ge(k1_ready, n + 1)
                        pe.wait_ge(vmasked, n + 1)
                        if n >= 1:
                            pe.wait_ge(stated, HEADS * TILE_CH * n)
                        for h in range(HEADS):
                            nc.tensor.matmul(g.bank[2 + h][:], k1t[:, n % 2, h], vmask[:, n % 2, h], start=True, stop=True).then_inc(located, 1)
                        if n >= 2:
                            pe.wait_ge(added, n - 1)
                        for h in range(HEADS):
                            pe.wait_ge(masked, n * HEADS + h + 1)
                            out = g.bank[6 + n % 2][:, h * P:(h + 1) * P]
                            first = n == 0
                            nc.tensor.matmul(out, sc[:, d, n % 2, h], s["v"][:, i, h * P:(h + 1) * P], start=True, stop=False, skip_group_check=True)
                            for m, c in enumerate(chunk_order):
                                pe.wait_ge(stated, HEADS * (n * TILE_CH + m)) if n or m else pe.wait_ge(state_zeroed, 1)
                                at = h * T + i * P + c * CHUNK
                                slot = (n * TILE_CH + m) % SR
                                last = nc.tensor.matmul(out[c * CHUNK:(c + 1) * CHUNK, :], Q1[:, at:at + CHUNK], st[:, h, slot],
                                                        start=False, stop=m == TILE_CH - 1, skip_group_check=True)
                        last.then_inc(out_ready, 1)

                @block.scalar
                def _(act):
                    for n, i in enumerate(tiles):
                        act.wait_ge(turned, n + 1)
                        if n >= 2:
                            act.wait_ge(located, HEADS * (n - 1))
                        nc.scalar.activation(k1t[:, n % 2], g.bank[0][:].rearrange("p (h t) -> p h t", h=HEADS), ACT.Copy).then_inc(k1_ready, 1)

                @block.gpsimd
                def _(pool):
                    for n, i in enumerate(tiles):
                        if n >= 2:
                            pool.wait_ge(located, HEADS * (n - 1))
                        for h in range(HEADS):
                            src = s["v"][:, i, h * P:(h + 1) * P].unsqueeze(1).broadcast_to([P, TILE_CH, P])
                            last = pool.tensor_tensor(vmask[:, n % 2, h].rearrange("p (c v) -> p c v", v=P), src,
                                                      g.chunk_of.unsqueeze(2).broadcast_to([P, TILE_CH, P]), ALU.mult)
                        last.then_inc(vmasked, 1)

                @block.vector
                def _(dve):
                    nc.vector.memset(st[:, :, 0], 0.0).then_inc(state_zeroed, 1)
                    dve.wait_ge(state_zeroed, 1)
                    for n, i in enumerate(tiles):
                        if n >= 2:
                            dve.wait_ge(out_ready, n - 1)
                        dve.wait_ge(scored, n + 1)
                        for h in range(HEADS):
                            nc.vector.copy_predicated(sc[:, d, n % 2, h], keep.bitcast(U32), g.bank[1][:, h * P:(h + 1) * P]).then_inc(masked, 1)
                        for m, c in enumerate(chunk_order):
                            gc = n * TILE_CH + m
                            for h in range(HEADS):
                                if m == 0:
                                    dve.wait_ge(located, n * HEADS + h + 1)
                                if gc >= 1:
                                    dve.wait_ge(stated, HEADS * (gc - 1) + h + 1)
                                at = h * NCH + i * TILE_CH + c
                                nc.vector.scalar_tensor_tensor(st[:, h, (gc + 1) % SR], st[:, h, gc % SR], dend[:, at:at + 1],
                                                               g.bank[2 + h][:, c * P:(c + 1) * P], ALU.mult, ALU.add).then_inc(stated, 1)
                        dve.wait_ge(out_ready, n + 1)
                        src = g.bank[6 + n % 2][:]
                        if d == 0:
                            nc.vector.tensor_copy(s["y"][:, i], src).then_inc(added, 1)
                        else:
                            nc.vector.tensor_tensor(s["y"][:, i], s["y"][:, i], src, ALU.add).then_inc(added, 1)


def residual_stage(g, l, which, tiles, source, w_out=None):
    nc = g.nc
    (w_loaded, ln_loaded, produced, freed, step, rooted) = (new_sem(g, x) for x in (
        "w_out_loaded", "ln_loaded", "y_produced", "y_freed", "ln_step", "ln_root"))
    tag = f"{l}{which}"
    with ExitStack() as ctx:
        if w_out is not None:
            w = ctx.enter_context(nc.sbuf_tensor(f"w_out{tag}", [P, KT, D], F32))
        ln = ctx.enter_context(nc.sbuf_tensor(f"ln{tag}", [P, 2, D], F32))
        z = ctx.enter_context(nc.sbuf_tensor(f"ln_z{tag}", [P, 2, D], F32))
        stats = ctx.enter_context(nc.sbuf_tensor(f"ln_stats{tag}", [P, 2, 2, 6], F32))
        mv = ctx.enter_context(nc.sbuf_tensor(f"ln_mv{tag}", [P, 4, 4], F32))
        marks = {}
        with nc.Block() as block:
            @block.sync
            def _(sp):
                if w_out is not None:
                    sp.dma_start(w[:], w_out).then_inc(w_loaded, 16)
                sp.dma_start(ln[:], g.dram["ln_rows"][l, which]).then_inc(ln_loaded, 16)

            if w_out is not None:
                @block.tensor
                def _(pe):
                    pe.wait_ge(w_loaded, 16)
                    for n, i in enumerate(tiles):
                        for half in range(2):
                            u = 2 * n + half
                            for k in range(KT):
                                last = nc.tensor.matmul(g.bank[u % 8][:], g.mix[:, k, i * P:(i + 1) * P], w[:, k, half * 512:(half + 1) * 512],
                                                        start=k == 0, stop=k == KT - 1)
                            last.then_inc(produced, 1)

            @block.vector
            def _(dve):
                link = Chain(dve, step)
                for n, i in enumerate(tiles):
                    v = 1 if i < 2 else 0
                    zz = z[:, n % 2]
                    for half in range(2):
                        cols = slice(half * 512, (half + 1) * 512)
                        if w_out is not None:
                            dve.wait_ge(produced, 2 * n + half + 1)
                            y = g.bank[2 * n + half][:]
                        else:
                            y = source[:, n, cols]
                        link(nc.vector.tensor_tensor(zz[:, cols], y, g.mod_row[:, v, cols], ALU.mult))
                    link(nc.vector.scalar_tensor_tensor(zz, g.h[:, i], ALPHA, zz, ALU.mult, ALU.add))
                    for half in range(2):
                        link(nc.vector.bn_stats(stats[:, n % 2, half], zz[:, half * 512:(half + 1) * 512]))
                    link(nc.vector.bn_aggr(mv[:, n, 0:2], stats[:, n % 2]))
                    link(nc.vector.tensor_scalar(mv[:, n, 2:3], mv[:, n, 1:2], EPS, None, ALU.add))
                    marks[n] = link.n
                    dve.wait_ge(rooted, n + 1)
                    link(nc.vector.reciprocal(mv[:, n, 2:3], mv[:, n, 3:4]))
                    link(nc.vector.tensor_scalar(zz, zz, mv[:, n, 0:1], mv[:, n, 2:3], ALU.subtract, ALU.mult))
                    if n == 0:
                        dve.wait_ge(ln_loaded, 16)
                    link(nc.vector.tensor_tensor(zz, zz, ln[:, 0], ALU.mult))
                    link(nc.vector.tensor_tensor(g.h[:, i], zz, ln[:, 1], ALU.add))

            @block.scalar
            def _(act):
                for n, i in enumerate(tiles):
                    act.wait_ge(step, marks[n])
                    nc.scalar.activation(mv[:, n, 3:4], mv[:, n, 2:3], ACT.Sqrt).then_inc(rooted, 1)


def moe_input_stage(g, l, tiles, v_dram):
    nc = g.nc
    nt = len(tiles)
    streams = [0, 1] if tiles[0] == 0 else [0]
    (row_made, row_copied, stepped, shifted, stored, turned, copied) = (new_sem(g, x) for x in (
        "row_made", "row_copied", "v_step", "v_ready", "v_stored", "v_turned", "v_copied"))
    mods = g.mods[:, l]
    rows = [(which, v, half) for v in streams for which in (4, 3, 5) for half in range(2)]
    with ExitStack() as ctx:
        vrow = ctx.enter_context(nc.sbuf_tensor(f"v_row{l}", [P, 2, 2, D], F32))
        vt = ctx.enter_context(nc.sbuf_tensor(f"v_tok{l}", [P, nt, D], F32))

        def row_tile(which, v):
            return g.mod_row[:, v] if which == 5 else vrow[:, which - 3, v]

        with nc.Block() as block:
            @block.tensor
            def _(pe):
                for n, (which, v, half) in enumerate(rows):
                    if n >= 4:
                        pe.wait_ge(row_copied, n - 3)
                    for j in range(4):
                        col = mods[:, which * KT + 4 * half + j, v:v + 1].broadcast_to([P, P])
                        last = nc.tensor.matmul(g.bank[n % 4][:, j * P:(j + 1) * P], col, g.ident, start=True, stop=True)
                    last.then_inc(row_made, 1)
                for n in range(nt):
                    pe.wait_ge(shifted, n + 1)
                    for half in range(2):
                        u = 2 * n + half
                        if u >= 4:
                            pe.wait_ge(copied, u - 3)
                        for j in range(4):
                            k = 4 * half + j
                            last = nc.tensor.transpose(g.bank[4 + u % 4][:, j * P:(j + 1) * P], vt[:, n, k * P:(k + 1) * P], g.ident)
                        last.then_inc(turned, 1)

            @block.scalar
            def _(act):
                for n, (which, v, half) in enumerate(rows):
                    act.wait_ge(row_made, n + 1)
                    nc.scalar.activation(row_tile(which, v)[:, half * 512:(half + 1) * 512], g.bank[n % 4][:], ACT.Copy).then_inc(row_copied, 1)
                for u in range(2 * nt):
                    n, half = u // 2, u % 2
                    act.wait_ge(turned, u + 1)
                    nc.scalar.activation(g.xt[:, 4 * half:4 * half + 4, tiles[n] * P:(tiles[n] + 1) * P],
                                         g.bank[4 + u % 4][:].rearrange("p (k t) -> p k t", k=4), ACT.Copy).then_inc(copied, 1)

            @block.vector
            def _(dve):
                link = Chain(dve, stepped)
                for n, i in enumerate(tiles):
                    v = 1 if i < 2 else 0
                    dve.wait_ge(row_copied, 6 * streams.index(v) + 4)
                    link(nc.vector.tensor_tensor(vt[:, n], g.h[:, i], vrow[:, 1, v], ALU.mult))
                    nc.vector.tensor_tensor(vt[:, n], vt[:, n], vrow[:, 0, v], ALU.add).then_inc(shifted, 1)

            @block.sync
            def _(sp):
                for n in range(nt):
                    sp.wait_ge(shifted, n + 1)
                    sp.dma_start(v_dram.rearrange("(n p) d -> n p d", p=P)[n], vt[:, n]).then_inc(stored, 16)
                sp.wait_ge(stored, 16 * nt)


def routing_stage(g, l, tiles, r):
    nc = g.nc
    nt = len(tiles)
    NB = r["max_blocks"]
    (loaded, scored, squashed, step, ranked, turned, filled, scattered, idx_loaded, tok_ready) = (new_sem(g, x) for x in (
        "router_loaded", "router_scored", "router_sigmoid", "router_step", "ranks_ready", "table_turned", "slots_filled",
        "slots_scattered", "idx_loaded", "tok_ready"))
    marks = {}
    with ExitStack() as ctx:
        sb = lambda n, shape, dt=F32: ctx.enter_context(nc.sbuf_tensor(f"router_{n}{l}", shape, dt))
        rw, rb = sb("w", [P, KT, EXPERTS]), sb("b", [P, EXPERTS])
        sig, pick, mask, posn, inblk, blk = (sb(n, [P, nt, EXPERTS]) for n in ("sig", "pick", "mask", "posn", "inblk", "blk"))
        top, tot = sb("top", [P, nt, TOPK]), sb("tot", [P, nt, 2])
        chosen = sb("chosen", [P, nt, TOPK], U32)
        chosen_f = sb("chosen_f", [P, nt, TOPK])
        onehot, prod = sb("onehot", [P, nt, TOPK, EXPERTS]), sb("prod", [P, TOPK, EXPERTS])
        picked = sb("picked", [P, 2, nt, TOPK])
        addr = sb("addr", [P, nt, TOPK], U32)
        tok = sb("tok", [P, nt], U32)
        skip = sb("skip", [P, NB], U32)
        nblk, incl, start, cnt = (sb(n, [P, EXPERTS]) for n in ("nblk", "incl", "start", "cnt"))
        owner = sb("owner", [P, EXPERTS])
        ecol = sb("ecol", [P, 2])
        with nc.Block() as block:
            @block.sync
            def _(sp):
                sp.dma_start(rw[:], g.dram["router_w"][l]).then_inc(loaded, 16)
                sp.dma_start(rb[:], g.dram["router_b"][l]).then_inc(loaded, 16)
                sp.wait_ge(tok_ready, 1)
                sp.dma_start(r["slot_dram"].rearrange("(p b) a -> p (b a)", p=P), skip[:]).then_inc(filled, 16)
                sp.wait_ge(scattered, 16 * nt * TOPK)
                sp.dma_start(r["idx_all"][:], r["slot_dram"].rearrange("(p b) a -> p (b a)", p=P)).then_inc(idx_loaded, 16)
                sp.wait_ge(idx_loaded, 16)

            @block.vector
            def _(dve):
                link = Chain(dve, step)
                nc.vector.memset(skip[:], SKIP).then_inc(tok_ready, 1)
                dve.wait_ge(loaded, 32)
                for n in range(nt):
                    link(nc.vector.tensor_scalar(tok[:, n:n + 1], g.pcol, float(n * P), None, ALU.add))
                for n in range(nt):
                    dve.wait_ge(squashed, n + 1)
                    link(nc.vector.tensor_tensor(pick[:, n], sig[:, n], rb[:], ALU.add))
                    link(nc.vector.max(top[:, n], pick[:, n]))
                    link(nc.vector.max_index(chosen[:, n], top[:, n], pick[:, n]))
                    link(nc.vector.match_replace(mask[:, n], top[:, n], pick[:, n], NEG_BIG))
                    link(nc.vector.tensor_tensor(mask[:, n], mask[:, n], pick[:, n], ALU.not_equal))
                marks["mask"] = link.n
                for n in range(nt):
                    link(nc.vector.tensor_copy(chosen_f[:, n], chosen[:, n]))
                    link(nc.vector.tensor_tensor(onehot[:, n], g.iota_e.unsqueeze(1).broadcast_to([P, TOPK, EXPERTS]),
                                                 chosen_f[:, n].unsqueeze(2).broadcast_to([P, TOPK, EXPERTS]), ALU.is_equal))
                    link(nc.vector.tensor_tensor(prod[:], onehot[:, n], sig[:, n].unsqueeze(1).broadcast_to([P, TOPK, EXPERTS]), ALU.mult))
                    link(nc.vector.tensor_reduce(r["gate"][:, n], prod[:], AX.X, ALU.add))
                    link(nc.vector.tensor_reduce(tot[:, n, 0:1], r["gate"][:, n], AX.X, ALU.add))
                    link(nc.vector.reciprocal(tot[:, n, 1:2], tot[:, n, 0:1]))
                    link(nc.vector.tensor_scalar(r["gate"][:, n], r["gate"][:, n], tot[:, n, 1:2], ROUTED_SCALE, ALU.mult, ALU.mult))
                dve.wait_ge(ranked, 1)
                link(nc.vector.tensor_copy(cnt[:], g.bank[7][:, 0:EXPERTS]))
                link(nc.vector.tensor_scalar(nblk[:], cnt[:], 0.5, None, ALU.is_gt))
                for j in range(1, nt):
                    link(nc.vector.scalar_tensor_tensor(nblk[:], cnt[:], j * P + 0.5, nblk[:], ALU.is_gt, ALU.add))
                link(nc.vector.tensor_tensor_scan(incl[:], g.ones[:, 0:EXPERTS], nblk[:], 0.0, ALU.mult, ALU.add))
                link(nc.vector.tensor_tensor(start[:], incl[:], nblk[:], ALU.subtract))
                link(nc.vector.tensor_scalar(owner[:], incl[:], g.pcol, None, ALU.is_le))
                link(nc.vector.tensor_reduce(ecol[:, 0:1], owner[:], AX.X, ALU.add))
                link(nc.vector.tensor_scalar(ecol[:, 0:1], ecol[:, 0:1], EXPERTS - 1.0, None, ALU.min))
                link(nc.vector.tensor_scalar(owner[:], g.iota_e, 2.0, None, ALU.mult))
                link(nc.vector.tensor_scalar(owner[:], owner[:], incl[:, EXPERTS - 1:EXPERTS], None, ALU.is_lt))
                link(nc.vector.tensor_reduce(ecol[:, 1:2], owner[:], AX.X, ALU.add))
                link(nc.vector.tensor_scalar(ecol[:, 1:2], ecol[:, 1:2], -float(MIN_PAIRS), None, ALU.add))
                marks["ecol"] = link.n
                for n in range(nt):
                    pos = posn[:, n]
                    link(nc.vector.tensor_scalar(pos, g.bank[3 + n][:, 0:EXPERTS], -1.0, None, ALU.add))
                    link(nc.vector.tensor_copy(blk[:, n], start[:]))
                    link(nc.vector.tensor_copy(inblk[:, n], pos))
                    for j in range(1, nt):
                        link(nc.vector.tensor_scalar(mask[:, n], pos, j * P - 0.5, None, ALU.is_gt))
                        link(nc.vector.tensor_tensor(blk[:, n], blk[:, n], mask[:, n], ALU.add))
                        link(nc.vector.scalar_tensor_tensor(inblk[:, n], mask[:, n], -float(P), inblk[:, n], ALU.mult, ALU.add))
                    link(nc.vector.scalar_tensor_tensor(pos, blk[:, n], float(P), inblk[:, n], ALU.mult, ALU.add))
                    link(nc.vector.scalar_tensor_tensor(inblk[:, n], inblk[:, n], float(NB), blk[:, n], ALU.mult, ALU.add))
                    for c, src in enumerate((pos, inblk[:, n])):
                        link(nc.vector.tensor_tensor(prod[:], onehot[:, n], src.unsqueeze(1).broadcast_to([P, TOPK, EXPERTS]), ALU.mult))
                        link(nc.vector.tensor_reduce(picked[:, c, n], prod[:], AX.X, ALU.add))
                    link(nc.vector.tensor_copy(r["y_row"][:, n], picked[:, 0, n]))
                    link(nc.vector.tensor_copy(addr[:, n], picked[:, 1, n]))
                    marks["addr", n] = link.n
                dve.wait_ge(turned, 1)
                link(nc.vector.tensor_copy(r["table"][0:1, 0:P], g.bank[0][0:1, 0:P]))
                link(nc.vector.tensor_copy(r["table"][0:1, P:P + 1], ecol[0:1, 1:2]))

            @block.tensor
            def _(pe):
                pe.wait_ge(loaded, 32)
                for n, i in enumerate(tiles):
                    for k in range(KT):
                        last = nc.tensor.matmul(g.bank[n % 3][:, 0:EXPERTS] if n < 3 else g.bank[7][:, 0:EXPERTS],
                                                g.xt[:, k, i * P:(i + 1) * P], rw[:, k], start=k == 0, stop=k == KT - 1)
                    last.then_inc(scored, 1)
                pe.wait_ge(step, marks["mask"])
                for n in range(nt):
                    for m in range(n + 1):
                        nc.tensor.matmul(g.bank[3 + n][:, 0:EXPERTS], g.upper if m == n else g.ones, mask[:, m],
                                         start=m == 0, stop=m == n)
                for m in range(nt):
                    last = nc.tensor.matmul(g.bank[7][:, 0:EXPERTS], g.ones, mask[:, m], start=m == 0, stop=m == nt - 1)
                last.then_inc(ranked, 1)
                pe.wait_ge(step, marks["ecol"])
                nc.tensor.transpose(g.bank[0][0:1, 0:P], ecol[:, 0:1], g.ident).then_inc(turned, 1)

            @block.scalar
            def _(act):
                for n in range(nt):
                    act.wait_ge(scored, n + 1)
                    nc.scalar.activation(sig[:, n], (g.bank[n % 3] if n < 3 else g.bank[7])[:, 0:EXPERTS], ACT.Sigmoid).then_inc(squashed, 1)

            @block.gpsimd
            def _(pool):
                pool.wait_ge(filled, 16)
                for n in range(nt):
                    pool.wait_ge(step, marks["addr", n])
                    for k in range(TOPK):
                        pool.indirect_dma_start(r["slot_dram"], bass.IndirectOffsetOnAxis(ap=addr[:, n, k:k + 1], axis=0),
                                                tok[:, n:n + 1], None).then_inc(scattered, 16)


def shared_stage(g, l, tiles, acc):
    nc = g.nc
    nt = len(tiles)
    a0, n_tok = tiles[0] * P, nt * P
    loaded, up_ready, silu_ready, hidden_ready, y_ready, copied = (new_sem(g, x) for x in (
        "shared_loaded", "sh_up_ready", "sh_silu_ready", "sh_hidden_ready", "sh_y_ready", "sh_copied"))
    with ExitStack() as ctx:
        w = ctx.enter_context(nc.sbuf_tensor(f"sh_w{l}", [P, WEXP], F32))
        silu = ctx.enter_context(nc.sbuf_tensor(f"sh_silu{l}", [P, 2, n_tok], F32))
        hidden = ctx.enter_context(nc.sbuf_tensor(f"sh_hidden{l}", [P, 2, n_tok], F32))
        up = w[:, 0:W13].rearrange("p (k a c) -> p k a c", k=KT, a=2)
        down = w[:, W13:WEXP].rearrange("p (m c) -> p m c", m=2)
        with nc.Block() as block:
            @block.sync
            def _(sp):
                sp.dma_start(w[:], g.dram["experts"][l * (EXPERTS + 1)]).then_inc(loaded, 16)

            @block.tensor
            def _(pe):
                pe.wait_ge(loaded, 16)
                for m in range(2):
                    for a in range(2):
                        for k in range(KT):
                            last = nc.tensor.matmul(g.bank[2 * m + a][:, 0:n_tok], up[:, k, a, m * P:(m + 1) * P],
                                                    g.xt[:, k, a0:a0 + n_tok], start=k == 0, stop=k == KT - 1)
                    last.then_inc(up_ready, 1)
                pe.wait_ge(hidden_ready, 2)
                for u in range(2 * nt):
                    if u >= 4:
                        pe.wait_ge(copied, u - 3)
                    for m in range(2):
                        last = nc.tensor.matmul(g.bank[4 + u % 4][:], hidden[:, m, (u // 2) * P:(u // 2 + 1) * P],
                                                down[:, m, (u % 2) * 512:(u % 2 + 1) * 512], start=m == 0, stop=m == 1)
                    last.then_inc(y_ready, 1)

            @block.scalar
            def _(act):
                for m in range(2):
                    act.wait_ge(up_ready, m + 1)
                    nc.scalar.activation(silu[:, m], g.bank[2 * m][:, 0:n_tok], ACT.Silu).then_inc(silu_ready, 1)

            @block.vector
            def _(dve):
                for m in range(2):
                    dve.wait_ge(silu_ready, m + 1)
                    nc.vector.tensor_tensor(hidden[:, m], silu[:, m], g.bank[2 * m + 1][:, 0:n_tok], ALU.mult).then_inc(hidden_ready, 1)
                for u in range(2 * nt):
                    dve.wait_ge(y_ready, u + 1)
                    nc.vector.tensor_copy(acc[:, u // 2, (u % 2) * 512:(u % 2 + 1) * 512], g.bank[4 + u % 4][:]).then_inc(copied, 1)


def blocks_stage(g, l, n_tok, r, v_dram, y_dram):
    nc = g.nc
    (idx_ready, turned, xt_ready, up_done, silu_done, hidden_done, hid_turned, hid_ready, y_done, y_ready) = (new_sem(g, x) for x in (
        "idx_ready", "x_turned", "xt_ready", "up_done", "silu_done", "hidden_done", "hid_turned", "hid_ready", "y_done", "y_ready"))
    up_loaded, down_loaded, gathered, stored = ([new_sem(g, f"{x}{q}") for q in range(2)] for x in (
        "up_loaded", "down_loaded", "gathered", "stored"))
    x_zeroed, gathers_sent, all_stored = (new_sem(g, x) for x in ("x_zeroed", "gathers_sent", "all_stored"))
    wd, base = g.dram["experts"], l * (EXPERTS + 1) + 1
    with ExitStack() as ctx:
        sb = lambda n, shape, dt=F32: ctx.enter_context(nc.sbuf_tensor(f"blk_{n}{l}", shape, dt))
        up, down = sb("up", [P, 2, KT, 2 * HID]), sb("down", [P, 2, 2, D])
        x, xT = sb("x", [P, 2, D]), sb("xT", [P, 2, KT, P])
        silu, hidden, hT = sb("silu", [P, 2, HID]), sb("hidden", [P, 2, HID]), sb("hT", [P, 2, 2, P])
        y = sb("y", [P, 2, D])
        idx = [sb(f"idx{q}", [P, 1], U32) for q in range(2)]

        def extra_pairs(eng):
            return eng.value_load(r["table"][0:1, P:P + 1], min_val=0, max_val=r["max_blocks"] // 2 - MIN_PAIRS)

        def over_pairs(eng, first, step, last):
            extra = extra_pairs(eng)
            first()
            with eng.Fori(1, extra + (MIN_PAIRS - 1)) as p:
                step(p)
            last(extra + (MIN_PAIRS - 1))

        with nc.Block() as block:
            @block.sync
            def _(sp):
                def load_up(b, q):
                    e = sp.value_load(r["table"][0:1, bass.ds(b, 1)], min_val=0, max_val=EXPERTS - 1)
                    sp.dma_start(up[:, q], wd[base + e, :, 0:W13].rearrange("p (k c) -> p k c", k=KT)).then_inc(up_loaded[q], 16)
                    return e

                def load_down(e, q):
                    sp.dma_start(down[:, q], wd[base + e, :, W13:WEXP].rearrange("p (m c) -> p m c", m=2)).then_inc(down_loaded[q], 16)

                def store(b, q):
                    sp.wait_ge(y_ready, 2 * b + 2)
                    sp.dma_start(y_dram[b], y[:, q]).then_inc(stored[q], 16)

                def turn(p, q, more, before):
                    b = 2 * p + q
                    e = None
                    if more:
                        sp.wait_ge(up_done, b + 1)
                        e = load_up(b + 2, q)
                    if before:
                        store(b - 1, 1 - q)
                    if more:
                        sp.wait_ge(y_done, b + 1)
                        load_down(e, q)

                for q in range(2):
                    load_down(load_up(q, q), q)
                sp.wait_ge(g.y_cleared, 16 * (MAX_BLOCKS - MIN_BLOCKS) // CLEAR)

                def first():
                    turn(0, 0, True, False)
                    turn(0, 1, True, True)

                def step(p):
                    turn(p, 0, True, True)
                    turn(p, 1, True, True)

                def last(p):
                    turn(p, 0, False, True)
                    turn(p, 1, False, True)
                    store(2 * p + 1, 1)
                    for q in range(2):
                        sp.wait_ge(stored[q], 16 * (p + 1))
                    sp.sem_inc(all_stored, 1)

                over_pairs(sp, first, step, last)

            @block.gpsimd
            def _(pool):
                def gather(p, q, first):
                    b = 2 * p + q
                    if not first:
                        pool.wait_ge(gathered[q], 16 * p)
                        pool.wait_ge(turned, b - 1)
                    pool.tensor_copy(idx[q][:], r["idx_all"][:, bass.ds(b, 1)]).then_inc(idx_ready, 1)
                    pool.wait_ge(idx_ready, b + 1)
                    pool.sem_inc(gathers_sent, 1)
                    pool.indirect_dma_start(x[:, q], None, v_dram, bass.IndirectOffsetOnAxis(ap=idx[q][:], axis=0),
                                            bounds_check=n_tok - 1, oob_is_err=False).then_inc(gathered[q], 16)

                pool.memset(x[:], 0.0).then_inc(x_zeroed, 1)
                pool.wait_ge(x_zeroed, 1)

                def step(p):
                    gather(p, 0, False)
                    gather(p, 1, False)

                over_pairs(pool, lambda: (gather(0, 0, True), gather(0, 1, True)), step, step)

            @block.tensor
            def _(pe):
                def turn_x(p, q):
                    b = 2 * p + q
                    pe.wait_ge(gathered[q], 16 * (p + 1))
                    if not (isinstance(b, int) and b == 0):
                        pe.wait_ge(xt_ready, 2 * b)
                    for k in range(KT):
                        last = nc.tensor.transpose(g.bank[k // 4][:, (k % 4) * P:(k % 4 + 1) * P], x[:, q, k * P:(k + 1) * P], g.ident)
                    last.then_inc(turned, 1)

                def turn_hidden(b, q, early):
                    pe.wait_ge(hidden_done, b + 1)
                    if not early:
                        pe.wait_ge(hid_ready, b)
                    for m in range(2):
                        last = nc.tensor.transpose(g.bank[4][:, m * P:(m + 1) * P], hidden[:, q, m * P:(m + 1) * P], g.ident)
                    last.then_inc(hid_turned, 1)

                def down_project(p, q, early):
                    b = 2 * p + q
                    pe.wait_ge(hid_ready, b + 1)
                    pe.wait_ge(down_loaded[q], 16 * (p + 1))
                    if not early:
                        pe.wait_ge(y_ready, 2 * b)
                    for half in range(2):
                        for m in range(2):
                            last = nc.tensor.matmul(g.bank[5 + half][:], hT[:, q, m], down[:, q, m, half * 512:(half + 1) * 512],
                                                    start=m == 0, stop=m == 1)
                    last.then_inc(y_done, 1)

                def turn(p, q, before, after, early):
                    b = 2 * p + q
                    if after:
                        turn_x(p if q == 0 else p + 1, 1 - q)
                    pe.wait_ge(xt_ready, 2 * b + 2)
                    pe.wait_ge(up_loaded[q], 16 * (p + 1))
                    if not (isinstance(b, int) and b < 2):
                        pe.wait_ge(hidden_done, b - 1)
                    for k in range(KT):
                        if k == KT // 2 and before:
                            turn_hidden(b - 1, 1 - q, early)
                        last = nc.tensor.matmul(g.bank[2 + q][:], xT[:, q, k], up[:, q, k], start=k == 0, stop=k == KT - 1)
                    last.then_inc(up_done, 1)
                    if before:
                        down_project(p if q == 1 else p - 1, 1 - q, early)

                turn_x(0, 0)

                def first():
                    turn(0, 0, False, True, True)
                    turn(0, 1, True, True, True)

                def step(p):
                    turn(p, 0, True, True, False)
                    turn(p, 1, True, True, False)

                def last(p):
                    turn(p, 0, True, True, False)
                    turn(p, 1, True, False, False)
                    turn_hidden(2 * p + 1, 1, False)
                    down_project(p, 1, False)

                over_pairs(pe, first, step, last)

            @block.scalar
            def _(act):
                def copy_x(b, q, early):
                    act.wait_ge(turned, b + 1)
                    if not early:
                        act.wait_ge(up_done, b - 1)
                    for half in range(2):
                        nc.scalar.activation(xT[:, q, 4 * half:4 * half + 4], g.bank[half][:].rearrange("p (k t) -> p k t", k=4),
                                             ACT.Copy).then_inc(xt_ready, 1)

                def copy_hidden(b, q, early):
                    act.wait_ge(hid_turned, b + 1)
                    if not early:
                        act.wait_ge(y_done, b - 1)
                    nc.scalar.activation(hT[:, q], g.bank[4][:, 0:2 * P].rearrange("p (m t) -> p m t", m=2), ACT.Copy).then_inc(hid_ready, 1)

                def turn(p, q, before, after, early):
                    b = 2 * p + q
                    if after:
                        copy_x(b + 1, 1 - q, isinstance(b, int) and b == 0)
                    if before:
                        copy_hidden(b - 1, 1 - q, isinstance(b, int) and b < 3)
                    act.wait_ge(up_done, b + 1)
                    if not early:
                        act.wait_ge(hidden_done, b - 1)
                    nc.scalar.activation(silu[:, q], g.bank[2 + q][:, 0:HID], ACT.Silu).then_inc(silu_done, 1)

                copy_x(0, 0, True)

                def first():
                    turn(0, 0, False, True, True)
                    turn(0, 1, True, True, True)

                def step(p):
                    turn(p, 0, True, True, False)
                    turn(p, 1, True, True, False)

                def last(p):
                    turn(p, 0, True, True, False)
                    turn(p, 1, True, False, False)
                    copy_hidden(2 * p + 1, 1, False)

                over_pairs(act, first, step, last)

            @block.vector
            def _(dve):
                def gate(b, q, early):
                    dve.wait_ge(silu_done, b + 1)
                    if not early:
                        dve.wait_ge(hid_turned, b - 1)
                    nc.vector.tensor_tensor(hidden[:, q], silu[:, q], g.bank[2 + q][:, HID:2 * HID], ALU.mult).then_inc(hidden_done, 1)

                def copy_y(p, q, early):
                    b = 2 * p + q
                    dve.wait_ge(y_done, b + 1)
                    if not early:
                        dve.wait_ge(stored[q], 16 * p)
                    for half in range(2):
                        nc.vector.tensor_copy(y[:, q, half * 512:(half + 1) * 512], g.bank[5 + half][:]).then_inc(y_ready, 1)

                def first():
                    gate(0, 0, True)
                    gate(1, 1, True)
                    copy_y(0, 0, True)

                def pair(p, early):
                    gate(2 * p, 0, False)
                    copy_y(p - 1, 1, early)
                    gate(2 * p + 1, 1, False)
                    copy_y(p, 0, False)

                extra = extra_pairs(dve)
                first()
                pair(1, True)
                with dve.Fori(2, extra + MIN_PAIRS) as p:
                    pair(p, False)
                copy_y(extra + (MIN_PAIRS - 1), 1, False)


def combine_stage(g, l, tiles, r, y_dram, acc):
    nc = g.nc
    nt = len(tiles)
    SLOTS = 6
    fetched = [new_sem(g, f"y_fetched{s}") for s in range(SLOTS)]
    added = new_sem(g, "y_added")
    rows = y_dram.rearrange("b p d -> (b p) d")
    with ExitStack() as ctx:
        ring = ctx.enter_context(nc.sbuf_tensor(f"comb_ring{l}", [P, SLOTS, D], F32))
        order = [(n, k) for k in range(TOPK) for n in range(nt)]
        with nc.Block() as block:
            @block.gpsimd
            def _(pool):
                for u, (n, k) in enumerate(order):
                    if u >= SLOTS:
                        pool.wait_ge(added, u - SLOTS + 1)
                    pool.indirect_dma_start(ring[:, u % SLOTS], None, rows,
                                            bass.IndirectOffsetOnAxis(ap=r["y_row"][:, n, k:k + 1], axis=0)).then_inc(fetched[u % SLOTS], 16)

            @block.vector
            def _(dve):
                for u, (n, k) in enumerate(order):
                    dve.wait_ge(fetched[u % SLOTS], 16 * (u // SLOTS + 1))
                    if u >= nt:
                        dve.wait_ge(added, u - nt + 1)
                    nc.vector.scalar_tensor_tensor(acc[:, n], ring[:, u % SLOTS], r["gate"][:, n, k:k + 1], acc[:, n],
                                                   ALU.mult, ALU.add).then_inc(added, 1)


def moe(g, l, tiles):
    nc = g.nc
    nt = len(tiles)
    n_tok = nt * P
    max_blocks = (EXPERTS + (n_tok * TOPK - EXPERTS) // P + 1) // 2 * 2
    v_dram = nc.dram_tensor(f"v_tokens{l}", (n_tok, D), F32, kind="Internal").ap()
    slot_dram = nc.dram_tensor(f"slot_tokens{l}", (P * max_blocks, 1), U32, kind="Internal").ap()
    y_dram = g.y_dram[0:max_blocks]
    moe_input_stage(g, l, tiles, v_dram)
    with ExitStack() as ctx:
        sb = lambda n, shape, dt=F32: ctx.enter_context(nc.sbuf_tensor(f"moe_{n}{l}", shape, dt))
        acc = sb("acc", [P, nt, D])
        r = {"max_blocks": max_blocks, "slot_dram": slot_dram, "gate": sb("gate", [P, nt, TOPK]),
             "y_row": sb("y_row", [P, nt, TOPK], U32), "idx_all": sb("idx_all", [P, max_blocks], U32),
             "table": sb("table", [1, P + 1], mybir.dt.int32)}
        routing_stage(g, l, tiles, r)
        shared_stage(g, l, tiles, acc[:])
        blocks_stage(g, l, n_tok, r, v_dram, y_dram)
        combine_stage(g, l, tiles, r, y_dram, acc[:])
        residual_stage(g, l, 1, tiles, acc[:])


def even_layer(g):
    nc = g.nc
    modulate_stage(g, 0, 0, 1, list(range(NT)), 2)
    with ExitStack() as ctx:
        g.mix = ctx.enter_context(nc.sbuf_tensor("mix0", [P, KT, T], F32))
        with ExitStack() as c2:
            sb = lambda n, shape: c2.enter_context(nc.sbuf_tensor(n, shape, F32))
            qT, kT = sb("m_qT", [P, 2, T]), sb("m_kT", [P, 2, T])
            v1, o, y = sb("m_v1", [P, NT, HEADS, P + 1]), sb("m_o", [P, NT, 512]), sb("m_y", [P, NT, 512])
            s = {"qT": qT, "kT": kT, "v1": v1, "y": y, "a_col": sb("a_col", [P, 2, NT * HEADS]),
                 "floor_col": sb("floor_col", [P, 2, NT * HEADS]), "max_row": sb("max_row", [HEADS, 2, T])}
            ones = new_sem(g, "v_ones")
            with nc.Block() as block:
                @block.gpsimd
                def _(pool):
                    pool.memset(v1[:, :, :, P:P + 1], 1.0).then_inc(ones, 1)
                    pool.wait_ge(ones, 1)
            allt = list(range(NT))
            projection_stage(g, g.dram["even_w_in"], [
                (0, "T", allt, lambda j: (qT if j < 2 else kT)[:, j % 2], "q_scale"),
                (1, "N", allt, lambda j: v1[:, j, :, 0:P], "heads"),
                (2, "N", allt, lambda j: o[:, j], "sigmoid")])
            gates_wrapped(g, s)
            mlstm_stage(g, s)
            norm_stage(g, y[:], allt, HEADS, True, o[:], "mlstm_norm_w", 0, "m")
        with ExitStack() as c2:
            sb = lambda n, shape: c2.enter_context(nc.sbuf_tensor(n, shape, F32))
            q, v, hg, ff, fb, y = (sb(n, [P, HEADS, T]) for n in ("h_q", "h_v", "h_g", "h_ff", "h_fb", "h_y"))
            projection_stage(g, g.dram["even_w_in"], [
                (3, "T", allt, lambda j: q[:, j], "silu"),
                (4, "N", allt, lambda j: v[:, j], "copy"),
                (5, "T", allt, lambda j: ff[:, j], "sigmoid"),
                (6, "T", allt, lambda j: fb[:, j], "sigmoid"),
                (7, "N", allt, lambda j: hg[:, j], "silu")])
            hgrn_stage(g, {"q": q[:], "v": v, "f": (ff[:], fb[:]), "y": y})
            norm_stage(g, y[:], allt, HEADS, False, hg[:], "hgrn_norm_w", 4, "h")
        residual_stage(g, 0, 0, allt, None, g.dram["even_w_out"])


def gates_wrapped(g, s):
    s["n_abs"] = 1 + 4 + 1
    s["n_rows"] = s["n_abs"] + 1 + 3 + 1 + 3 + 1
    gates_stage(g, s)


def hyena_filter_stage(g, filt):
    nc = g.nc
    loaded, mm, step, act_s, hsem = (new_sem(g, x) for x in ("hyf_loaded", "hyf_mm", "hyf_step", "hyf_sin", "hyf_h"))
    TWO_PI = 2.0 * math.pi
    HI = float(np.float32(TWO_PI))
    LO = float(TWO_PI - np.float64(np.float32(TWO_PI)))
    MAGIC = 1.5 * 2.0 ** 23
    PI_F = float(np.float32(3.1415925))
    with ExitStack() as ctx:
        sb = lambda n, shape: ctx.enter_context(nc.sbuf_tensor(f"hyf_{n}", shape, F32))
        z = sb("z", [HYEMB, LAT])
        w1, w23 = sb("w1", [HYEMB, HYHID]), sb("w23", [HYHID, 2, HYHID])
        cols = sb("cols", [HYHID, 4])
        wout = sb("wout", [HYHID, 4, HYW])
        dec = sb("dec", [P, 2, 2, HYW])
        hid, x, r = sb("hid", [HYHID, LAT]), sb("x", [HYHID, LAT]), sb("r", [HYHID, LAT])
        loads = [(z[:], g.dram["t_z"]), (w1[:], g.dram["hy_w1"]), (w23[:], g.dram["hy_w23"]), (cols[:], g.dram["hy_cols"]),
                 (wout[:], g.dram["hy_wout"]), (dec[:], g.dram["t_decay"].rearrange("p (a b c) -> p a b c", a=2, b=2))]
        PER = 7
        with nc.Block() as block:
            @block.sync
            def _(sp):
                for dst, src in loads:
                    sp.dma_start(dst, src).then_inc(loaded, 16)

            @block.tensor
            def _(pe):
                pe.wait_ge(loaded, 16 * len(loads))
                for n in range(3):
                    if n:
                        pe.wait_ge(act_s, n)
                    nc.tensor.matmul(g.bank[n][0:HYHID, 0:LAT], w1[:] if n == 0 else w23[:, n - 1], z[:] if n == 0 else hid[:],
                                     start=True, stop=True).then_inc(mm, 1)
                pe.wait_ge(act_s, 3)
                for u in range(8):
                    q, i = u // 2, u % 2
                    if u >= 5:
                        pe.wait_ge(hsem, u - 4)
                    nc.tensor.matmul(g.bank[3 + u % 5][:], hid[:, i * P:(i + 1) * P], wout[:, q], start=True, stop=True).then_inc(mm, 1)

            @block.scalar
            def _(act):
                for n in range(3):
                    act.wait_ge(step, PER * (n + 1))
                    nc.scalar.activation(hid[:], x[:], ACT.Sin).then_inc(act_s, 1)

            @block.vector
            def _(dve):
                link = Chain(dve, step)
                dve.wait_ge(loaded, 16 * len(loads))
                for n in range(3):
                    dve.wait_ge(mm, n + 1)
                    link(nc.vector.tensor_scalar(x[:], g.bank[n][0:HYHID, 0:LAT], cols[:, n:n + 1], cols[:, 3:4], ALU.add, ALU.mult))
                    link(nc.vector.tensor_scalar(r[:], x[:], 1.0 / TWO_PI, MAGIC, ALU.mult, ALU.add))
                    link(nc.vector.tensor_scalar(r[:], r[:], -MAGIC, None, ALU.add))
                    link(nc.vector.scalar_tensor_tensor(x[:], r[:], -HI, x[:], ALU.mult, ALU.add))
                    link(nc.vector.scalar_tensor_tensor(x[:], r[:], -LO, x[:], ALU.mult, ALU.add))
                    link(nc.vector.tensor_scalar(x[:], x[:], PI_F, None, ALU.min))
                    link(nc.vector.tensor_scalar(x[:], x[:], -PI_F, None, ALU.max))
                for u in range(8):
                    q, i = u // 2, u % 2
                    dve.wait_ge(mm, 3 + u + 1)
                    nc.vector.tensor_tensor(filt[:, q // 2, q % 2, i], g.bank[3 + u % 5][:], dec[:, q % 2, i], ALU.mult).then_inc(hsem, 1)
                dve.wait_ge(hsem, 8)
                for order in range(2):
                    fwd, bwd = filt[:, order, 0], filt[:, order, 1]
                    link(nc.vector.tensor_tensor(fwd, fwd, bwd, ALU.add))
                    link(nc.vector.scalar_tensor_tensor(bwd, bwd, -2.0, fwd, ALU.mult, ALU.add))


def hyena_stage(g, u, filt):
    nc = g.nc
    loaded, shifted, zeroed, step = (new_sem(g, x) for x in ("hy_loaded", "hy_shifted", "hy_zeroed", "hy_step"))
    with ExitStack() as ctx:
        sb = lambda n, shape: ctx.enter_context(nc.sbuf_tensor(f"hy_{n}", shape, F32))
        HW = 3 * HYW
        with ExitStack() as c2:
            prev = c2.enter_context(nc.sbuf_tensor("hy_prev", [P, 2, HW], F32))
            nxt = c2.enter_context(nc.sbuf_tensor("hy_next", [P, 2, HW], F32))
            cw = c2.enter_context(nc.sbuf_tensor("hy_cw", [P, 4, HW], F32))
            uf = u.rearrange("p i s c -> p i (s c)")
            with nc.Block() as block:
                @block.gpsimd
                def _(pool):
                    pool.memset(prev[:, 0], 0.0).then_inc(zeroed, 1)
                    pool.memset(nxt[:, 1], 0.0).then_inc(zeroed, 1)

                @block.sync
                def _(sp):
                    sp.dma_start(cw[:], g.dram["hy_conv"]).then_inc(loaded, 16)
                    sp.wait_ge(zeroed, 2)
                    sp.dma_start(prev[1:P, 0], uf[0:P - 1, 0]).then_inc(shifted, 16)
                    sp.dma_start(prev[0:1, 1], uf[P - 1:P, 0]).then_inc(shifted, 16)
                    sp.dma_start(prev[1:P, 1], uf[0:P - 1, 1]).then_inc(shifted, 16)
                    sp.dma_start(nxt[0:P - 1, 0], uf[1:P, 0]).then_inc(shifted, 16)
                    sp.dma_start(nxt[P - 1:P, 0], uf[0:1, 1]).then_inc(shifted, 16)
                    sp.dma_start(nxt[0:P - 1, 1], uf[1:P, 1]).then_inc(shifted, 16)

                @block.vector
                def _(dve):
                    link = Chain(dve, step)
                    dve.wait_ge(loaded, 16)
                    dve.wait_ge(shifted, 96)
                    for i in range(2):
                        link(nc.vector.tensor_tensor(uf[:, i], uf[:, i], cw[:, 1], ALU.mult))
                        link(nc.vector.tensor_tensor(prev[:, i], prev[:, i], cw[:, 0], ALU.mult))
                        link(nc.vector.tensor_tensor(nxt[:, i], nxt[:, i], cw[:, 2], ALU.mult))
                        link(nc.vector.tensor_tensor(uf[:, i], uf[:, i], prev[:, i], ALU.add))
                        link(nc.vector.tensor_tensor(uf[:, i], uf[:, i], nxt[:, i], ALU.add))
                        link(nc.vector.tensor_tensor(uf[:, i], uf[:, i], cw[:, 3], ALU.add))

        dft = sb("dft", [P, 2, 2, 2, LAT])
        skip = sb("skip", [P, 2, HYW])
        ker = sb("ker", [P, 2, 2, HYW])
        spec = sb("spec", [P, 2, 2, HYW])
        tmp = sb("tmp", [P, 2, HYW])
        t_loaded, uspec, kspec, kcopied, pointed, inv, step2 = (new_sem(g, x) for x in (
            "dft_loaded", "u_spectrum", "k_spectrum", "k_copied", "spec_ready", "conv_ready", "hy_step2"))
        STEPS = 2 * 6 + 2 * 3
        z = u[:, :, 2]
        with nc.Block() as block:
            @block.sync
            def _(sp):
                sp.dma_start(dft[:], g.dram["t_dft"].rearrange("p (d c i f) -> p d c i f", d=2, c=2, i=2)).then_inc(t_loaded, 16)
                sp.dma_start(skip[:], g.dram["hy_skip"]).then_inc(t_loaded, 16)

            @block.tensor
            def _(pe):
                pe.wait_ge(t_loaded, 32)
                for order in range(2):
                    if order:
                        pe.wait_ge(step2, STEPS * order)
                    for c in range(2):
                        for f in range(2):
                            for i in range(2):
                                last = nc.tensor.matmul(g.bank[2 * c + f][:], dft[:, 0, c, i, f * P:(f + 1) * P], filt[:, order, c, i],
                                                        start=i == 0, stop=i == 1)
                    last.then_inc(kspec, 1)
                    for c in range(2):
                        for f in range(2):
                            for i in range(2):
                                last = nc.tensor.matmul(g.bank[4 + 2 * c + f][:], dft[:, 0, c, i, f * P:(f + 1) * P], z[:, i],
                                                        start=i == 0, stop=i == 1)
                    last.then_inc(uspec, 1)
                    pe.wait_ge(pointed, order + 1)
                    for i in range(2):
                        n = 0
                        for c in range(2):
                            for f in range(2):
                                last = nc.tensor.matmul(g.bank[i][:], dft[:, 1, c, f, i * P:(i + 1) * P], spec[:, c, f], start=n == 0, stop=n == 3)
                                n += 1
                    last.then_inc(inv, 1)

            @block.scalar
            def _(act):
                for order in range(2):
                    act.wait_ge(kspec, order + 1)
                    if order:
                        act.wait_ge(pointed, order)
                    for c in range(2):
                        for f in range(2):
                            nc.scalar.activation(ker[:, c, f], g.bank[2 * c + f][:], ACT.Copy).then_inc(kcopied, 1)

            @block.vector
            def _(dve):
                link = Chain(dve, step2)
                for order in range(2):
                    dve.wait_ge(uspec, order + 1)
                    dve.wait_ge(kcopied, 4 * (order + 1))
                    for f in range(2):
                        uc, us = g.bank[4 + f][:], g.bank[6 + f][:]
                        kc, ks = ker[:, 0, f], ker[:, 1, f]
                        link(nc.vector.tensor_tensor(spec[:, 0, f], uc, kc, ALU.mult))
                        link(nc.vector.tensor_tensor(tmp[:, 0], us, ks, ALU.mult))
                        link(nc.vector.tensor_tensor(spec[:, 0, f], spec[:, 0, f], tmp[:, 0], ALU.subtract))
                        link(nc.vector.tensor_tensor(spec[:, 1, f], uc, ks, ALU.mult))
                        link(nc.vector.tensor_tensor(tmp[:, 1], us, kc, ALU.mult))
                        link(nc.vector.scalar_tensor_tensor(spec[:, 1, f], spec[:, 1, f], -1.0, tmp[:, 1], ALU.mult, ALU.subtract))
                    dve.sem_inc(pointed, 1)
                    dve.wait_ge(inv, order + 1)
                    for i in range(2):
                        link(nc.vector.tensor_tensor(z[:, i], z[:, i], skip[:, order], ALU.mult))
                        link(nc.vector.tensor_tensor(z[:, i], z[:, i], g.bank[i][:], ALU.add))
                        link(nc.vector.tensor_tensor(z[:, i], z[:, i], u[:, i, order], ALU.mult))


def rope_stage(g, q, k):
    nc = g.nc
    loaded, step = new_sem(g, "rope_loaded"), new_sem(g, "rope_step")
    with ExitStack() as ctx:
        tab = ctx.enter_context(nc.sbuf_tensor("rope_tab", [P, 2, 2, P], F32))
        rot = ctx.enter_context(nc.sbuf_tensor("rope_rot", [P, 512], F32))
        with nc.Block() as block:
            @block.sync
            def _(sp):
                sp.dma_start(tab[:], g.dram["t_rope"].rearrange("p (c i d) -> p c i d", c=2, i=2)).then_inc(loaded, 16)

            @block.vector
            def _(dve):
                link = Chain(dve, step)
                dve.wait_ge(loaded, 16)
                for x, off in ((q, 0), (k, 2)):
                    for i in range(2):
                        src = x[:, i + off]
                        for h in range(HEADS):
                            xs = src[:, h * P:(h + 1) * P].rearrange("p (a b c) -> p a b c", a=2, b=2)
                            rs = rot[:, h * P:(h + 1) * P].rearrange("p (a b c) -> p a b c", a=2, b=2)
                            sn = tab[:, 1, i].rearrange("p (a b c) -> p a b c", a=2, b=2)
                            for b in range(2):
                                link(nc.vector.tensor_tensor(rs[:, :, b], xs[:, :, 1 - b], sn[:, :, b], ALU.mult))
                        cos = tab[:, 0, i].unsqueeze(1).broadcast_to([P, HEADS, P])
                        s3 = src.rearrange("p (h d) -> p h d", h=HEADS)
                        link(nc.vector.tensor_tensor(s3, s3, cos, ALU.mult))
                        link(nc.vector.tensor_tensor(src, src, rot[:], ALU.add))


def retention_stage(g, q, k, v, y):
    nc = g.nc
    loaded, turned, copied, scored, exped, weighted, summed, ycopied, step = (new_sem(g, x) for x in (
        "ret_loaded", "qk_turned", "qk_copied", "ret_scored", "ret_exp", "ret_weighted", "ret_summed", "ret_copied", "ret_step"))
    with ExitStack() as ctx:
        sb = lambda n, shape: ctx.enter_context(nc.sbuf_tensor(f"ret_{n}", shape, F32))
        delta, keep, lg = sb("delta", [P, 2, NT, LAT]), sb("keep", [P, 2, 2, LAT]), sb("lg", [P, 2, HEADS])
        qT, kT = sb("qT", [P, HEADS, LAT]), sb("kT", [P, HEADS, T])
        e = sb("e", [P, 2, 2, NT, LAT])
        with nc.Block() as block:
            @block.sync
            def _(sp):
                sp.dma_start(delta[:], g.dram["t_delta"].rearrange("p (d j t) -> p d j t", d=2, j=NT)).then_inc(loaded, 16)
                sp.dma_start(keep[:], g.dram["t_keep"].rearrange("p (d j t) -> p d j t", d=2, j=2)).then_inc(loaded, 16)
                sp.dma_start(lg[:], g.dram["ret_lg"]).then_inc(loaded, 16)

            def values(pe, h):
                pe.wait_ge(weighted, NT * (h + 1))
                if h >= 2:
                    pe.wait_ge(ycopied, h - 1)
                for i in range(2):
                    for j in range(NT):
                        last = nc.tensor.matmul(g.bank[4 + h % 2][:, i * P:(i + 1) * P], e[:, h % 2, 0, j, i * P:(i + 1) * P],
                                                v[:, j, h * P:(h + 1) * P], start=j == 0, stop=j == NT - 1)
                last.then_inc(summed, 1)

            def finish(dve, h):
                dve.wait_ge(summed, h + 1)
                nc.vector.tensor_copy(y[:, :, h * P:(h + 1) * P], g.bank[4 + h % 2][:, 0:LAT].rearrange("p (i d) -> p i d", i=2)).then_inc(ycopied, 1)

            @block.tensor
            def _(pe):
                for h in range(HEADS):
                    if h >= 2:
                        pe.wait_ge(copied, 2 * (h - 1))
                    b = g.bank[2 * (h % 2)]
                    for i in range(2):
                        last = nc.tensor.transpose(b[:, i * P:(i + 1) * P], q[:, i, h * P:(h + 1) * P], g.ident)
                    last.then_inc(turned, 1)
                    b = g.bank[2 * (h % 2) + 1]
                    for i in range(NT):
                        last = nc.tensor.transpose(b[:, i * P:(i + 1) * P], k[:, i, h * P:(h + 1) * P], g.ident)
                    last.then_inc(turned, 1)
                pe.wait_ge(copied, 2 * HEADS)
                for h in range(HEADS):
                    if h >= 2:
                        pe.wait_ge(weighted, NT * (h - 1))
                    for j in range(NT):
                        nc.tensor.matmul(g.bank[2 * (h % 2) + j // 2][:, (j % 2) * LAT:(j % 2 + 1) * LAT], kT[:, h, j * P:(j + 1) * P], qT[:, h],
                                         start=True, stop=True).then_inc(scored, 1)
                    if h >= 1:
                        values(pe, h - 1)
                values(pe, HEADS - 1)

            @block.scalar
            def _(act):
                for h in range(HEADS):
                    act.wait_ge(turned, 2 * h + 1)
                    nc.scalar.activation(qT[:, h], g.bank[2 * (h % 2)][:, 0:LAT], ACT.Copy, scale=float(P) ** -0.5).then_inc(copied, 1)
                    act.wait_ge(turned, 2 * h + 2)
                    nc.scalar.activation(kT[:, h], g.bank[2 * (h % 2) + 1][:], ACT.Copy).then_inc(copied, 1)
                act.wait_ge(loaded, 48)
                for h in range(HEADS):
                    if h >= 2:
                        act.wait_ge(summed, h - 1)
                    for d in range(2):
                        nc.scalar.activation(e[:, h % 2, d], delta[:, d], ACT.Exp, scale=lg[:, d, h:h + 1]).then_inc(exped, 1)

            @block.vector
            def _(dve):
                link = Chain(dve, step)
                dve.wait_ge(loaded, 48)
                for h in range(HEADS):
                    dve.wait_ge(exped, 2 * (h + 1))
                    ef, eb = e[:, h % 2, 0], e[:, h % 2, 1]
                    link(nc.vector.tensor_tensor(ef[:, 2:4], ef[:, 2:4], keep[:, 0], ALU.mult))
                    link(nc.vector.tensor_tensor(eb[:, 2:4], eb[:, 2:4], keep[:, 1], ALU.mult))
                    link(nc.vector.tensor_tensor(ef, ef, eb, ALU.add))
                    for j in range(NT):
                        dve.wait_ge(scored, h * NT + j // 2 * 2 + 2)
                        nc.vector.tensor_tensor(ef[:, j], ef[:, j], g.bank[2 * (h % 2) + j // 2][:, (j % 2) * LAT:(j % 2 + 1) * LAT], ALU.mult).then_inc(weighted, 1)
                    if h >= 1:
                        finish(dve, h - 1)
                finish(dve, HEADS - 1)


def odd_layer(g):
    nc = g.nc
    allt, lat = list(range(NT)), [2, 3]
    modulate_stage(g, 1, 0, 1, allt, 2)
    with ExitStack() as ctx:
        g.mix = ctx.enter_context(nc.sbuf_tensor("mix1", [P, KT, T], F32))
        with ExitStack() as c2:
            sb = lambda n, shape: c2.enter_context(nc.sbuf_tensor(n, shape, F32))
            u, filt = sb("hy_u", [P, 2, 3, HYW]), sb("hy_filt", [P, 2, 2, 2, HYW])
            hyena_filter_stage(g, filt)
            projection_stage(g, g.dram["odd_w_in"], [
                (i, "N", lat, (lambda i: lambda j: u[:, j, i])(i), "copy") for i in range(3)])
            hyena_stage(g, u[:], filt)
            norm_stage(g, u[:, :, 2], lat, HYW // GROUP, False, None, "hy_norm_w", 0, "y")
        with ExitStack() as c2:
            sb = lambda n, shape: c2.enter_context(nc.sbuf_tensor(n, shape, F32))
            q, k, v, rg, y = (sb(n, [P, w, 512]) for n, w in (("r_q", 2), ("r_k", 4), ("r_v", 4), ("r_g", 2), ("r_y", 2)))
            projection_stage(g, g.dram["odd_w_in"], [
                (3, "N", lat, lambda j: q[:, j], "copy"),
                (4, "N", allt, lambda j: k[:, j], "copy"),
                (5, "N", allt, lambda j: v[:, j], "copy"),
                (6, "N", lat, lambda j: rg[:, j], "silu")])
            rope_stage(g, q, k)
            retention_stage(g, q, k, v, y)
            norm_stage(g, y[:], lat, HEADS, True, rg[:], "ret_norm_w", 4, "r")
        residual_stage(g, 1, 0, lat, None, g.dram["odd_w_out"])


def build(nc, dram, out):
    g = Net()
    g.nc, g.dram, g.n_sems, g.sems = nc, dram, 0, []
    with ExitStack() as ctx:
        sb = lambda n, shape: ctx.enter_context(nc.sbuf_tensor(n, shape, F32))
        g.h = sb("h", [P, NT, D])
        g.xt = sb("xt", [P, KT, T])
        c0 = 5 * P + P // CHUNK
        g.base = sb("base", [P, c0 + EXPERTS + 1 + P])
        g.c_cols, g.c_act = sb("c_cols", [P, KT, 2]), sb("c_act", [P, KT, 2])
        g.mods = sb("mods", [P, 2, MODS * KT, 2])
        g.mod_row = sb("mod_row", [P, 2, D])
        g.ident, g.upper, g.lower = (g.base[:, i * P:(i + 1) * P] for i in range(3))
        g.tri_chunk = [g.base[:, (3 + i) * P:(4 + i) * P] for i in range(2)]
        g.chunk_of = g.base[:, 5 * P:c0]
        g.iota_e, g.pcol = g.base[:, c0:c0 + EXPERTS], g.base[:, c0 + EXPERTS:c0 + EXPERTS + 1]
        g.ones = g.base[:, c0 + EXPERTS + 1:]
        g.bank = [ctx.enter_context(nc.psum_tensor(f"bank{i}", [P, 512], F32)) for i in range(8)]
        g.y_dram = nc.dram_tensor("y_slots", (MAX_BLOCKS, P, D), F32, kind="Internal").ap()
        g.y_cleared = nc.alloc_semaphore("y_cleared")
        g.zero_row = sb("zero_row", [P, D])
        load_stage(g)
        ada_stage(g, 0)
        ada_stage(g, 1)
        even_layer(g)
        recycle_sems(g)
        moe(g, 0, list(range(NT)))
        recycle_sems(g)
        odd_layer(g)
        recycle_sems(g)
        moe(g, 1, [2, 3])
        stored = new_sem(g, "out_stored")
        with nc.Block() as block:
            @block.sync
            def _(sp):
                sp.dma_start(out.rearrange("b (i p) d -> p (b i) d", p=P), g.h[:, 2:4]).then_inc(stored, 16)
                sp.wait_ge(stored, 16)


def on_rows(a):
    return np.ascontiguousarray(np.broadcast_to(a[..., None, :, :] if a.ndim > 1 else a[None, None, :], a.shape[:-2] + (P,) + a.shape[-2:] if a.ndim > 1 else (P, 1) + a.shape))


def layout(i):
    i = {k: np.asarray(v) for k, v in i.items()}
    L = 2
    a = dict(shape_tables())
    tok = np.concatenate([i["ctx"][0], i["x"][0]], 0)
    a["x_all"] = tok.reshape(NT, P, D).transpose(1, 0, 2)
    a["c_cols"] = np.stack([i["c"][0], i["c_ctx"]]).reshape(2, KT, P).transpose(2, 1, 0)
    a["ada_w"] = i["ada_w"].reshape(L, KT, P, MODS * D // 512, 512).transpose(0, 3, 2, 1, 4)
    a["ada_b"] = i["ada_b"].reshape(L, MODS * KT, P).transpose(0, 2, 1)
    ln = np.stack([i["ln_w"], i["ln_b"]], 2)
    a["ln_rows"] = np.broadcast_to(ln[:, :, None], (L, 2, P, 2, D))
    we = i["even_w_in"][0]
    groups, gates = np.concatenate([we[:, :1536], we[:, 1552:]], 1), we[:, 1536:1552]
    a["even_w_in"] = groups.reshape(KT, P, 8, 512).transpose(2, 1, 0, 3)
    a["w_gates"] = gates.reshape(KT, P, 16).transpose(1, 0, 2)
    a["gate_b"] = i["mlstm_gate_b"][0].T
    a["odd_w_in"] = i["odd_w_in"][0].reshape(KT, P, 7, 512).transpose(2, 1, 0, 3)
    for n in ("even_w_out", "odd_w_out"):
        a[n] = i[n][0].reshape(KT, P, D).transpose(1, 0, 2)
    for n in ("mlstm_norm_w", "hgrn_norm_w", "ret_norm_w", "hy_norm_w"):
        a[n] = np.broadcast_to(i[n][0][None], (P, 512))
    a["lb_cols"] = i["hgrn_lb"][0].reshape(HEADS, P).T
    a["hy_conv"] = np.broadcast_to(np.concatenate([i["hy_conv_w"][0], i["hy_conv_b"]], 0)[None], (P, 4, 3 * HYW))
    a["hy_w1"] = i["hy_f_w1"][0]
    a["hy_w23"] = np.stack([i["hy_f_w2"][0], i["hy_f_w3"][0]], 1)
    a["hy_cols"] = np.stack([i["hy_f_b1"][0], i["hy_f_b2"][0], i["hy_f_b3"][0], i["hy_f_freq"][0]], 1)
    a["hy_wout"] = i["hy_f_wout"][0].reshape(HYHID, 4, HYW)
    a["hy_skip"] = np.broadcast_to(i["hy_skip"][0][None], (P, 2, HYW))
    a["ret_lg"] = np.broadcast_to(i["ret_log_decay"][0][None], (P, 2, HEADS))
    a["router_w"] = i["router_w"].reshape(L, KT, P, EXPERTS).transpose(0, 2, 1, 3)
    a["router_b"] = np.broadcast_to(i["router_bias"][:, None], (L, P, EXPERTS))

    def expert_rows(w1, w3, w2):
        n = w1.shape[:-2]
        up = np.concatenate([w1, w3], -1).reshape(*n, KT, P, 2 * HID).swapaxes(-3, -2).reshape(*n, P, W13)
        down = w2.reshape(*n, 2, P, D).swapaxes(-3, -2).reshape(*n, P, 2 * D)
        return np.concatenate([up, down], -1)
    routed = expert_rows(i["exp_w1"], i["exp_w3"], i["exp_w2"])
    shared = expert_rows(i["sh_w1"], i["sh_w3"], i["sh_w2"])[:, None]
    a["experts"] = np.concatenate([shared, routed, ], 1).reshape(L * (EXPERTS + 1), P, WEXP)
    return {k: np.ascontiguousarray(v) for k, v in a.items()}


def kernel(**inputs):
    import concourse.bacc as bacc
    from concourse.bass_utils import run_bass_kernel_spmd

    nc = bacc.Bacc("TRN2", target_bir_lowering=False, num_devices=1)
    arrays = {f"in_{k}": v for k, v in layout(inputs).items()}
    dram = {k[3:]: nc.dram_tensor(k, v.shape, F32, kind="ExternalInput").ap() for k, v in arrays.items()}
    out = nc.dram_tensor("out", (1, LAT, D), F32, kind="ExternalOutput").ap()
    build(nc, dram, out)
    return run_bass_kernel_spmd(nc, [arrays], core_ids=[0]).results[0]["out"]
```

```python
import math
from contextlib import ExitStack

import numpy as np
import concourse.bass as bass
from concourse import mybir

P = 128
D = 1024
KT = D // P
T = 512
NT = T // P
CTX = 256
LAT = 256
TW = 512
HEADS = 4
CHUNK = 32
NCH = T // CHUNK
MODS = 6
EXPERTS = 64
TOPK = 8
HID = 256
ROUTED_SCALE = 2.5
ALPHA = 4.0 ** 0.25
EPS = 1e-5
NEG_BIG = -1e30
TINY = 2.0 ** -63
SKIP = 4095
SB = P // 2


def most_blocks(tokens):
    return (EXPERTS + (tokens * TOPK - EXPERTS) // SB + 1) // 2 * 2


MAX_BLOCKS, MIN_BLOCKS = most_blocks(T), T * TOPK // SB
CLEAR = 16
CLEARS = (MAX_BLOCKS - MIN_BLOCKS) // CLEAR
SLOTS = 4
MIN_PAIRS = EXPERTS // 2
HYW = 512
HYHID = 64
HYEMB = 33
NFREQ = 256
GROUP = 64
W13 = 2 * KT * HID
WEXP = W13 + 2 * D
EVEN_GROUPS = ("qk", "v", "o", "hq", "hi", "ff", "fb", "hg")
ODD_GROUPS = ("gate0", "gate1", "z", "rq", "rk", "rv", "rg")

F32 = mybir.dt.float32
U32 = mybir.dt.uint32
ALU = mybir.AluOpType
ACT = mybir.ActivationFunctionType
AX = mybir.AxisListType


def shape_tables():
    i = np.arange(P)
    ident = np.eye(P, dtype=np.float32)
    upper = (i[:, None] <= i[None, :]).astype(np.float32)
    lower = (i[:, None] >= i[None, :]).astype(np.float32)
    same = (i[:, None] // CHUNK) == (i[None, :] // CHUNK)
    chunk_of = (i[:, None] // CHUNK == np.arange(P // CHUNK)[None, :]).astype(np.float32)
    iota_e = np.broadcast_to(np.arange(EXPERTS, dtype=np.float32), (P, EXPERTS))
    base = np.concatenate([ident, upper, lower, upper * same, lower * same, chunk_of, iota_e,
                           i[:, None].astype(np.float32), np.ones((P, P), np.float32)], axis=1)
    negsel = np.zeros((HEADS, HEADS, P), np.float32)
    for h in range(HEADS):
        negsel[h, h] = -1.0

    pos = np.arange(LAT, dtype=np.float32)
    inv = (np.float32(10000.0) ** (-np.arange(0, 64, 2, dtype=np.float32) / np.float32(64))).astype(np.float32)
    parts_c, parts_s = [], []
    for p in (np.floor(pos / 64), np.mod(pos, 64)):
        ang = (p[:, None].astype(np.float32) * inv[None, :]).astype(np.float32)
        c, s = np.cos(ang).astype(np.float32), np.sin(ang).astype(np.float32)
        parts_c += [c, c]
        parts_s += [-s, s]
    rope = np.stack([np.concatenate(parts_c, 1), np.concatenate(parts_s, 1)])
    rope = rope.reshape(2, 2, P, P).transpose(2, 0, 1, 3).reshape(P, -1)

    s = np.arange(T)[:, None]
    t = np.arange(LAT)[None, :]
    is_ctx = s < CTX
    d_fwd = np.where(is_ctx, CTX + t - s, t - (s - CTX))
    d_bwd = np.where(is_ctx, CTX - t + s, (s - CTX) - t)
    delta = np.stack([np.maximum(d_fwd, 0), np.maximum(d_bwd, 0)]).astype(np.float32)
    keep = np.stack([d_fwd >= 0, d_bwd >= 0]).astype(np.float32)[:, CTX:]
    delta = delta.reshape(2, NT, P, LAT).transpose(2, 0, 1, 3).reshape(P, -1)
    keep = keep.reshape(2, 2, P, LAT).transpose(2, 0, 1, 3).reshape(P, -1)

    lags = np.arange(LAT, dtype=np.float64)
    omega = 2.0 * np.pi * (np.arange(NFREQ) + 0.5) / (2 * LAT)
    cos = np.cos(lags[:, None] * omega[None, :]).astype(np.float32)
    sin = np.sin(lags[:, None] * omega[None, :]).astype(np.float32)
    fwd = np.stack([cos, sin]).reshape(2, 2, P, NFREQ).transpose(2, 0, 1, 3).reshape(P, -1)
    inv_t = np.stack([cos.T, -sin.T]).astype(np.float64) / NFREQ
    inv_t = inv_t.astype(np.float32).reshape(2, 2, P, LAT).transpose(2, 0, 1, 3).reshape(P, -1)
    dft = np.concatenate([fwd, inv_t], axis=1)

    tt = (pos / np.float32(LAT - 1))[:, None]
    bands = (HYEMB - 1) // 2
    w = (np.float32(2.0 * math.pi) * pos[:, None] / np.float32(LAT)
         * np.linspace(1e-4, bands - 1, bands, dtype=np.float32)[None, :]).astype(np.float32)
    z = np.concatenate([tt, np.cos(w), np.sin(w)], -1).astype(np.float32)
    deltas = np.abs(np.linspace(math.log(1e-2) / 1.5, math.log(1e-2) / 0.3, HYW, dtype=np.float32))
    decay = np.exp(-tt * deltas[None, :]).astype(np.float32)
    decay_b = decay.copy()
    decay_b[0] = 0.0
    decay = np.stack([decay, decay_b]).reshape(2, 2, P, HYW).transpose(2, 0, 1, 3).reshape(P, -1)
    return {
        "t_base": base, "t_negsel": negsel.reshape(HEADS, -1), "t_rope": rope, "t_delta": delta,
        "t_keep": keep, "t_dft": dft, "t_z": np.ascontiguousarray(z.T), "t_decay": decay,
    }


class Net:
    pass


def new_sem(g, name):
    g.n_sems += 1
    sem = g.nc.alloc_semaphore(f"{name}_{g.n_sems}")
    g.sems.append(sem)
    return sem


def recycle_sems(g):
    g.nc.clear_and_free_semaphores(g.sems)
    g.sems = []
    g.nc.all_engine_barrier()


class Chain:

    def __init__(self, eng, sem):
        self.eng, self.sem, self.n = eng, sem, 0

    def __call__(self, ins):
        self.n += 1
        ins.then_inc(self.sem, 1)
        self.eng.wait_ge(self.sem, self.n)


class Prefetch:
    def __init__(self, g, ctx, name, shape, source):
        self.tile = ctx.enter_context(g.nc.sbuf_tensor(name, shape, F32))
        self.loaded, self.source = new_sem(g, f"{name}_loaded"), source

    def start(self, eng):
        eng.dma_start(self.tile[:], self.source).then_inc(self.loaded, 16)


def load_stage(g):
    nc = g.nc
    loaded = new_sem(g, "const_loaded")
    act_done = new_sem(g, "silu_done")
    zeroed = new_sem(g, "zero_row_ready")
    loads = [(g.h[:], g.dram["x_all"]), (g.base[:], g.dram["t_base"]), (g.c_cols[:], g.dram["c_cols"])]
    with nc.Block() as block:
        @block.sync
        def _(sp):
            for dst, src in loads:
                sp.dma_start(dst, src).then_inc(loaded, 16)

        @block.gpsimd
        def _(pool):
            pool.memset(g.zero_row[:], 0.0).then_inc(zeroed, 1)
            pool.memset(g.ada_rows[:], 0.0).then_inc(zeroed, 1)
            pool.wait_ge(zeroed, 2)

        @block.scalar
        def _(act):
            act.wait_ge(loaded, 16 * len(loads))
            nc.scalar.activation(g.c_act[:], g.c_cols[:], ACT.Silu).then_inc(act_done, 1)
            act.wait_ge(act_done, 1)


class AdaRows:
    PIECES, PER_GROUP = 12, 4

    def __init__(self, g, l, ring, slots, banks):
        self.g, self.l, self.slots, self.banks = g, l, slots, banks
        self.ring = ring.rearrange("p (s k c) -> p s k c", s=slots, k=2)
        self.loaded = [new_sem(g, "ada_w_loaded") for _ in range(slots)]
        self.used, self.copied = new_sem(g, "ada_w_used"), new_sem(g, "ada_rows_copied")

    def load_piece(self, eng, n):
        if n >= self.slots:
            eng.wait_ge(self.used, n - self.slots + 1)
        src = self.g.dram["ada_w"][self.l, n // self.PER_GROUP, n % self.PER_GROUP]
        eng.dma_start(self.ring[:, n % self.slots], src).then_inc(self.loaded[n % self.slots], 16)

    def multiply(self, pe, n):
        group, part = n // self.PER_GROUP, n % self.PER_GROUP
        pe.wait_ge(self.loaded[n % self.slots], 16 * (n // self.slots + 1))
        if part == 0 and group >= 2:
            pe.wait_ge(self.copied, 4 * (group - 1))
        bank = self.g.bank[self.banks[group % 2]]
        for kk in range(2):
            k = 2 * part + kk
            for j in range(4):
                last = self.g.nc.tensor.matmul(bank[32 * j:32 * j + 2, :], self.g.c_act[:, k, :],
                                               self.ring[:, n % self.slots, kk, j * 512:(j + 1) * 512],
                                               start=k == 0, stop=k == KT - 1)
        last.then_inc(self.used, 1)

    def copy(self, act, group):
        act.wait_ge(self.used, self.PER_GROUP * (group + 1))
        for j in range(4):
            self.g.nc.scalar.activation(self.g.ada_rows[32 * j:32 * j + 2, group], self.g.bank[self.banks[group % 2]][32 * j:32 * j + 2, :],
                                        ACT.Copy).then_inc(self.copied, 1)


    def load(self, eng):
        for n in range(self.PIECES):
            self.load_piece(eng, n)

    def pe(self, pe, n):
        if 4 <= n < 4 + self.PIECES:
            self.multiply(pe, n - 4)

    def act(self, act, n):
        if n in (8, 12, 16):
            self.copy(act, n // 4 - 2)

    def dve(self, dve, n):
        pass


def ada_rows_stage(g, l):
    nc = g.nc
    with ExitStack() as ctx:
        ring = ctx.enter_context(nc.sbuf_tensor(f"ada_ring{l}", [P, 4 * 2 * 2048], F32))
        rows = AdaRows(g, l, ring[:], 4, (0, 1))
        with nc.Block() as block:
            @block.sync
            def _(sp):
                rows.load(sp)

            @block.tensor
            def _(pe):
                for n in range(rows.PIECES):
                    rows.multiply(pe, n)

            @block.scalar
            def _(act):
                for group in range(3):
                    rows.copy(act, group)


def ada_columns_stage(g, l):
    nc = g.nc
    bias_loaded, turned, added = (new_sem(g, n) for n in ("ada_b_loaded", "ada_turned", "ada_added"))
    with ExitStack() as ctx:
        bias = ctx.enter_context(nc.sbuf_tensor(f"ada_bias{l}", [P, MODS * KT], F32))
        with nc.Block() as block:
            @block.sync
            def _(sp):
                sp.dma_start(bias[:], g.dram["ada_b"][l]).then_inc(bias_loaded, 16)

            @block.tensor
            def _(pe):
                for group in range(3):
                    for c in range(4):
                        last = nc.tensor.transpose(g.bank[group][:, c * P:(c + 1) * P], g.ada_rows[:, group, c * P:(c + 1) * P], g.ident)
                    last.then_inc(turned, 1)

            @block.vector
            def _(dve):
                link = Chain(dve, added)
                dve.wait_ge(bias_loaded, 16)
                mods = g.mods[:, l]
                for group in range(3):
                    dve.wait_ge(turned, group + 1)
                    part = slice(group * 16, group * 16 + 16)
                    src = g.bank[group][:].rearrange("p (c j x) -> p j c x", c=4, x=32)[:, :, :, 0:2]
                    link(nc.vector.tensor_tensor(mods[:, part].rearrange("p (j c) v -> p j c v", j=4), src,
                                                 bias[:, part].rearrange("p (j c) -> p j c", j=4).unsqueeze(3).broadcast_to([P, 4, 4, 2]), ALU.add))
                for which in (1, 4):
                    part = mods[:, which * KT:(which + 1) * KT, :]
                    link(nc.vector.tensor_scalar(part, part, 1.0, None, ALU.add))


def modulate_stage(g, l, shift, scale, tiles, rows, prefetch):
    nc = g.nc
    t0, n = tiles[0] * P, len(tiles) * P
    streams = [(1, 0, CTX), (0, CTX, T)] if tiles[0] == 0 else [(0, CTX, T)]
    turned, modulated, row_ready, row_copied = (new_sem(g, x) for x in ("turned", "modulated", "row_ready", "row_copied"))
    mods = g.mods[:, l]
    with nc.Block() as block:
        @block.sync
        def _(sp):
            prefetch.start(sp)

        @block.tensor
        def _(pe):
            for k in range(KT):
                if k >= 4:
                    pe.wait_ge(modulated, len(streams) * (k - 3))
                for i in tiles:
                    last = nc.tensor.transpose(g.bank[k % 4][:, i * P:(i + 1) * P], g.h[:, i, k * P:(k + 1) * P], g.ident)
                last.then_inc(turned, 1)
            for v in range(2):
                for k in range(KT):
                    col = mods[:, rows * KT + k, v:v + 1].broadcast_to([P, P])
                    last = nc.tensor.matmul(g.bank[4 + 2 * v + k // 4][:, (k % 4) * P:(k % 4 + 1) * P], col, g.ident,
                                            start=True, stop=True)
            last.then_inc(row_ready, 1)

        @block.scalar
        def _(act):
            for k in range(KT):
                act.wait_ge(turned, k + 1)
                for v, a, b in streams:
                    nc.scalar.activation(g.xt[:, k, a:b], g.bank[k % 4][:, a:b], ACT.Identity,
                                         bias=mods[:, shift * KT + k, v:v + 1],
                                         scale=mods[:, scale * KT + k, v:v + 1]).then_inc(modulated, 1)

        @block.vector
        def _(dve):
            dve.wait_ge(row_ready, 1)
            for v in range(2):
                for half in range(2):
                    nc.vector.tensor_copy(g.mod_row[:, v, half * 512:(half + 1) * 512],
                                          g.bank[4 + 2 * v + half][:]).then_inc(row_copied, 1)


class InputWeights:
    SLOTS = 3

    def __init__(self, g, ctx, weights, groups):
        self.weights, self.groups = weights, groups
        self.ring = ctx.enter_context(g.nc.sbuf_tensor(f"w_in_ring{g.n_sems}", [P, self.SLOTS, KT, 512], F32))
        self.loaded = [new_sem(g, "w_in_loaded") for _ in range(self.SLOTS)]
        self.next = 0

    def load(self, eng):
        slot = self.next % self.SLOTS
        eng.dma_start(self.ring[:, slot], self.weights[self.groups[self.next]]).then_inc(self.loaded[slot], 16)
        self.next += 1

    def start(self, eng):
        for _ in self.groups[:self.SLOTS]:
            self.load(eng)


def projection_stage(g, weights, jobs, side=None, prefetched=None):
    nc = g.nc
    produced, squashed, act_evac, dve_evac = (new_sem(g, x) for x in ("proj_produced", "proj_sigmoid", "proj_act_evac", "proj_dve_evac"))
    outs = []
    for gi, (_, kind, tiles, dst, fn) in enumerate(jobs):
        for j in (range(4) if kind == "T" else range(len(tiles))):
            outs.append((gi, kind, tiles, j, dst, fn))
    last_of = {gi: n for n, (gi, *_) in enumerate(outs)}
    emptied, counts = [], {"act": 0, "dve": 0}
    for *_, fn in outs:
        who = "act" if fn == "sigmoid" else "dve"
        counts[who] += 1
        emptied.append((act_evac if who == "act" else dve_evac, counts[who]))
    silus = [n for n, o in enumerate(outs) if o[-1] == "silu"]
    with ExitStack() as ctx:
        w_in = prefetched or InputWeights(g, ctx, weights, [w for w, *_ in jobs])
        ring, loaded, SLOTS = w_in.ring, w_in.loaded, w_in.SLOTS
        sig = ctx.enter_context(nc.sbuf_tensor(f"sig{g.n_sems}", [P, 2, 512], F32))
        side = side(ctx) if side else None
        BANKS = 6 if side else 8
        if side:
            side.emptied = emptied
        with nc.Block() as block:
            @block.sync
            def _(sp):
                for gi in range(w_in.next, len(jobs)):
                    if gi >= SLOTS:
                        sp.wait_ge(produced, last_of[gi - SLOTS] + 1)
                    w_in.load(sp)

            if side:
                @block.gpsimd
                def _(pool):
                    side.load(pool)

            @block.tensor
            def _(pe):
                for n, (gi, kind, tiles, j, dst, fn) in enumerate(outs):
                    if side:
                        side.pe(pe, n)
                    w = ring[:, gi % SLOTS]
                    if j == 0:
                        pe.wait_ge(loaded[gi % SLOTS], 16 * (gi // SLOTS + 1))
                    if n >= BANKS:
                        pe.wait_ge(*emptied[n - BANKS])
                    a, b = tiles[0] * P, (tiles[-1] + 1) * P
                    for k in range(KT):
                        if kind == "T":
                            last = nc.tensor.matmul(g.bank[n % BANKS][:, 0:b - a], w[:, k, j * P:(j + 1) * P], g.xt[:, k, a:b],
                                                    start=k == 0, stop=k == KT - 1)
                        else:
                            i = tiles[j]
                            last = nc.tensor.matmul(g.bank[n % BANKS][:], g.xt[:, k, i * P:(i + 1) * P], w[:, k, :],
                                                    start=k == 0, stop=k == KT - 1)
                    last.then_inc(produced, 1)

            @block.scalar
            def _(act):
                for n, (gi, kind, tiles, j, dst, fn) in enumerate(outs):
                    if side:
                        side.act(act, n)
                    wd = (tiles[-1] + 1 - tiles[0]) * P if kind == "T" else 512
                    src = g.bank[n % BANKS][:, 0:wd]
                    if fn == "sigmoid":
                        act.wait_ge(produced, n + 1)
                        nc.scalar.activation(dst(j), src, ACT.Sigmoid).then_inc(act_evac, 1)
                    elif fn == "silu":
                        m = silus.index(n)
                        act.wait_ge(produced, n + 1)
                        if m >= 2:
                            act.wait_ge(*emptied[silus[m - 2]])
                        nc.scalar.activation(sig[:, m % 2, 0:wd], src, ACT.Sigmoid).then_inc(squashed, 1)

            @block.vector
            def _(dve):
                for n, (gi, kind, tiles, j, dst, fn) in enumerate(outs):
                    if side:
                        side.dve(dve, n)
                    wd = (tiles[-1] + 1 - tiles[0]) * P if kind == "T" else 512
                    src = g.bank[n % BANKS][:, 0:wd]
                    if fn == "sigmoid":
                        continue
                    if fn == "silu":
                        m = silus.index(n)
                        dve.wait_ge(squashed, m + 1)
                        nc.vector.tensor_tensor(dst(j), src, sig[:, m % 2, 0:wd], ALU.mult).then_inc(dve_evac, 1)
                        continue
                    dve.wait_ge(produced, n + 1)
                    if fn == "heads":
                        src = src.rearrange("p (h d) -> p h d", h=HEADS)
                    if fn == "q_scale" and j < 2:
                        nc.vector.tensor_scalar(dst(j), src, 64.0 ** -0.5, None, ALU.mult).then_inc(dve_evac, 1)
                    else:
                        nc.vector.tensor_copy(dst(j), src).then_inc(dve_evac, 1)


def mlstm_tiles(d, j):
    if d == 0:
        return [(j, j + 1)] + ([(j + 1, NT)] if j + 1 < NT else [])
    if j >= 2:
        return [(j, j + 1)] + ([(2, j)] if j > 2 else [])
    return [(j, j + 1)] + ([(0, j)] if j > 0 else []) + [(2, NT)]


def key_tiles(d, i):
    return [j for j in range(NT) if any(a <= i < b for a, b in mlstm_tiles(d, j))]


def gates_stage(g, s):
    nc = g.nc
    loaded, made, activated, step, turned = (new_sem(g, x) for x in ("gate_w_loaded", "gates_made", "gate_act", "gate_step", "gate_turned"))
    act_step, moved = new_sem(g, "gate_act_step"), new_sem(g, "gates_moved")
    with ExitStack() as ctx:
        wg = ctx.enter_context(nc.sbuf_tensor("w_gates", [P, KT, 4 * HEADS], F32))
        gb = ctx.enter_context(nc.sbuf_tensor("gate_b", [HEADS, 4], F32))
        tmp = {n: ctx.enter_context(nc.sbuf_tensor(f"gate_{n}", [HEADS, 2, T], F32)) for n in ("x", "e", "lf", "B", "a", "m", "ones")}
        with nc.Block() as block:
            @block.sync
            def _(sp):
                sp.dma_start(wg[:], g.dram["w_gates"]).then_inc(loaded, 16)
                sp.dma_start(gb[:], g.dram["gate_b"]).then_inc(loaded, 16)

            @block.tensor
            def _(pe):
                pe.wait_ge(loaded, 32)
                for k in range(KT):
                    for q in range(4):
                        last = nc.tensor.matmul(g.bank[0][32 * q:32 * q + HEADS, :], wg[:, k, q * HEADS:(q + 1) * HEADS], g.xt[:, k, :],
                                                start=k == 0, stop=k == KT - 1)
                last.then_inc(made, 1)
                pe.wait_ge(step, s["n_rows"])
                for d in range(2):
                    for c, src in enumerate((tmp["a"], tmp["m"])):
                        for i in range(NT):
                            at = ((d * 2 + c) * NT + i) * HEADS
                            last = nc.tensor.transpose(g.bank[4][:, at:at + HEADS], src[:, d, i * P:(i + 1) * P],
                                                       g.ident[0:HEADS, 0:HEADS])
                last.then_inc(turned, 1)

            @block.scalar
            def _(act):
                act.wait_ge(made, 1)
                for q in range(4):
                    nc.scalar.activation(tmp["x" if q % 2 else "a"][:, q // 2], g.bank[0][32 * q:32 * q + HEADS, :], ACT.Copy).then_inc(moved, 1)
                act.wait_ge(step, s["n_abs"])
                nc.scalar.activation(tmp["e"][:], tmp["e"][:], ACT.Exp, scale=-1.0).then_inc(act_step, 1)
                act.wait_ge(act_step, 1)
                nc.scalar.activation(tmp["e"][:], tmp["e"][:], ACT.Ln, bias=1.0).then_inc(activated, 1)
                act.wait_ge(turned, 1)
                cols = g.bank[4][:, 0:2 * 2 * NT * HEADS].rearrange("p (d c i) -> p d c i", d=2, c=2)
                nc.scalar.activation(s["a_col"][:], cols[:, :, 0, :], ACT.Copy).then_inc(activated, 1)
                nc.scalar.activation(s["floor_col"][:], cols[:, :, 1, :], ACT.Exp, scale=-1.0).then_inc(activated, 1)

            @block.vector
            def _(dve):
                link = Chain(dve, step)
                link(nc.vector.memset(tmp["ones"][:], 1.0))
                dve.wait_ge(loaded, 32)
                for d in range(2):
                    dve.wait_ge(moved, 2 * d + 2)
                    link(nc.vector.tensor_scalar(tmp["x"][:, d], tmp["x"][:, d], gb[:, 2 * d + 1:2 * d + 2], None, ALU.add))
                    link(nc.vector.tensor_scalar(tmp["a"][:, d], tmp["a"][:, d], gb[:, 2 * d:2 * d + 1], None, ALU.add))
                link(nc.vector.scalar_tensor_tensor(tmp["e"][:], tmp["x"][:], -1.0, tmp["x"][:], ALU.mult, ALU.max))
                s["n_abs"] = link.n
                dve.wait_ge(activated, 1)
                link(nc.vector.scalar_tensor_tensor(tmp["lf"][:], tmp["x"][:], 0.0, tmp["e"][:], ALU.min, ALU.subtract))
                ones, lf, B, a, M = tmp["ones"], tmp["lf"], tmp["B"], tmp["a"], s["max_row"]
                link(nc.vector.tensor_tensor_scan(B[:, 0, :], ones[:, 0, :], lf[:, 0, :], 0.0, ALU.mult, ALU.add))
                link(nc.vector.tensor_tensor_scan(B[:, 1, 0:CTX][:, ::-1], ones[:, 0, 0:CTX], lf[:, 1, 0:CTX][:, ::-1], 0.0, ALU.mult, ALU.add))
                link(nc.vector.tensor_tensor_scan(B[:, 1, CTX:T][:, ::-1], ones[:, 0, 0:LAT], lf[:, 1, CTX:T][:, ::-1], B[:, 1, 0:1], ALU.mult, ALU.add))
                link(nc.vector.tensor_tensor(a[:], a[:], B[:], ALU.subtract))
                link(nc.vector.tensor_tensor_scan(M[:, 0, :], a[:, 0, :], a[:, 0, :], NEG_BIG, ALU.max, ALU.max))
                ac, al = a[:, 1, 0:CTX][:, ::-1], a[:, 1, CTX:T][:, ::-1]
                link(nc.vector.tensor_tensor_scan(M[:, 1, 0:CTX][:, ::-1], ac, ac, NEG_BIG, ALU.max, ALU.max))
                link(nc.vector.tensor_tensor_scan(M[:, 1, CTX:T][:, ::-1], al, al, M[:, 1, 0:1], ALU.max, ALU.max))
                link(nc.vector.tensor_tensor(tmp["m"][:], B[:], M[:], ALU.add))
                s["n_rows"] = link.n


def mlstm_stage(g, s):
    nc = g.nc
    scored, row_max_ready, clamped, exped, weighted, read, summed, step = (
        new_sem(g, x) for x in ("scores_ready", "max_rows_ready", "clamped", "exp_ready", "weights_ready",
                                "scores_used", "values_summed", "dve_step"))
    units = [(h, d) for h in range(HEADS) for d in range(2)]
    pieces = [(u, j, n, rng) for u, (h, d) in enumerate(units) for j in range(NT)
              for n, rng in enumerate(mlstm_tiles(d, j))]
    tri = {0: g.upper, 1: g.lower}
    with ExitStack() as ctx:
        e = ctx.enter_context(nc.sbuf_tensor("mlstm_e", [P, 2, NT, T], F32))
        sm = ctx.enter_context(nc.sbuf_tensor("mlstm_small", [P, 2, 3, NT], F32))
        loaded = new_sem(g, "negsel_loaded")
        negsel = ctx.enter_context(nc.sbuf_tensor("negsel", [HEADS, HEADS, P], F32))
        S = g.bank[0:4]
        ndone = {u: sum(1 for p in pieces if p[0] <= u) for u in range(len(units))}
        ndone[-1] = 0
        with nc.Block() as block:
            @block.sync
            def _(sp):
                sp.dma_start(negsel[:], g.dram["t_negsel"].rearrange("h (a b) -> h a b", a=HEADS)).then_inc(loaded, 16)
                src = g.zero_row[:].unsqueeze(1).broadcast_to([P, CLEAR // 2, D])
                for b in range(MIN_BLOCKS, MAX_BLOCKS, CLEAR):
                    sp.dma_start(g.y_dram[b:b + CLEAR].rearrange("(b c) s d -> (c s) b d", c=2), src).then_inc(g.y_cleared, 16)

            @block.tensor
            def _(pe):
                pe.wait_ge(loaded, 16)

                def scores(u):
                    h, d = units[u]
                    if u >= 2:
                        pe.wait_ge(clamped, ndone[u - 2])
                    nc.tensor.matmul(g.bank[4 + d][:], negsel[:, h, :], s["max_row"][:, d, :], start=True, stop=True).then_inc(row_max_ready, 1)
                    if d == 0:
                        if u >= 1:
                            pe.wait_ge(weighted, ndone[u - 1])
                        r = slice(64 * (h % 2), 64 * (h % 2) + 64)
                        for j in range(NT):
                            nc.tensor.matmul(S[j][:], s["kT"][r, h // 2, j * P:(j + 1) * P], s["qT"][r, h // 2, :],
                                             start=True, stop=True).then_inc(scored, 1)

                def values(u):
                    h, d = units[u]
                    pe.wait_ge(weighted, ndone[u])
                    if u >= 1:
                        pe.wait_ge(read, u)
                    for i in range(NT):
                        keys = key_tiles(d, i)
                        for j in keys:
                            last = nc.tensor.matmul(g.bank[6 + i // 2][:, (i % 2) * 256:(i % 2) * 256 + P + 1],
                                                    e[:, u % 2, j, i * P:(i + 1) * P], s["v1"][:, j, h, :],
                                                    start=j == keys[0], stop=j == keys[-1])
                    last.then_inc(summed, 1)

                scores(0)
                scores(1)
                for u in range(len(units)):
                    values(u)
                    if u + 2 < len(units):
                        scores(u + 2)

            @block.scalar
            def _(act):
                for n, (u, j, k, (a, b)) in enumerate(pieces):
                    act.wait_ge(clamped, n + 1)
                    w = e[:, u % 2, j, a * P:b * P]
                    nc.scalar.activation(w, w, ACT.Exp).then_inc(exped, 1)

            @block.vector
            def _(dve):
                link = Chain(dve, step)

                def clamp(u):
                    h, d = units[u]
                    dve.wait_ge(row_max_ready, u + 1)
                    if u >= 2:
                        dve.wait_ge(summed, u - 1)
                    for (uu, j, k, (a, b)) in pieces:
                        if uu == u:
                            nc.vector.tensor_scalar(e[:, u % 2, j, a * P:b * P], g.bank[4 + d][:, a * P:b * P],
                                                    s["a_col"][:, d, j * HEADS + h:j * HEADS + h + 1], 0.0,
                                                    ALU.add, ALU.min).then_inc(clamped, 1)

                def weigh(u):
                    h, d = units[u]
                    for n, (uu, j, k, (a, b)) in enumerate(pieces):
                        if uu != u:
                            continue
                        dve.wait_ge(exped, n + 1)
                        w = e[:, u % 2, j, a * P:b * P]
                        if k == 0:
                            if d == 0:
                                dve.wait_ge(scored, h * NT + j + 1)
                            link(nc.vector.tensor_tensor(w, w, tri[d], ALU.mult))
                        nc.vector.tensor_tensor(w, w, S[j][:, a * P:b * P], ALU.mult).then_inc(weighted, 1)

                def finish(u):
                    h, d = units[u]
                    dve.wait_ge(summed, u + 1)
                    x = sm[:, u % 2]
                    den, neg, inv = x[:, 0], x[:, 1], x[:, 2]
                    for half in range(2):
                        b = g.bank[6 + half][:].rearrange("p (i w) -> p i w", i=2)[:, :, P]
                        link(nc.vector.tensor_copy(den[:, 2 * half:2 * half + 2], b))
                    link(nc.vector.scalar_tensor_tensor(neg, den, -1.0, den, ALU.mult, ALU.max))
                    fl = s["floor_col"][:, d].rearrange("p (i h) -> p i h", h=HEADS)[:, :, h]
                    link(nc.vector.tensor_tensor(neg, neg, fl, ALU.max))
                    link(nc.vector.reciprocal(inv, neg))
                    for i in range(NT):
                        src = g.bank[6 + i // 2][:, (i % 2) * 256:(i % 2) * 256 + P]
                        dst = s["y"][:, i, h * P:(h + 1) * P]
                        if d == 0:
                            ins = nc.vector.tensor_scalar(dst, src, inv[:, i:i + 1], None, ALU.mult)
                        else:
                            ins = nc.vector.scalar_tensor_tensor(dst, src, inv[:, i:i + 1], dst, ALU.mult, ALU.add)
                        link(ins)
                    dve.sem_inc(read, 1)

                clamp(0)
                clamp(1)
                weigh(0)
                for u in range(len(units)):
                    if u + 1 < len(units):
                        weigh(u + 1)
                    finish(u)
                    if u + 2 < len(units):
                        clamp(u + 2)


def norm_stage(g, y, tiles, groups, center, gate, w_name, mix_base, tag, prefetch=None):
    nc = g.nc
    nt = len(tiles)
    width = 512 // groups
    loaded, step, rooted, turned, copied = (new_sem(g, x) for x in ("norm_w_loaded", "norm_step", "norm_root", "mix_turned", "mix_copied"))
    with ExitStack() as ctx:
        sq = ctx.enter_context(nc.sbuf_tensor(f"norm_sq_{tag}", [P, nt, 512], F32))
        st = ctx.enter_context(nc.sbuf_tensor(f"norm_st_{tag}", [P, 2, nt, groups], F32))
        w = ctx.enter_context(nc.sbuf_tensor(f"norm_w_{tag}", [P, 512], F32))
        marks = {}
        flat = y.rearrange("p i (n w) -> p i n w", w=width)
        sqf = sq[:].rearrange("p i (n w) -> p i n w", w=width)
        with nc.Block() as block:
            @block.sync
            def _(sp):
                sp.dma_start(w[:], g.dram[w_name]).then_inc(loaded, 16)
                if prefetch:
                    prefetch.start(sp)

            @block.vector
            def _(dve):
                link = Chain(dve, step)
                if center:
                    link(nc.vector.tensor_reduce(st[:, 0], flat, AX.X, ALU.add))
                    link(nc.vector.tensor_scalar(st[:, 0], st[:, 0], 1.0 / width, None, ALU.mult))
                    link(nc.vector.tensor_tensor(flat, flat, st[:, 0].unsqueeze(3).broadcast_to([P, nt, groups, width]), ALU.subtract))
                link(nc.vector.tensor_tensor(sq[:], y, y, ALU.mult))
                link(nc.vector.tensor_reduce(st[:, 1], sqf, AX.X, ALU.add))
                link(nc.vector.tensor_scalar(st[:, 1], st[:, 1], 1.0 / width, EPS, ALU.mult, ALU.add))
                marks["var"] = link.n
                dve.wait_ge(rooted, 1)
                link(nc.vector.reciprocal(st[:, 1], st[:, 1]))
                link(nc.vector.tensor_tensor(flat, flat, st[:, 1].unsqueeze(3).broadcast_to([P, nt, groups, width]), ALU.mult))
                dve.wait_ge(loaded, 16)
                link(nc.vector.tensor_tensor(y, y, w[:].unsqueeze(1).broadcast_to([P, nt, 512]), ALU.mult))
                if gate is not None:
                    link(nc.vector.tensor_tensor(y, y, gate, ALU.mult))
                marks["gated"] = link.n

            @block.scalar
            def _(act):
                act.wait_ge(step, marks["var"])
                nc.scalar.activation(st[:, 1], st[:, 1], ACT.Sqrt).then_inc(rooted, 1)
                for c in range(4):
                    act.wait_ge(turned, c + 1)
                    nc.scalar.activation(g.mix[:, mix_base + c, tiles[0] * P:(tiles[-1] + 1) * P],
                                         g.bank[c][:, 0:nt * P], ACT.Copy).then_inc(copied, 1)

            @block.tensor
            def _(pe):
                pe.wait_ge(step, marks["gated"])
                for c in range(4):
                    for n in range(nt):
                        last = nc.tensor.transpose(g.bank[c][:, n * P:(n + 1) * P], y[:, n, c * P:(c + 1) * P], g.ident)
                    last.then_inc(turned, 1)


def hgrn_stage(g, work, s):
    nc = g.nc
    TILE_CH = P // CHUNK
    SR = 2 * TILE_CH + 1
    (lb_loaded, prep, act_prep, vmasked, zeroed, turned, k1_ready, scored, masked, located, stated, out_ready,
     added) = (new_sem(g, x) for x in (
        "lb_loaded", "hgrn_prep", "hgrn_act", "v_masked", "sc_zeroed", "k1_turned", "k1_ready", "hgrn_scored",
        "hgrn_masked", "s_loc_ready", "state_ready", "hgrn_out_ready", "hgrn_added"))
    lb_step = new_sem(g, "lb_step")
    lb_act = new_sem(g, "lb_act")
    with ExitStack() as ctx:
        sb = lambda n, shape: ctx.enter_context(nc.sbuf_tensor(f"hgrn_{n}", shape, F32))
        lbw = sb("lb", [P, 4, HEADS])
        k, A = (sb(n, [P, HEADS * T]) for n in ("k", "A"))
        E, D1, Q1, K1 = (work[:, i * HEADS * T:(i + 1) * HEADS * T] for i in range(4))
        reset = sb("reset", [P, T])
        dend = sb("dend", [P, HEADS * NCH])
        vmask = sb("vmask", [P, 2, HEADS, TILE_CH * P])
        k1t = sb("k1t", [P, 2, HEADS, P])
        sc = sb("sc", [P, 2, 2, HEADS, P])
        st = sb("state", [P, HEADS, TILE_CH + 1, P])
        st_more = E.rearrange("p (h s v) -> p h s v", h=HEADS, v=P)

        def state(h, chunk):
            slot = chunk % SR
            return st[:, h, slot] if slot <= TILE_CH else st_more[:, h, slot - TILE_CH - 1]

        def per_chunk(x):
            return x.rearrange("p (c t) -> p c t", t=CHUNK)

        with nc.Block() as block:
            @block.sync
            def _(sp):
                sp.dma_start(lbw[:, 0], g.dram["lb_cols"]).then_inc(lb_loaded, 16)

            @block.scalar
            def _(act):
                act.wait_ge(lb_step, 1)
                nc.scalar.activation(lbw[:, 1], lbw[:, 1], ACT.Exp).then_inc(lb_act, 1)

            @block.vector
            def _(dve):
                link = Chain(dve, lb_step)
                dve.wait_ge(lb_loaded, 16)
                link(nc.vector.tensor_tensor(lbw[:, 1], lbw[:, 0], lbw[:, 0], ALU.subtract))
                dve.wait_ge(lb_act, 1)
                link(nc.vector.reciprocal(lbw[:, 2], lbw[:, 1]))
                link(nc.vector.tensor_tensor(lbw[:, 1], lbw[:, 1], lbw[:, 2], ALU.mult))
                link(nc.vector.tensor_tensor(lbw[:, 2], lbw[:, 1], lbw[:, 1], ALU.subtract))
                link(nc.vector.tensor_scalar(lbw[:, 3], lbw[:, 2], -1.0, 1.0, ALU.mult, ALU.add))

            @block.gpsimd
            def _(pool):
                pool.memset(reset[:], 1.0).then_inc(zeroed, 1)
                pool.wait_ge(zeroed, 1)
                pool.memset(per_chunk(reset[:])[:, :, 0:1], 0.0).then_inc(zeroed, 1)
                pool.memset(sc[:], 0.0).then_inc(zeroed, 1)
                pool.wait_ge(zeroed, 3)

        for d in range(2):
            f = s["f"][d]
            Q2 = f.rearrange("p h t -> p (h t)")
            rev = slice(None, None, -1) if d else slice(None)
            last_t, mid_t = (CHUNK - 1, CHUNK // 2 - 1) if d == 0 else (0, CHUNK // 2)
            tiles = [0, 1, 2, 3] if d == 0 else [1, 0, 3, 2]
            chunk_order = list(range(TILE_CH)) if d == 0 else list(range(TILE_CH))[::-1]
            marks = {}
            ff = f.rearrange("p h t -> p (h t)")
            halves = [slice(0, 2 * T), slice(2 * T, 4 * T)]

            def chunks(half):
                Ac = per_chunk(A[:, half])
                shape = [P, 2 * NCH, CHUNK]
                return Ac, Ac[:, :, mid_t:mid_t + 1].broadcast_to(shape), Ac[:, :, last_t:last_t + 1].broadcast_to(shape)

            prep, act_prep = new_sem(g, "hgrn_prep"), new_sem(g, "hgrn_act")
            with nc.Block() as block:
                @block.vector
                def _(dve):
                    link = Chain(dve, prep)
                    q = s["q"].rearrange("p h t -> p (h t)")
                    for half in halves:
                        for h in range(half.start // T, half.stop // T):
                            link(nc.vector.tensor_scalar(f[:, h], f[:, h], lbw[:, 3, h:h + 1], lbw[:, 2, h:h + 1], ALU.mult, ALU.add))
                        link(nc.vector.tensor_scalar(k[:, half], ff[:, half], -1.0, 1.0, ALU.mult, ALU.add))
                        link(nc.vector.tensor_scalar(ff[:, half], ff[:, half], TINY, None, ALU.max))
                        marks["floor", half.start] = link.n
                    for n, half in enumerate(halves):
                        dve.wait_ge(act_prep, n + 1)
                        for at in range(half.start, half.stop, T):
                            own = slice(at, at + T)
                            link(nc.vector.tensor_tensor_scan(A[:, own][:, rev], reset[:], E[:, own][:, rev], 0.0, ALU.mult, ALU.add))
                        marks["A", half.start] = link.n
                        Ac, mid, end = chunks(half)
                        link(nc.vector.tensor_tensor(per_chunk(D1[:, half]), Ac, mid, ALU.subtract))
                    for n, half in enumerate(halves):
                        dve.wait_ge(act_prep, 4 + 2 * n)
                        link(nc.vector.tensor_tensor(Q1[:, half], E[:, half], q[:, half], ALU.mult))
                        marks["Q1", half.start] = link.n
                    for n, half in enumerate(halves):
                        Ac, mid, end = chunks(half)
                        link(nc.vector.tensor_tensor(per_chunk(K1[:, half]), end, Ac, ALU.subtract))
                        marks["K1", half.start] = link.n
                    for n, half in enumerate(halves):
                        dve.wait_ge(act_prep, 7 + 2 * n)
                        link(nc.vector.tensor_tensor(Q2[:, half], E[:, half], q[:, half], ALU.mult))
                    for n, half in enumerate(halves):
                        dve.wait_ge(act_prep, 10)
                        link(nc.vector.tensor_tensor(D1[:, half], D1[:, half], k[:, half], ALU.mult))
                    for n, half in enumerate(halves):
                        dve.wait_ge(act_prep, 11 + n)
                        link(nc.vector.tensor_tensor(K1[:, half], K1[:, half], k[:, half], ALU.mult))

                @block.scalar
                def _(act):
                    for half in halves:
                        act.wait_ge(prep, marks["floor", half.start])
                        nc.scalar.activation(E[:, half], ff[:, half], ACT.Ln).then_inc(act_prep, 1)
                    for half in halves:
                        act.wait_ge(prep, marks["A", half.start])
                        ends = per_chunk(A[:, half])[:, :, last_t]
                        nc.scalar.activation(dend[:, half.start // CHUNK:half.stop // CHUNK], ends, ACT.Exp).then_inc(act_prep, 1)
                        nc.scalar.activation(E[:, half], A[:, half], ACT.Exp).then_inc(act_prep, 1)
                    for n, half in enumerate(halves):
                        act.wait_ge(prep, marks["Q1", half.start])
                        nc.scalar.activation(E[:, half], D1[:, half], ACT.Exp).then_inc(act_prep, 1)
                        act.wait_ge(act_prep, 7 + 2 * n)
                        nc.scalar.activation(D1[:, half], D1[:, half], ACT.Exp, scale=-1.0).then_inc(act_prep, 1)
                    for half in halves:
                        act.wait_ge(prep, marks["K1", half.start])
                        nc.scalar.activation(K1[:, half], K1[:, half], ACT.Exp).then_inc(act_prep, 1)

            (vmasked, turned, k1_ready, scored, masked, located, stated, out_ready, added) = (new_sem(g, x) for x in (
                "v_masked", "k1_turned", "k1_ready", "hgrn_scored", "hgrn_masked", "s_loc_ready", "state_ready",
                "hgrn_out_ready", "hgrn_added"))
            keep = g.tri_chunk[d]
            state_zeroed = new_sem(g, "state_zeroed")
            with nc.Block() as block:
                @block.tensor
                def _(pe):
                    def turn_keys(n):
                        i = tiles[n]
                        if n >= 1:
                            pe.wait_ge(k1_ready, n)
                        for h in range(HEADS):
                            at = h * T + i * P
                            last = nc.tensor.transpose(g.bank[0][:, h * P:(h + 1) * P], K1[:, at:at + P], g.ident)
                        last.then_inc(turned, 1)
                        if n >= 1:
                            pe.wait_ge(masked, n * HEADS)
                        for h in range(HEADS):
                            at = h * T + i * P
                            last = nc.tensor.matmul(g.bank[1][:, h * P:(h + 1) * P], D1[:, at:at + P], Q2[:, at:at + P],
                                                    start=True, stop=True)
                        last.then_inc(scored, 1)

                    def locate(n):
                        pe.wait_ge(k1_ready, n + 1)
                        pe.wait_ge(vmasked, n + 1)
                        if n >= 1:
                            pe.wait_ge(stated, HEADS * TILE_CH * n)
                        for h in range(HEADS):
                            nc.tensor.matmul(g.bank[2 + h][:], k1t[:, n % 2, h], vmask[:, n % 2, h], start=True, stop=True).then_inc(located, 1)

                    turn_keys(0)
                    locate(0)
                    for n, i in enumerate(tiles):
                        if n + 1 < len(tiles):
                            turn_keys(n + 1)
                            locate(n + 1)
                        if n >= 2:
                            pe.wait_ge(added, n - 1)
                        for h in range(HEADS):
                            pe.wait_ge(masked, n * HEADS + h + 1)
                            out = g.bank[6 + n % 2][:, h * P:(h + 1) * P]
                            nc.tensor.matmul(out, sc[:, d, n % 2, h], s["v"][:, i, h * P:(h + 1) * P], start=True, stop=False, skip_group_check=True)
                            for m, c in enumerate(chunk_order):
                                pe.wait_ge(stated, HEADS * (n * TILE_CH + m)) if n or m else pe.wait_ge(state_zeroed, 1)
                                at = h * T + i * P + c * CHUNK
                                last = nc.tensor.matmul(out[c * CHUNK:(c + 1) * CHUNK, :], Q1[:, at:at + CHUNK], state(h, n * TILE_CH + m),
                                                        start=False, stop=m == TILE_CH - 1, skip_group_check=True)
                        last.then_inc(out_ready, 1)

                @block.scalar
                def _(act):
                    for n, i in enumerate(tiles):
                        act.wait_ge(turned, n + 1)
                        if n >= 2:
                            act.wait_ge(located, HEADS * (n - 1))
                        nc.scalar.activation(k1t[:, n % 2], g.bank[0][:].rearrange("p (h t) -> p h t", h=HEADS), ACT.Copy).then_inc(k1_ready, 1)

                @block.gpsimd
                def _(pool):
                    for n, i in enumerate(tiles):
                        if n >= 2:
                            pool.wait_ge(located, HEADS * (n - 1))
                        for h in range(HEADS):
                            src = s["v"][:, i, h * P:(h + 1) * P].unsqueeze(1).broadcast_to([P, TILE_CH, P])
                            last = pool.tensor_tensor(vmask[:, n % 2, h].rearrange("p (c v) -> p c v", v=P), src,
                                                      g.chunk_of.unsqueeze(2).broadcast_to([P, TILE_CH, P]), ALU.mult)
                        last.then_inc(vmasked, 1)

                @block.vector
                def _(dve):
                    nc.vector.memset(st[:, :, 0], 0.0).then_inc(state_zeroed, 1)
                    dve.wait_ge(state_zeroed, 1)

                    def add(n):
                        i = tiles[n]
                        dve.wait_ge(out_ready, n + 1)
                        src = g.bank[6 + n % 2][:]
                        if d == 0:
                            nc.vector.tensor_copy(s["y"][:, i], src).then_inc(added, 1)
                        else:
                            nc.vector.tensor_tensor(s["y"][:, i], s["y"][:, i], src, ALU.add).then_inc(added, 1)

                    for n, i in enumerate(tiles):
                        dve.wait_ge(scored, n + 1)
                        for h in range(HEADS):
                            nc.vector.copy_predicated(sc[:, d, n % 2, h], keep.bitcast(U32), g.bank[1][:, h * P:(h + 1) * P]).then_inc(masked, 1)
                        for m, c in enumerate(chunk_order):
                            gc = n * TILE_CH + m
                            for h in range(HEADS):
                                if m == 0:
                                    dve.wait_ge(located, n * HEADS + h + 1)
                                if gc >= 1:
                                    dve.wait_ge(stated, HEADS * (gc - 1) + h + 1)
                                at = h * NCH + i * TILE_CH + c
                                nc.vector.scalar_tensor_tensor(state(h, gc + 1), state(h, gc), dend[:, at:at + 1],
                                                               g.bank[2 + h][:, c * P:(c + 1) * P], ALU.mult, ALU.add).then_inc(stated, 1)
                        if n:
                            add(n - 1)
                    add(len(tiles) - 1)


def residual_stage(g, l, which, tiles, w_out=None, experts=None):
    nc = g.nc
    nt = len(tiles)
    (ln_loaded, produced, step, rooted, added, diag_made, rows_used) = (new_sem(g, x) for x in (
        "ln_loaded", "y_produced", "ln_step", "ln_root", "y_added", "diag_made", "y_rows_used"))
    tag = f"{l}{which}"
    RING, BY_PE = 16, 4
    BY_DVE = TOPK - BY_PE
    with ExitStack() as ctx:
        if experts:
            r, y_dram, acc = experts
            fetched = [new_sem(g, f"y_fetched{s}") for s in range(RING)]
            rows = y_dram.rearrange("b p d -> (b p) d")
            room = r["w"][:].rearrange("p s c -> p (s c)")
            ring = room[:, 0:RING * D].rearrange("p (u d) -> p u d", d=D)
            diag = room[:, RING * D:RING * D + nt * BY_PE * P].rearrange("p (u c) -> p u c", c=P)
        ln = ctx.enter_context(nc.sbuf_tensor(f"ln{tag}", [P, 2, D], F32))
        z = ctx.enter_context(nc.sbuf_tensor(f"ln_z{tag}", [P, 2, D], F32))
        stats = ctx.enter_context(nc.sbuf_tensor(f"ln_stats{tag}", [P, 2, 2, 6], F32))
        mv = ctx.enter_context(nc.sbuf_tensor(f"ln_mv{tag}", [P, 4, 4], F32))
        marks = {}
        with nc.Block() as block:
            @block.sync
            def _(sp):
                sp.dma_start(ln[:], g.dram["ln_rows"][l, which]).then_inc(ln_loaded, 16)

            if experts:
                @block.gpsimd
                def _(pool):
                    for u in range(nt * TOPK):
                        if u >= RING:
                            n, k = (u - RING) // TOPK, (u - RING) % TOPK
                            if k < BY_PE:
                                pool.wait_ge(rows_used, n * BY_PE + k + 1)
                            else:
                                pool.wait_ge(added, n * BY_DVE + k - BY_PE + 1)
                        pool.indirect_dma_start(ring[:, u % RING], None, rows,
                                                bass.IndirectOffsetOnAxis(ap=r["y_row"][:, u // TOPK, u % TOPK:u % TOPK + 1], axis=0)).then_inc(fetched[u % RING], 16)

                @block.tensor
                def _(pe):
                    for n in range(nt):
                        for k in range(BY_PE):
                            u = n * TOPK + k
                            pe.wait_ge(fetched[u % RING], 16 * (u // RING + 1))
                            pe.wait_ge(diag_made, n * BY_PE + k + 1)
                            for half in range(2):
                                last = nc.tensor.matmul(g.bank[2 * n + half][:], diag[:, n * BY_PE + k], ring[:, u % RING, half * 512:(half + 1) * 512],
                                                        start=k == 0, stop=k == BY_PE - 1)
                            last.then_inc(rows_used, 1)

            if w_out is not None:
                w = w_out.tile

                @block.tensor
                def _(pe):
                    pe.wait_ge(w_out.loaded, 16)
                    for n, i in enumerate(tiles):
                        for half in range(2):
                            u = 2 * n + half
                            for k in range(KT):
                                last = nc.tensor.matmul(g.bank[u % 8][:], g.mix[:, k, i * P:(i + 1) * P], w[:, k, half * 512:(half + 1) * 512],
                                                        start=k == 0, stop=k == KT - 1)
                            last.then_inc(produced, 1)

            @block.vector
            def _(dve):
                link = Chain(dve, step)
                for n, i in enumerate(tiles):
                    v = 1 if i < 2 else 0
                    zz = z[:, n % 2]
                    if experts:
                        for k in range(BY_PE, TOPK):
                            u = n * TOPK + k
                            dve.wait_ge(fetched[u % RING], 16 * (u // RING + 1))
                            if k > BY_PE:
                                dve.wait_ge(added, n * BY_DVE + k - BY_PE)
                            nc.vector.scalar_tensor_tensor(acc[:, n], ring[:, u % RING], r["gate"][:, n, u % TOPK:u % TOPK + 1], acc[:, n],
                                                           ALU.mult, ALU.add).then_inc(added, 1)
                        dve.wait_ge(added, (n + 1) * BY_DVE)
                        dve.wait_ge(rows_used, (n + 1) * BY_PE)
                    for half in range(2):
                        cols = slice(half * 512, (half + 1) * 512)
                        y = g.bank[2 * n + half][:]
                        if w_out is not None:
                            dve.wait_ge(produced, 2 * n + half + 1)
                            link(nc.vector.tensor_tensor(zz[:, cols], y, g.mod_row[:, v, cols], ALU.mult))
                        else:
                            link(nc.vector.tensor_tensor(zz[:, cols], y, acc[:, n, cols], ALU.add))
                    if experts:
                        link(nc.vector.tensor_tensor(zz, zz, g.mod_row[:, v], ALU.mult))
                    link(nc.vector.scalar_tensor_tensor(zz, g.h[:, i], ALPHA, zz, ALU.mult, ALU.add))
                    for half in range(2):
                        link(nc.vector.bn_stats(stats[:, n % 2, half], zz[:, half * 512:(half + 1) * 512]))
                    link(nc.vector.bn_aggr(mv[:, n, 0:2], stats[:, n % 2]))
                    link(nc.vector.tensor_scalar(mv[:, n, 2:3], mv[:, n, 1:2], EPS, None, ALU.add))
                    marks[n] = link.n
                    dve.wait_ge(rooted, n + 1)
                    link(nc.vector.reciprocal(mv[:, n, 2:3], mv[:, n, 3:4]))
                    link(nc.vector.tensor_scalar(zz, zz, mv[:, n, 0:1], mv[:, n, 2:3], ALU.subtract, ALU.mult))
                    if n == 0:
                        dve.wait_ge(ln_loaded, 16)
                    link(nc.vector.tensor_tensor(zz, zz, ln[:, 0], ALU.mult))
                    link(nc.vector.tensor_tensor(g.h[:, i], zz, ln[:, 1], ALU.add))

            @block.scalar
            def _(act):
                if experts:
                    for n in range(nt):
                        for k in range(BY_PE):
                            nc.scalar.activation(diag[:, n * BY_PE + k], g.ident, ACT.Copy, scale=r["gate"][:, n, k:k + 1]).then_inc(diag_made, 1)
                for n, i in enumerate(tiles):
                    act.wait_ge(step, marks[n])
                    nc.scalar.activation(mv[:, n, 3:4], mv[:, n, 2:3], ACT.Sqrt).then_inc(rooted, 1)


def moe_input_stage(g, l, tiles, v_dram):
    nc = g.nc
    nt = len(tiles)
    streams = [0, 1] if tiles[0] == 0 else [0]
    (row_made, row_copied, stepped, shifted, stored, turned, copied) = (new_sem(g, x) for x in (
        "row_made", "row_copied", "v_step", "v_ready", "v_stored", "v_turned", "v_copied"))
    mods = g.mods[:, l]
    rows = [(which, v, half) for v in streams for which in (4, 3, 5) for half in range(2)]
    with ExitStack() as ctx:
        vrow = ctx.enter_context(nc.sbuf_tensor(f"v_row{l}", [P, 2, 2, D], F32))
        vt = ctx.enter_context(nc.sbuf_tensor(f"v_tok{l}", [P, nt, D], F32))

        def row_tile(which, v):
            return g.mod_row[:, v] if which == 5 else vrow[:, which - 3, v]

        with nc.Block() as block:
            @block.tensor
            def _(pe):
                for n, (which, v, half) in enumerate(rows):
                    if n >= 4:
                        pe.wait_ge(row_copied, n - 3)
                    for j in range(4):
                        col = mods[:, which * KT + 4 * half + j, v:v + 1].broadcast_to([P, P])
                        last = nc.tensor.matmul(g.bank[n % 4][:, j * P:(j + 1) * P], col, g.ident, start=True, stop=True)
                    last.then_inc(row_made, 1)
                for n in range(nt):
                    pe.wait_ge(shifted, n + 1)
                    for half in range(2):
                        u = 2 * n + half
                        if u >= 4:
                            pe.wait_ge(copied, u - 3)
                        for j in range(4):
                            k = 4 * half + j
                            last = nc.tensor.transpose(g.bank[4 + u % 4][:, j * P:(j + 1) * P], vt[:, n, k * P:(k + 1) * P], g.ident)
                        last.then_inc(turned, 1)

            @block.scalar
            def _(act):
                for n, (which, v, half) in enumerate(rows):
                    act.wait_ge(row_made, n + 1)
                    nc.scalar.activation(row_tile(which, v)[:, half * 512:(half + 1) * 512], g.bank[n % 4][:], ACT.Copy).then_inc(row_copied, 1)
                for u in range(2 * nt):
                    n, half = u // 2, u % 2
                    act.wait_ge(turned, u + 1)
                    nc.scalar.activation(g.xt[:, 4 * half:4 * half + 4, tiles[n] * P:(tiles[n] + 1) * P],
                                         g.bank[4 + u % 4][:].rearrange("p (k t) -> p k t", k=4), ACT.Copy).then_inc(copied, 1)

            @block.vector
            def _(dve):
                link = Chain(dve, stepped)
                for n, i in enumerate(tiles):
                    v = 1 if i < 2 else 0
                    dve.wait_ge(row_copied, 6 * streams.index(v) + 4)
                    link(nc.vector.tensor_tensor(vt[:, n], g.h[:, i], vrow[:, 1, v], ALU.mult))
                    nc.vector.tensor_tensor(vt[:, n], vt[:, n], vrow[:, 0, v], ALU.add).then_inc(shifted, 1)

            @block.sync
            def _(sp):
                for n in range(nt):
                    sp.wait_ge(shifted, n + 1)
                    sp.dma_start(v_dram.rearrange("(n p) d -> n p d", p=P)[n], vt[:, n]).then_inc(stored, 16)
                sp.wait_ge(stored, 16 * nt)


def routing_stage(g, l, tiles, r, acc):
    nc = g.nc
    nt = len(tiles)
    NB = r["max_blocks"] + 2
    (loaded, scored, squashed, step, ranked, filled, scattered, idx_loaded, tok_ready) = (new_sem(g, x) for x in (
        "router_loaded", "router_scored", "router_sigmoid", "router_step", "ranks_ready", "slots_filled",
        "slots_scattered", "idx_loaded", "tok_ready"))
    sh_loaded, sh_up_ready, sh_silu_ready, sh_hidden_ready, sh_y_ready, sh_copied = (new_sem(g, x) for x in (
        "shared_loaded", "sh_up_ready", "sh_silu_ready", "sh_hidden_ready", "sh_y_ready", "sh_copied"))
    marks = {}
    experts = g.dram["experts"][l * (EXPERTS + 1):(l + 1) * (EXPERTS + 1)]
    shared = r["w"][:, SLOTS - 1]
    sh_up = shared[:, 0:W13].rearrange("p (k m a c) -> p k m a c", k=KT, m=2, a=2)
    sh_down = shared[:, W13:WEXP].rearrange("p (m c) -> p m c", m=2)
    a0, n_tok = tiles[0] * P, nt * P
    with ExitStack() as ctx:
        sb = lambda n, shape, dt=F32: ctx.enter_context(nc.sbuf_tensor(f"router_{n}{l}", shape, dt))
        rw, rb = sb("w", [P, KT, EXPERTS]), sb("b", [P, EXPERTS])
        sig, pick, mask, posn, inblk, blk = (sb(n, [P, nt, EXPERTS]) for n in ("sig", "pick", "mask", "posn", "inblk", "blk"))
        top, tot = sb("top", [P, nt, TOPK]), sb("tot", [P, nt, 2])
        chosen = sb("chosen", [P, nt, TOPK], U32)
        chosen_f = sb("chosen_f", [P, nt, TOPK])
        onehot, prod = sb("onehot", [P, nt, TOPK, EXPERTS]), sb("prod", [P, TOPK, EXPERTS])
        picked = sb("picked", [P, 2, nt, TOPK])
        addr = sb("addr", [P, nt, TOPK], U32)
        tok = sb("tok", [P, nt], U32)
        skip = sb("skip", [P, NB // 2], U32)
        half = sb("half", [P, 1])
        nblk, incl, start, cnt = (sb(n, [P, EXPERTS]) for n in ("nblk", "incl", "start", "cnt"))
        silu, hidden = sb("sh_silu", [P, 2, n_tok]), sb("sh_hidden", [P, 2, n_tok])
        odd, ecol = sb("odd", [P, EXPERTS]), sb("ecol", [P, 2])
        with nc.Block() as block:
            @block.sync
            def _(sp):
                sp.dma_start(rw[:], g.dram["router_w"][l]).then_inc(loaded, 16)
                sp.dma_start(rb[:], g.dram["router_b"][l]).then_inc(loaded, 16)
                sp.dma_start(shared, experts[0]).then_inc(sh_loaded, 16)
                for s in range(SLOTS - 1):
                    sp.dma_start(r["w"][:, s], experts[1 + s]).then_inc(r["expert_loaded"][s], 16)
                sp.wait_ge(tok_ready, 1)
                sp.dma_start(r["slot_dram"].rearrange("(p b) a -> p (b a)", p=P), skip[:]).then_inc(filled, 16)
                sp.wait_ge(scattered, 16 * nt * TOPK)
                for h in range(2):
                    sp.dma_start(r["idx_all"][SB * h:SB * (h + 1)], r["slot_dram"].rearrange("(s b) a -> s (b a)", s=SB)).then_inc(idx_loaded, 16)

            @block.vector
            def _(dve):
                link = Chain(dve, step)
                nc.vector.memset(skip[:], SKIP).then_inc(tok_ready, 1)
                dve.wait_ge(loaded, 32)
                for n in range(nt):
                    link(nc.vector.tensor_scalar(tok[:, n:n + 1], g.pcol, float(n * P), None, ALU.add))
                for n in range(nt):
                    dve.wait_ge(squashed, n + 1)
                    link(nc.vector.tensor_tensor(pick[:, n], sig[:, n], rb[:], ALU.add))
                    link(nc.vector.max(top[:, n], pick[:, n]))
                    link(nc.vector.max_index(chosen[:, n], top[:, n], pick[:, n]))
                    link(nc.vector.match_replace(mask[:, n], top[:, n], pick[:, n], NEG_BIG))
                    link(nc.vector.tensor_tensor(mask[:, n], mask[:, n], pick[:, n], ALU.not_equal))
                marks["mask"] = link.n
                for n in range(nt):
                    link(nc.vector.tensor_copy(chosen_f[:, n], chosen[:, n]))
                    link(nc.vector.tensor_tensor(onehot[:, n], g.iota_e.unsqueeze(1).broadcast_to([P, TOPK, EXPERTS]),
                                                 chosen_f[:, n].unsqueeze(2).broadcast_to([P, TOPK, EXPERTS]), ALU.is_equal))
                dve.wait_ge(ranked, 1)
                link(nc.vector.tensor_copy(cnt[:], g.bank[7][:, 0:EXPERTS]))
                for j in range(1, 2 * nt):
                    link(nc.vector.scalar_tensor_tensor(nblk[:], cnt[:], j * SB + 0.5, nblk[:] if j > 1 else g.ones[:, 0:EXPERTS], ALU.is_gt, ALU.add))
                link(nc.vector.tensor_tensor_scan(incl[:], g.ones[:, 0:EXPERTS], nblk[:], 0.0, ALU.mult, ALU.add))
                link(nc.vector.tensor_tensor(start[:], incl[:], nblk[:], ALU.subtract))
                link(nc.vector.tensor_scalar(odd[:], g.iota_e, 2.0, None, ALU.mult))
                link(nc.vector.tensor_scalar(odd[:], odd[:], incl[:, EXPERTS - 1:EXPERTS], None, ALU.is_lt))
                link(nc.vector.tensor_reduce(ecol[:, 0:1], odd[:], AX.X, ALU.add))
                link(nc.vector.tensor_scalar(ecol[:, 1:2], ecol[:, 0:1], -float(MIN_PAIRS), None, ALU.add))
                link(nc.vector.tensor_scalar(incl[:, EXPERTS - 1:EXPERTS], ecol[:, 0:1], 2.0, None, ALU.mult))
                link(nc.vector.tensor_copy(r["pairs"][:], ecol[0:1, 1:2]))
                link(nc.vector.tensor_scalar(odd[:], start[:], -1.0, None, ALU.add))
                link(nc.vector.tensor_copy(r["befores"][:], odd[0:1, :]))
                link(nc.vector.tensor_scalar(odd[:], incl[:], -1.0, None, ALU.add))
                link(nc.vector.tensor_copy(r["lasts"][:], odd[0:1, :]))
                link(nc.vector.tensor_copy(r["ends"][:], incl[0:1, :]))
                for n in range(nt):
                    link(nc.vector.tensor_scalar(posn[:, n], g.bank[3 + n][:, 0:EXPERTS], -1.0, None, ALU.add))
                marks["ranks_taken"] = link.n
                whole = lambda t: t[:].rearrange("p n e -> p (n e)")
                link(nc.vector.tensor_scalar(whole(blk), whole(posn), SB - 0.5, None, ALU.is_gt))
                for j in range(2, 2 * nt):
                    link(nc.vector.scalar_tensor_tensor(whole(blk), whole(posn), j * SB - 0.5, whole(blk), ALU.is_gt, ALU.add))
                link(nc.vector.scalar_tensor_tensor(whole(inblk), whole(blk), -float(SB), whole(posn), ALU.mult, ALU.add))
                link(nc.vector.tensor_tensor(blk[:], blk[:], start[:].unsqueeze(1).broadcast_to([P, nt, EXPERTS]), ALU.add))
                link(nc.vector.scalar_tensor_tensor(whole(posn), whole(blk), float(SB), whole(inblk), ALU.mult, ALU.add))
                link(nc.vector.scalar_tensor_tensor(whole(inblk), whole(inblk), float(NB), whole(blk), ALU.mult, ALU.add))
                for n in range(nt):
                    pos = posn[:, n]
                    for c, src in enumerate((pos, inblk[:, n])):
                        link(nc.vector.tensor_tensor(prod[:], onehot[:, n], src.unsqueeze(1).broadcast_to([P, TOPK, EXPERTS]), ALU.mult))
                        link(nc.vector.tensor_reduce(picked[:, c, n], prod[:], AX.X, ALU.add))
                    link(nc.vector.tensor_copy(r["y_row"][:, n], picked[:, 0, n]))
                    link(nc.vector.tensor_copy(addr[:, n], picked[:, 1, n]))
                    marks["addr", n] = link.n
                for n in range(nt):
                    link(nc.vector.tensor_tensor(prod[:], onehot[:, n], sig[:, n].unsqueeze(1).broadcast_to([P, TOPK, EXPERTS]), ALU.mult))
                    link(nc.vector.tensor_reduce(r["gate"][:, n], prod[:], AX.X, ALU.add))
                    link(nc.vector.tensor_reduce(tot[:, n, 0:1], r["gate"][:, n], AX.X, ALU.add))
                    link(nc.vector.reciprocal(tot[:, n, 1:2], tot[:, n, 0:1]))
                    link(nc.vector.tensor_scalar(r["gate"][:, n], r["gate"][:, n], tot[:, n, 1:2], ROUTED_SCALE, ALU.mult, ALU.mult))
                for m in range(2):
                    dve.wait_ge(sh_silu_ready, m + 1)
                    nc.vector.tensor_tensor(hidden[:, m], silu[:, m], g.bank[2 * m + 1][:, 0:n_tok], ALU.mult).then_inc(sh_hidden_ready, 1)
                link(nc.vector.tensor_scalar(half[:], g.pcol, SB - 0.5, None, ALU.is_gt))
                dve.wait_ge(idx_loaded, 32)
                link(nc.vector.tensor_scalar(r["idx_all"][:], r["idx_all"][:], 2.0, half[:], ALU.mult, ALU.add))

            @block.tensor
            def _(pe):
                pe.wait_ge(loaded, 32)
                for n, i in enumerate(tiles):
                    for k in range(KT):
                        last = nc.tensor.matmul(g.bank[n % 3][:, 0:EXPERTS] if n < 3 else g.bank[7][:, 0:EXPERTS],
                                                g.xt[:, k, i * P:(i + 1) * P], rw[:, k], start=k == 0, stop=k == KT - 1)
                    last.then_inc(scored, 1)
                pe.wait_ge(step, marks["mask"])
                for n in range(nt):
                    for m in range(n + 1):
                        nc.tensor.matmul(g.bank[3 + n][:, 0:EXPERTS], g.upper if m == n else g.ones, mask[:, m],
                                         start=m == 0, stop=m == n)
                for m in range(nt):
                    last = nc.tensor.matmul(g.bank[7][:, 0:EXPERTS], g.ones, mask[:, m], start=m == 0, stop=m == nt - 1)
                last.then_inc(ranked, 1)
                pe.wait_ge(step, marks["ranks_taken"])
                pe.wait_ge(sh_loaded, 16)
                for m in range(2):
                    for a in range(2):
                        for k in range(KT):
                            last = nc.tensor.matmul(g.bank[2 * m + a][:, 0:n_tok], sh_up[:, k, m, a], g.xt[:, k, a0:a0 + n_tok],
                                                    start=k == 0, stop=k == KT - 1)
                    last.then_inc(sh_up_ready, 1)
                pe.wait_ge(sh_hidden_ready, 2)
                for u in range(2 * nt):
                    if u >= 4:
                        pe.wait_ge(sh_copied, u - 3)
                    for m in range(2):
                        last = nc.tensor.matmul(g.bank[4 + u % 4][:], hidden[:, m, (u // 2) * P:(u // 2 + 1) * P],
                                                sh_down[:, m, (u % 2) * 512:(u % 2 + 1) * 512], start=m == 0, stop=m == 1)
                    last.then_inc(sh_y_ready, 1)

            @block.scalar
            def _(act):
                for n in range(nt):
                    act.wait_ge(scored, n + 1)
                    nc.scalar.activation(sig[:, n], (g.bank[n % 3] if n < 3 else g.bank[7])[:, 0:EXPERTS], ACT.Sigmoid).then_inc(squashed, 1)
                for m in range(2):
                    act.wait_ge(sh_up_ready, m + 1)
                    nc.scalar.activation(silu[:, m], g.bank[2 * m][:, 0:n_tok], ACT.Silu).then_inc(sh_silu_ready, 1)
                for u in range(2 * nt):
                    act.wait_ge(sh_y_ready, u + 1)
                    nc.scalar.activation(acc[:, u // 2, (u % 2) * 512:(u % 2 + 1) * 512], g.bank[4 + u % 4][:], ACT.Copy).then_inc(sh_copied, 1)
                act.dma_start(shared, experts[SLOTS]).then_inc(r["expert_loaded"][SLOTS - 1], 16)

            @block.gpsimd
            def _(pool):
                pool.wait_ge(filled, 16)
                for n in range(nt):
                    pool.wait_ge(step, marks["addr", n])
                    for k in range(TOPK):
                        pool.indirect_dma_start(r["slot_dram"], bass.IndirectOffsetOnAxis(ap=addr[:, n, k:k + 1], axis=0),
                                                tok[:, n:n + 1], None).then_inc(scattered, 16)


def blocks_stage(g, l, n_tok, r, v_dram, y_dram):
    nc = g.nc
    (idx_ready, x_ready, turned, xt_ready, up_done, silu_done, hidden_done, hid_turned, hid_ready, y_done, y_ready) = (new_sem(g, x) for x in (
        "idx_ready", "x_ready", "x_turned", "xt_ready", "up_done", "silu_done", "hidden_done", "hid_turned", "hid_ready", "y_done", "y_ready"))
    gathered, stored = ([new_sem(g, f"{x}{q}") for q in range(2)] for x in ("gathered", "stored"))
    loaded, w = r["expert_loaded"], r["w"]
    x_zeroed, gathers_sent, stores_sent, all_stored, loads_sent, loads_met = (new_sem(g, x) for x in (
        "x_zeroed", "gathers_sent", "stores_sent", "all_stored", "loads_sent", "loads_met"))
    experts = g.dram["experts"][l * (EXPERTS + 1) + 1:(l + 1) * (EXPERTS + 1)]
    v_halves = v_dram.rearrange("t (h d) -> (t h) d", h=2)
    y_halves = y_dram.rearrange("b s (h d) -> b h s d", h=2)
    with ExitStack() as ctx:
        sb = lambda n, shape, dt=F32: ctx.enter_context(nc.sbuf_tensor(f"blk_{n}{l}", shape, dt))
        came, x, xT = sb("came", [P, 2, D // 2]), sb("x", [P, D // 2]), sb("xT", [P, KT // 2, P])
        silu, hidden, hT = sb("silu", [P, P]), sb("hidden", [P, P]), sb("hT", [P, P])
        y = sb("y", [P, 2, D // 2])
        idx = [sb(f"idx{q}", [P, 1], U32) for q in range(2)]

        def all_pairs(eng):
            return eng.value_load(r["pairs"][0:1, 0:1], min_val=0, max_val=r["max_blocks"] // 2 - MIN_PAIRS) + MIN_PAIRS

        with nc.Block() as block:
            @block.sync
            def _(sp):
                def load(e, s):
                    sp.dma_start(w[:, s], experts[e]).then_inc(loaded[s], 16)

                with sp.Fori(1, EXPERTS // SLOTS) as turn:
                    for s in range(SLOTS):
                        e = turn * SLOTS + s
                        sp.wait_ge(loaded[(s - 2) % SLOTS], 16 * (turn if s < 2 else turn + 1))
                        sp.sem_inc(loads_sent, 1)
                        end = sp.value_load(r["ends"][0:1, bass.ds(e - SLOTS, 1)], min_val=0, max_val=r["max_blocks"])
                        sp.wait_ge(y_done, end)
                        sp.sem_inc(loads_sent, 1)
                        load(e, s)

            @block.gpsimd
            def _(pool):
                def gather(b, q):
                    pool.tensor_copy(idx[q][:], r["idx_all"][:, bass.ds(b, 1)]).then_inc(idx_ready, 1)
                    pool.wait_ge(idx_ready, b + 1)
                    pool.sem_inc(gathers_sent, 1)
                    pool.indirect_dma_start(came[:, q], None, v_halves, bass.IndirectOffsetOnAxis(ap=idx[q][:], axis=0),
                                            bounds_check=2 * n_tok - 1, oob_is_err=False).then_inc(gathered[q], 16)

                def take(p, q):
                    b = 2 * p + q
                    pool.wait_ge(gathered[q], 16 * (p + 1))
                    pool.wait_ge(turned, b)
                    pool.sem_inc(gathers_sent, 1)
                    pool.tensor_copy(x[:], came[:, q]).then_inc(x_ready, 1)
                    pool.wait_ge(x_ready, b + 1)

                pool.memset(came[:], 0.0).then_inc(x_zeroed, 1)
                pool.wait_ge(x_zeroed, 1)
                pairs = all_pairs(pool)
                for q in range(2):
                    gather(q, q)
                with pool.Fori(1, pairs + 1) as p:
                    for q in range(2):
                        take(p - 1, q)
                        gather(2 * p + q, q)
                for q in range(2):
                    take(pairs, q)
                pool.sem_inc(gathers_sent, 1)

            @block.tensor
            def _(pe):
                def turn_x(b):
                    pe.wait_ge(x_ready, b + 1)
                    for c in range(KT // 2):
                        last = nc.tensor.transpose(g.bank[0][:, c * P:(c + 1) * P], x[:, c * P:(c + 1) * P], g.ident)
                    last.then_inc(turned, 1)

                def turn_hidden(b):
                    pe.wait_ge(hidden_done, b + 1)
                    nc.tensor.transpose(g.bank[2][:, 0:P], hidden[:], g.ident).then_inc(hid_turned, 1)

                def up_project(b, s):
                    pe.wait_ge(xt_ready, b + 1)
                    for k in range(KT):
                        c, half = k % 4, k // 4
                        for h in range(2):
                            last = nc.tensor.matmul(g.bank[1][64 * h:64 * h + 64, 0:HID], xT[:, c, 64 * half:64 * half + 64],
                                                    w[:, s, (2 * k + h) * HID:(2 * k + h + 1) * HID], start=k == 0, stop=k == KT - 1)
                    last.then_inc(up_done, 1)

                def down_project(b, s):
                    pe.wait_ge(hid_ready, b + 1)
                    pe.wait_ge(y_ready, b)
                    for m in range(2):
                        for h in range(2):
                            at = W13 + m * D + h * 512
                            last = nc.tensor.matmul(g.bank[3][64 * h:64 * h + 64, :], hT[:, 64 * m:64 * m + 64],
                                                    w[:, s, at:at + 512], start=m == 0, stop=m == 1)
                    last.then_inc(y_done, 1)

                def turn(before, s, s_before):
                    turn_hidden(before)
                    up_project(before + 1, s)
                    turn_x(before + 2)
                    down_project(before, s_before)

                def expert(turns, s):
                    e = turns * SLOTS + s
                    before = pe.value_load(r["befores"][0:1, bass.ds(e, 1)], min_val=0, max_val=r["max_blocks"])
                    last = pe.value_load(r["lasts"][0:1, bass.ds(e, 1)], min_val=0, max_val=r["max_blocks"])
                    pe.wait_ge(loaded[s], 16 * (turns + 1))
                    pe.sem_inc(loads_met, 1)
                    turn(before, s, (s - 1) % SLOTS)
                    rest(before + 1, last, s)

                def rest(first, last, s):
                    with pe.If(first < last):
                        with pe.Fori(first, last) as before:
                            turn(before, s, s)

                turn_x(0)
                pe.wait_ge(loaded[0], 16)
                up_project(0, 0)
                turn_x(1)
                rest(0, pe.value_load(r["lasts"][0:1, 0:1], min_val=0, max_val=r["max_blocks"]), 0)
                for s in range(1, SLOTS):
                    expert(0, s)
                with pe.Fori(1, EXPERTS // SLOTS) as turns:
                    for s in range(SLOTS):
                        expert(turns, s)
                final = pe.value_load(r["lasts"][0:1, EXPERTS - 1:EXPERTS], min_val=0, max_val=r["max_blocks"])
                turn_hidden(final)
                down_project(final, SLOTS - 1)

            @block.scalar
            def _(act):
                def copy_x(b):
                    act.wait_ge(turned, b + 1)
                    nc.scalar.activation(xT[:], g.bank[0][:].rearrange("p (k t) -> p k t", k=4), ACT.Copy).then_inc(xt_ready, 1)

                def squash(b):
                    act.wait_ge(up_done, b + 1)
                    act.wait_ge(hidden_done, b)
                    nc.scalar.activation(silu[:], g.bank[1][:, 0:P], ACT.Silu).then_inc(silu_done, 1)
                    copy_x(b + 1)

                def store(p, q):
                    act.wait_ge(y_ready, 2 * p + q + 1)
                    act.sem_inc(stores_sent, 1)
                    act.dma_start(y_halves[2 * p + q], y[:, q]).then_inc(stored[q], 16)

                act.wait_ge(g.y_cleared, 16 * CLEARS)
                copy_x(0)
                pairs = all_pairs(act)
                squash(0)
                squash(1)
                store(0, 0)
                with act.Fori(1, pairs) as p:
                    squash(2 * p)
                    store(p - 1, 1)
                    squash(2 * p + 1)
                    store(p, 0)
                store(pairs - 1, 1)
                for q in range(2):
                    act.wait_ge(stored[q], 16 * pairs)
                act.sem_inc(all_stored, 1)

            @block.vector
            def _(dve):
                def gate(b):
                    dve.wait_ge(silu_done, b + 1)
                    dve.wait_ge(hid_turned, b)
                    nc.vector.tensor_tensor(hidden[:], silu[:], g.bank[1][:, P:2 * P], ALU.mult).then_inc(hidden_done, 1)

                def copy_hidden(b):
                    dve.wait_ge(hid_turned, b + 1)
                    dve.wait_ge(y_done, b)
                    nc.vector.tensor_copy(hT[:], g.bank[2][:, 0:P]).then_inc(hid_ready, 1)

                def copy_y(p, q):
                    dve.wait_ge(y_done, 2 * p + q + 1)
                    dve.wait_ge(stored[q], 16 * p)
                    nc.vector.tensor_copy(y[:, q], g.bank[3][:]).then_inc(y_ready, 1)

                def turn(b, p, q):
                    copy_hidden(b - 1)
                    gate(b)
                    copy_y(p, q)

                pairs = all_pairs(dve)
                gate(0)
                turn(1, 0, 0)
                with dve.Fori(1, pairs) as p:
                    turn(2 * p, p - 1, 1)
                    turn(2 * p + 1, p, 0)
                copy_hidden(2 * pairs - 1)
                copy_y(pairs - 1, 1)


def moe(g, l, tiles):
    nc = g.nc
    nt = len(tiles)
    n_tok = nt * P
    max_blocks = most_blocks(n_tok)
    v_dram = nc.dram_tensor(f"v_tokens{l}", (n_tok, D), F32, kind="Internal").ap()
    slot_dram = nc.dram_tensor(f"slot_tokens{l}", (SB * (max_blocks + 2), 1), U32, kind="Internal").ap()
    y_dram = g.y_dram[0:max_blocks]
    moe_input_stage(g, l, tiles, v_dram)
    with ExitStack() as ctx:
        sb = lambda n, shape, dt=F32: ctx.enter_context(nc.sbuf_tensor(f"moe_{n}{l}", shape, dt))
        acc = sb("acc", [P, nt, D])
        r = {"max_blocks": max_blocks, "slot_dram": slot_dram, "gate": sb("gate", [P, nt, TOPK]),
             "y_row": sb("y_row", [P, nt, TOPK], U32), "idx_all": sb("idx_all", [P, max_blocks + 2], U32),
             "pairs": sb("pairs", [1, 1], mybir.dt.int32), "befores": sb("befores", [1, EXPERTS], mybir.dt.int32), "lasts": sb("lasts", [1, EXPERTS], mybir.dt.int32),
             "ends": sb("ends", [1, EXPERTS], mybir.dt.int32), "w": sb("w", [P, SLOTS, WEXP]),
             "expert_loaded": [new_sem(g, f"expert_loaded{s}") for s in range(SLOTS)]}
        routing_stage(g, l, tiles, r, acc[:])
        blocks_stage(g, l, n_tok, r, v_dram, y_dram)
        residual_stage(g, l, 1, tiles, experts=(r, y_dram, acc[:]))


def even_layer(g):
    nc = g.nc
    ada_columns_stage(g, 0)
    with ExitStack() as ctx:
        g.mix = ctx.enter_context(nc.sbuf_tensor("mix0", [P, KT, T], F32))
        with ExitStack() as c2:
            sb = lambda n, shape: c2.enter_context(nc.sbuf_tensor(n, shape, F32))
            qT, kT = sb("m_qT", [P, 2, T]), sb("m_kT", [P, 2, T])
            v1, o, y = sb("m_v1", [P, NT, HEADS, P + 1]), sb("m_o", [P, NT, 512]), sb("m_y", [P, NT, 512])
            s = {"qT": qT, "kT": kT, "v1": v1, "y": y, "a_col": sb("a_col", [P, 2, NT * HEADS]),
                 "floor_col": sb("floor_col", [P, 2, NT * HEADS]), "max_row": sb("max_row", [HEADS, 2, T])}
            ones = new_sem(g, "v_ones")
            with nc.Block() as block:
                @block.gpsimd
                def _(pool):
                    pool.memset(v1[:, :, :, P:P + 1], 1.0).then_inc(ones, 1)
                    pool.wait_ge(ones, 1)
            allt = list(range(NT))
            with ExitStack() as c3:
                w_in = InputWeights(g, c3, g.dram["even_w_in"], [0, 1, 2])
                modulate_stage(g, 0, 0, 1, allt, 2, w_in)
                projection_stage(g, g.dram["even_w_in"], [
                    (0, "T", allt, lambda j: (qT if j < 2 else kT)[:, j % 2], "q_scale"),
                    (1, "N", allt, lambda j: v1[:, j, :, 0:P], "heads"),
                    (2, "N", allt, lambda j: o[:, j], "sigmoid")], prefetched=w_in)
            gates_wrapped(g, s)
            mlstm_stage(g, s)
            norm_stage(g, y[:], allt, HEADS, True, o[:], "mlstm_norm_w", 0, "m")
        w_out = Prefetch(g, ctx, "w_out0", [P, KT, D], g.dram["even_w_out"])
        work = w_out.tile[:].rearrange("p k d -> p (k d)")
        with ExitStack() as c2:
            sb = lambda n, shape: c2.enter_context(nc.sbuf_tensor(n, shape, F32))
            q, v, hg, ff, fb, y = (sb(n, [P, HEADS, T]) for n in ("h_q", "h_v", "h_g", "h_ff", "h_fb", "h_y"))
            projection_stage(g, g.dram["even_w_in"], [
                (3, "T", allt, lambda j: q[:, j], "silu"),
                (4, "N", allt, lambda j: v[:, j], "copy"),
                (5, "T", allt, lambda j: ff[:, j], "sigmoid"),
                (6, "T", allt, lambda j: fb[:, j], "sigmoid"),
                (7, "N", allt, lambda j: hg[:, j], "silu")], lambda _: AdaRows(g, 1, work, 2, (6, 7)))
            hgrn_stage(g, work, {"q": q[:], "v": v, "f": (ff[:], fb[:]), "y": y})
            norm_stage(g, y[:], allt, HEADS, False, hg[:], "hgrn_norm_w", 4, "h", w_out)
        residual_stage(g, 0, 0, allt, w_out)


def gates_wrapped(g, s):
    s["n_abs"] = 1 + 4 + 1
    s["n_rows"] = s["n_abs"] + 1 + 3 + 1 + 3 + 1
    gates_stage(g, s)


class HyenaFilters:
    TWO_PI = 2.0 * math.pi
    HI = float(np.float32(TWO_PI))
    LO = float(TWO_PI - np.float64(np.float32(TWO_PI)))
    MAGIC = 1.5 * 2.0 ** 23
    PI_F = float(np.float32(3.1415925))
    PER_LAYER = 7
    BANKS = (6, 7)
    OUTPUTS = {4: (0, 1, 2, 3), 5: (4, 5, 6, 7)}

    def __init__(self, g, ctx, filt, then):
        self.g, self.filt, self.then = g, filt, then
        sb = lambda n, shape: ctx.enter_context(g.nc.sbuf_tensor(f"hyf_{n}", shape, F32))
        self.z, self.w1, self.w23 = sb("z", [HYEMB, LAT]), sb("w1", [HYEMB, HYHID]), sb("w23", [HYHID, 2, HYHID])
        self.cols, self.wout, self.dec = sb("cols", [HYHID, 4]), sb("wout", [HYHID, 4, HYW]), sb("dec", [P, 2, 2, HYW])
        self.hid, self.x, self.r = sb("hid", [HYHID, LAT]), sb("x", [HYHID, LAT]), sb("r", [HYHID, LAT])
        self.loaded, self.made, self.stepped, self.sines, self.decayed = (new_sem(g, x) for x in (
            "hyf_loaded", "hyf_mm", "hyf_step", "hyf_sin", "hyf_decayed"))
        self.loads = [(self.z[:], "t_z"), (self.w1[:], "hy_w1"), (self.w23[:], "hy_w23"), (self.cols[:], "hy_cols"),
                      (self.wout[:], "hy_wout"), (self.dec[:], "t_decay")]
        self.link = None

    def load(self, eng):
        for dst, name in self.loads:
            src = self.g.dram[name]
            if name == "t_decay":
                src = src.rearrange("p (a b c) -> p a b c", a=2, b=2)
            eng.dma_start(dst, src).then_inc(self.loaded, 16)
        for prefetch in self.then:
            prefetch.start(eng)

    def pe(self, pe, n):
        nc = self.g.nc
        if n == 0:
            return
        if n <= 3:
            if n == 1:
                pe.wait_ge(self.loaded, 16 * len(self.loads))
            else:
                pe.wait_ge(self.sines, n - 1)
            w, x = (self.w1[:], self.z[:]) if n == 1 else (self.w23[:, n - 2], self.hid[:])
            nc.tensor.matmul(self.g.bank[self.BANKS[n % 2]][0:HYHID, 0:LAT], w, x, start=True, stop=True).then_inc(self.made, 1)
            return
        pe.wait_ge(self.sines, 3)
        for u in self.OUTPUTS.get(n, ()):
            q, i = u // 2, u % 2
            if u >= 2:
                pe.wait_ge(self.decayed, u - 1)
            nc.tensor.matmul(self.g.bank[self.BANKS[u % 2]][:], self.hid[:, i * P:(i + 1) * P], self.wout[:, q],
                             start=True, stop=True).then_inc(self.made, 1)

    def act(self, act, n):
        if 1 <= n <= 3:
            act.wait_ge(self.stepped, self.PER_LAYER * n)
            self.g.nc.scalar.activation(self.hid[:], self.x[:], ACT.Sin).then_inc(self.sines, 1)

    def dve(self, dve, n):
        nc, x, r, filt = self.g.nc, self.x, self.r, self.filt
        link = self.link = self.link or Chain(dve, self.stepped)
        if n == 0:
            return
        if n <= 3:
            dve.wait_ge(self.made, n)
            link(nc.vector.tensor_scalar(x[:], self.g.bank[self.BANKS[n % 2]][0:HYHID, 0:LAT], self.cols[:, n - 1:n], self.cols[:, 3:4], ALU.add, ALU.mult))
            link(nc.vector.tensor_scalar(r[:], x[:], 1.0 / self.TWO_PI, self.MAGIC, ALU.mult, ALU.add))
            link(nc.vector.tensor_scalar(r[:], r[:], -self.MAGIC, None, ALU.add))
            link(nc.vector.scalar_tensor_tensor(x[:], r[:], -self.HI, x[:], ALU.mult, ALU.add))
            link(nc.vector.scalar_tensor_tensor(x[:], r[:], -self.LO, x[:], ALU.mult, ALU.add))
            link(nc.vector.tensor_scalar(x[:], x[:], self.PI_F, None, ALU.min))
            link(nc.vector.tensor_scalar(x[:], x[:], -self.PI_F, None, ALU.max))
            return
        for u in self.OUTPUTS.get(n, ()):
            q, i = u // 2, u % 2
            dve.wait_ge(self.made, 3 + u + 1)
            nc.vector.tensor_tensor(filt[:, q // 2, q % 2, i], self.g.bank[self.BANKS[u % 2]][:], self.dec[:, q % 2, i], ALU.mult).then_inc(self.decayed, 1)
        if n == 5:
            dve.wait_ge(self.decayed, 8)
            for order in range(2):
                fwd, bwd = filt[:, order, 0], filt[:, order, 1]
                link(nc.vector.tensor_tensor(fwd, fwd, bwd, ALU.add))
                link(nc.vector.scalar_tensor_tensor(bwd, bwd, -2.0, fwd, ALU.mult, ALU.add))


def hyena_stage(g, u, filt, tables):
    nc = g.nc
    shifted, zeroed, step = (new_sem(g, x) for x in ("hy_shifted", "hy_zeroed", "hy_step"))
    uspec, kspec, kcopied, pointed, inv = (new_sem(g, x) for x in (
        "u_spectrum", "k_spectrum", "k_copied", "spec_ready", "conv_ready"))
    with ExitStack() as ctx:
        sb = lambda n, shape: ctx.enter_context(nc.sbuf_tensor(f"hy_{n}", shape, F32))
        HW = 3 * HYW
        prev, nxt = sb("prev", [P, 2, HW]), sb("next", [P, 2, HW])
        cw, skip = tables["conv"].tile, tables["skip"].tile
        dft = tables["dft"].tile[:].rearrange("p (d c i f) -> p d c i f", d=2, c=2, i=2)
        uf = u.rearrange("p i s c -> p i (s c)")
        ker = sb("ker", [P, 2, 2, 2, HYW])
        spec = sb("spec", [P, 2, 2, HYW])
        tmp = sb("tmp", [P, 2, HYW])
        z = u[:, :, 2]
        marks = {}
        with nc.Block() as block:
            @block.gpsimd
            def _(pool):
                pool.memset(prev[:, 0], 0.0).then_inc(zeroed, 1)
                pool.memset(nxt[:, 1], 0.0).then_inc(zeroed, 1)

            @block.sync
            def _(sp):
                sp.wait_ge(zeroed, 2)
                sp.dma_start(prev[1:P, 0], uf[0:P - 1, 0]).then_inc(shifted, 16)
                sp.dma_start(prev[0:1, 1], uf[P - 1:P, 0]).then_inc(shifted, 16)
                sp.dma_start(prev[1:P, 1], uf[0:P - 1, 1]).then_inc(shifted, 16)
                sp.dma_start(nxt[0:P - 1, 0], uf[1:P, 0]).then_inc(shifted, 16)
                sp.dma_start(nxt[P - 1:P, 0], uf[0:1, 1]).then_inc(shifted, 16)
                sp.dma_start(nxt[0:P - 1, 1], uf[1:P, 1]).then_inc(shifted, 16)

            @block.vector
            def _(dve):
                link = Chain(dve, step)

                def convolve(stream):
                    part = slice(stream * HYW, (stream + 1) * HYW)
                    for i in range(2):
                        link(nc.vector.tensor_tensor(uf[:, i, part], uf[:, i, part], cw[:, 1, part], ALU.mult))
                        link(nc.vector.tensor_tensor(prev[:, i, part], prev[:, i, part], cw[:, 0, part], ALU.mult))
                        link(nc.vector.tensor_tensor(nxt[:, i, part], nxt[:, i, part], cw[:, 2, part], ALU.mult))
                        link(nc.vector.tensor_tensor(uf[:, i, part], uf[:, i, part], prev[:, i, part], ALU.add))
                        link(nc.vector.tensor_tensor(uf[:, i, part], uf[:, i, part], nxt[:, i, part], ALU.add))
                        link(nc.vector.tensor_tensor(uf[:, i, part], uf[:, i, part], cw[:, 3, part], ALU.add))

                dve.wait_ge(tables["conv"].loaded, 16)
                dve.wait_ge(shifted, 96)
                convolve(2)
                marks["z", 0] = link.n
                dve.wait_ge(tables["skip"].loaded, 16)
                for order in range(2):
                    convolve(order)
                    for f in range(2):
                        dve.wait_ge(uspec, 2 * order + f + 1)
                        dve.wait_ge(kcopied, 4 * (order + 1))
                        uc, us = g.bank[4 + f][:], g.bank[6 + f][:]
                        kc, ks = ker[:, order, 0, f], ker[:, order, 1, f]
                        link(nc.vector.tensor_tensor(spec[:, 0, f], uc, kc, ALU.mult))
                        link(nc.vector.tensor_tensor(tmp[:, 0], us, ks, ALU.mult))
                        link(nc.vector.tensor_tensor(spec[:, 0, f], spec[:, 0, f], tmp[:, 0], ALU.subtract))
                        link(nc.vector.tensor_tensor(spec[:, 1, f], uc, ks, ALU.mult))
                        link(nc.vector.tensor_tensor(tmp[:, 1], us, kc, ALU.mult))
                        link(nc.vector.scalar_tensor_tensor(spec[:, 1, f], spec[:, 1, f], -1.0, tmp[:, 1], ALU.mult, ALU.subtract))
                        dve.sem_inc(pointed, 1)
                    for i in range(2):
                        link(nc.vector.tensor_tensor(z[:, i], z[:, i], skip[:, order], ALU.mult))
                        dve.wait_ge(inv, 2 * order + i + 1)
                        link(nc.vector.tensor_tensor(z[:, i], z[:, i], g.bank[i][:], ALU.add))
                        link(nc.vector.tensor_tensor(z[:, i], z[:, i], u[:, i, order], ALU.mult))
                    marks["z", order + 1] = link.n

            @block.tensor
            def _(pe):
                pe.wait_ge(tables["dft"].loaded, 16)
                for order in range(2):
                    for c in range(2):
                        for f in range(2):
                            for i in range(2):
                                last = nc.tensor.matmul(g.bank[4 * order + 2 * c + f][:], dft[:, 0, c, i, f * P:(f + 1) * P],
                                                        filt[:, order, c, i], start=i == 0, stop=i == 1)
                            last.then_inc(kspec, 1)
                for order in range(2):
                    if order == 0:
                        pe.wait_ge(kcopied, 8)
                    pe.wait_ge(step, marks["z", order])
                    for f in range(2):
                        for c in range(2):
                            for i in range(2):
                                last = nc.tensor.matmul(g.bank[4 + 2 * c + f][:], dft[:, 0, c, i, f * P:(f + 1) * P], z[:, i],
                                                        start=i == 0, stop=i == 1)
                        last.then_inc(uspec, 1)
                    for f in range(2):
                        pe.wait_ge(pointed, 2 * order + f + 1)
                        for i in range(2):
                            for c in range(2):
                                last = nc.tensor.matmul(g.bank[i][:], dft[:, 1, c, f, i * P:(i + 1) * P], spec[:, c, f],
                                                        start=f == 0 and c == 0, stop=f == 1 and c == 1)
                            if f == 1:
                                last.then_inc(inv, 1)

            @block.scalar
            def _(act):
                for order in range(2):
                    for c in range(2):
                        for f in range(2):
                            act.wait_ge(kspec, 4 * order + 2 * c + f + 1)
                            nc.scalar.activation(ker[:, order, c, f], g.bank[4 * order + 2 * c + f][:], ACT.Copy).then_inc(kcopied, 1)


class RetentionSide:
    def __init__(self, g, work, decays, q, k):
        self.g, self.decays = g, decays
        self.turns = {6: (q[:, 0], 0, 0), 7: (q[:, 1], 1, 1), 8: (k[:, 2], 0, 4), 9: (k[:, 3], 1, 5)}
        size = 2 * NT * LAT
        at = 2 * size + 4 * LAT + 2 * HEADS
        self.tab = work[:, at:at + 4 * P].rearrange("p (c i d) -> p c i d", c=2, i=2)
        self.rot = work[:, at + 4 * P:at + 4 * P + 512]
        self.rope_loaded = new_sem(g, "rope_loaded")
        self.delta, self.back = (work[:, i * size:(i + 1) * size].rearrange("p (d j t) -> p d j t", d=2, j=NT) for i in range(2))
        self.keep = work[:, 2 * size:2 * size + 4 * LAT].rearrange("p (d j t) -> p d j t", d=2, j=2)
        self.lg = work[:, 2 * size + 4 * LAT:2 * size + 4 * LAT + 2 * HEADS].rearrange("p (d h) -> p d h", d=2)
        self.loaded, self.exped, self.stepped = (new_sem(g, x) for x in ("ret_loaded", "ret_exp", "ret_step"))
        self.link = None

    def load(self, eng):
        eng.dma_start(self.delta, self.g.dram["t_delta"].rearrange("p (d j t) -> p d j t", d=2, j=NT)).then_inc(self.loaded, 16)
        eng.dma_start(self.keep, self.g.dram["t_keep"].rearrange("p (d j t) -> p d j t", d=2, j=2)).then_inc(self.loaded, 16)
        eng.dma_start(self.lg, self.g.dram["ret_lg"]).then_inc(self.loaded, 16)
        eng.dma_start(self.tab, self.g.dram["t_rope"].rearrange("p (c i d) -> p c i d", c=2, i=2)).then_inc(self.rope_loaded, 16)

    def pe(self, pe, n):
        pass

    def act(self, act, h):
        if h >= HEADS:
            return
        if h == 0:
            act.wait_ge(self.loaded, 48)
        if h >= 2:
            act.wait_ge(self.stepped, 3 * (h - 1))
        for d, dst in enumerate((self.decays[:, h], self.back[:, h % 2])):
            self.g.nc.scalar.activation(dst, self.delta[:, d], ACT.Exp, scale=self.lg[:, d, h:h + 1]).then_inc(self.exped, 1)

    def rotate(self, dve, src, i, output):
        nc, link = self.g.nc, self.link
        if output == 0:
            dve.wait_ge(self.rope_loaded, 16)
        dve.wait_ge(*self.emptied[output])
        for h in range(HEADS):
            xs = src[:, h * P:(h + 1) * P].rearrange("p (a b c) -> p a b c", a=2, b=2)
            rs = self.rot[:, h * P:(h + 1) * P].rearrange("p (a b c) -> p a b c", a=2, b=2)
            sn = self.tab[:, 1, i].rearrange("p (a b c) -> p a b c", a=2, b=2)
            for b in range(2):
                link(nc.vector.tensor_tensor(rs[:, :, b], xs[:, :, 1 - b], sn[:, :, b], ALU.mult))
        cos = self.tab[:, 0, i].unsqueeze(1).broadcast_to([P, HEADS, P])
        s3 = src.rearrange("p (h d) -> p h d", h=HEADS)
        link(nc.vector.tensor_tensor(s3, s3, cos, ALU.mult))
        link(nc.vector.tensor_tensor(src, src, self.rot, ALU.add))

    def dve(self, dve, h):
        if h in self.turns:
            self.rotate(dve, *self.turns[h])
        if h >= HEADS:
            return
        nc, link = self.g.nc, self.link or Chain(dve, self.stepped)
        self.link = link
        if h == 0:
            dve.wait_ge(self.loaded, 48)
        dve.wait_ge(self.exped, 2 * (h + 1))
        ef, eb = self.decays[:, h], self.back[:, h % 2]
        link(nc.vector.tensor_tensor(ef[:, 2:4], ef[:, 2:4], self.keep[:, 0], ALU.mult))
        link(nc.vector.tensor_tensor(eb[:, 2:4], eb[:, 2:4], self.keep[:, 1], ALU.mult))
        link(nc.vector.tensor_tensor(ef, ef, eb, ALU.add))


def retention_stage(g, q, k, v, y, e):
    nc = g.nc
    turned, copied, scored, weighted, summed, ycopied = (new_sem(g, x) for x in (
        "qk_turned", "qk_copied", "ret_scored", "ret_weighted", "ret_summed", "ret_copied"))
    with ExitStack() as ctx:
        sb = lambda n, shape: ctx.enter_context(nc.sbuf_tensor(f"ret_{n}", shape, F32))
        qT, kT = sb("qT", [P, HEADS, LAT]), sb("kT", [P, HEADS, T])
        with nc.Block() as block:
            def values(pe, h):
                pe.wait_ge(weighted, NT * (h + 1))
                if h >= 2:
                    pe.wait_ge(ycopied, h - 1)
                for i in range(2):
                    for j in range(NT):
                        last = nc.tensor.matmul(g.bank[4 + h % 2][:, i * P:(i + 1) * P], e[:, h, j, i * P:(i + 1) * P],
                                                v[:, j, h * P:(h + 1) * P], start=j == 0, stop=j == NT - 1)
                last.then_inc(summed, 1)

            def finish(dve, h):
                dve.wait_ge(summed, h + 1)
                nc.vector.tensor_copy(y[:, :, h * P:(h + 1) * P], g.bank[4 + h % 2][:, 0:LAT].rearrange("p (i d) -> p i d", i=2)).then_inc(ycopied, 1)

            @block.tensor
            def _(pe):
                for h in range(HEADS):
                    if h >= 2:
                        pe.wait_ge(copied, 2 * (h - 1))
                    b = g.bank[2 * (h % 2)]
                    for i in range(2):
                        last = nc.tensor.transpose(b[:, i * P:(i + 1) * P], q[:, i, h * P:(h + 1) * P], g.ident)
                    last.then_inc(turned, 1)
                    b = g.bank[2 * (h % 2) + 1]
                    for i in range(NT):
                        last = nc.tensor.transpose(b[:, i * P:(i + 1) * P], k[:, i, h * P:(h + 1) * P], g.ident)
                    last.then_inc(turned, 1)
                pe.wait_ge(copied, 2 * HEADS)
                for h in range(HEADS):
                    if h >= 2:
                        pe.wait_ge(weighted, NT * (h - 1))
                    for j in range(NT):
                        nc.tensor.matmul(g.bank[2 * (h % 2) + j // 2][:, (j % 2) * LAT:(j % 2 + 1) * LAT], kT[:, h, j * P:(j + 1) * P], qT[:, h],
                                         start=True, stop=True).then_inc(scored, 1)
                    if h >= 1:
                        values(pe, h - 1)
                values(pe, HEADS - 1)

            @block.scalar
            def _(act):
                for h in range(HEADS):
                    act.wait_ge(turned, 2 * h + 1)
                    nc.scalar.activation(qT[:, h], g.bank[2 * (h % 2)][:, 0:LAT], ACT.Copy, scale=float(P) ** -0.5).then_inc(copied, 1)
                    act.wait_ge(turned, 2 * h + 2)
                    nc.scalar.activation(kT[:, h], g.bank[2 * (h % 2) + 1][:], ACT.Copy).then_inc(copied, 1)

            @block.vector
            def _(dve):
                for h in range(HEADS):
                    for j in range(NT):
                        dve.wait_ge(scored, h * NT + j // 2 * 2 + 2)
                        nc.vector.tensor_tensor(e[:, h, j], e[:, h, j], g.bank[2 * (h % 2) + j // 2][:, (j % 2) * LAT:(j % 2 + 1) * LAT], ALU.mult).then_inc(weighted, 1)
                    if h >= 1:
                        finish(dve, h - 1)
                finish(dve, HEADS - 1)


def odd_layer(g):
    nc = g.nc
    ada_columns_stage(g, 1)
    allt, lat = list(range(NT)), [2, 3]
    with ExitStack() as ctx:
        g.mix = ctx.enter_context(nc.sbuf_tensor("mix1", [P, KT, T], F32))
        with ExitStack() as c2:
            sb = lambda n, shape: c2.enter_context(nc.sbuf_tensor(n, shape, F32))
            u, filt = sb("hy_u", [P, 2, 3, HYW]), sb("hy_filt", [P, 2, 2, 2, HYW])
            tables = {name: Prefetch(g, c2, f"hy_{name}", shape, g.dram[source]) for name, shape, source in (
                ("conv", [P, 4, 3 * HYW], "hy_conv"), ("dft", [P, 8 * LAT], "t_dft"), ("skip", [P, 2, HYW], "hy_skip"))}
            with ExitStack() as c3:
                w_in = InputWeights(g, c3, g.dram["odd_w_in"], [0, 1, 2])
                modulate_stage(g, 1, 0, 1, allt, 2, w_in)
                projection_stage(g, g.dram["odd_w_in"], [
                    (i, "N", lat, (lambda i: lambda j: u[:, j, i])(i), "copy") for i in range(3)],
                    lambda ctx: HyenaFilters(g, ctx, filt, tables.values()), prefetched=w_in)
            hyena_stage(g, u[:], filt, tables)
            norm_stage(g, u[:, :, 2], lat, HYW // GROUP, False, None, "hy_norm_w", 0, "y")
        w_out = Prefetch(g, ctx, "w_out1", [P, KT, D], g.dram["odd_w_out"])
        with ExitStack() as c2:
            sb = lambda n, shape: c2.enter_context(nc.sbuf_tensor(n, shape, F32))
            q, k, v, rg, y = (sb(n, [P, w, 512]) for n, w in (("r_q", 2), ("r_k", 4), ("r_v", 4), ("r_g", 2), ("r_y", 2)))
            decays = sb("r_decays", [P, HEADS, NT, LAT])
            projection_stage(g, g.dram["odd_w_in"], [
                (3, "N", lat, lambda j: q[:, j], "copy"),
                (4, "N", allt, lambda j: k[:, j], "copy"),
                (5, "N", allt, lambda j: v[:, j], "copy"),
                (6, "N", lat, lambda j: rg[:, j], "silu")], lambda _: RetentionSide(g, w_out.tile[:].rearrange("p k d -> p (k d)"), decays, q, k))
            retention_stage(g, q, k, v, y, decays)
            norm_stage(g, y[:], lat, HEADS, True, rg[:], "ret_norm_w", 4, "r", w_out)
        residual_stage(g, 1, 0, lat, w_out)


def build(nc, dram, out):
    g = Net()
    g.nc, g.dram, g.n_sems, g.sems = nc, dram, 0, []
    with ExitStack() as ctx:
        sb = lambda n, shape: ctx.enter_context(nc.sbuf_tensor(n, shape, F32))
        g.h = sb("h", [P, NT, D])
        g.xt = sb("xt", [P, KT, T])
        c0 = 5 * P + P // CHUNK
        g.base = sb("base", [P, c0 + EXPERTS + 1 + P])
        g.c_cols, g.c_act = sb("c_cols", [P, KT, 2]), sb("c_act", [P, KT, 2])
        g.mods = sb("mods", [P, 2, MODS * KT, 2])
        g.mod_row = sb("mod_row", [P, 2, D])
        g.ident, g.upper, g.lower = (g.base[:, i * P:(i + 1) * P] for i in range(3))
        g.tri_chunk = [g.base[:, (3 + i) * P:(4 + i) * P] for i in range(2)]
        g.chunk_of = g.base[:, 5 * P:c0]
        g.iota_e, g.pcol = g.base[:, c0:c0 + EXPERTS], g.base[:, c0 + EXPERTS:c0 + EXPERTS + 1]
        g.ones = g.base[:, c0 + EXPERTS + 1:]
        g.bank = [ctx.enter_context(nc.psum_tensor(f"bank{i}", [P, 512], F32)) for i in range(8)]
        g.y_dram = nc.dram_tensor("y_slots", (MAX_BLOCKS, SB, D), F32, kind="Internal").ap()
        g.y_cleared = nc.alloc_semaphore("y_cleared")
        g.zero_row = sb("zero_row", [P, D])
        g.ada_rows = sb("ada_rows", [P, 3, 512])
        load_stage(g)
        ada_rows_stage(g, 0)
        even_layer(g)
        recycle_sems(g)
        moe(g, 0, list(range(NT)))
        recycle_sems(g)
        odd_layer(g)
        recycle_sems(g)
        moe(g, 1, [2, 3])
        stored = new_sem(g, "out_stored")
        with nc.Block() as block:
            @block.sync
            def _(sp):
                sp.dma_start(out.rearrange("b (i p) d -> p (b i) d", p=P), g.h[:, 2:4]).then_inc(stored, 16)
                sp.wait_ge(stored, 16)


def layout(i):
    i = {k: np.asarray(v) for k, v in i.items()}
    L = 2
    a = dict(shape_tables())
    tok = np.concatenate([i["ctx"][0], i["x"][0]], 0)
    a["x_all"] = tok.reshape(NT, P, D).transpose(1, 0, 2)
    a["c_cols"] = np.stack([i["c"][0], i["c_ctx"]]).reshape(2, KT, P).transpose(2, 1, 0)
    a["ada_w"] = i["ada_w"].reshape(L, 4, 2, P, 3, 2048).transpose(0, 4, 1, 3, 2, 5)
    a["ada_b"] = i["ada_b"].reshape(L, MODS * KT, P).transpose(0, 2, 1)
    ln = np.stack([i["ln_w"], i["ln_b"]], 2)
    a["ln_rows"] = np.broadcast_to(ln[:, :, None], (L, 2, P, 2, D))
    we = i["even_w_in"][0]
    groups, gates = np.concatenate([we[:, :1536], we[:, 1552:]], 1), we[:, 1536:1552]
    a["even_w_in"] = groups.reshape(KT, P, 8, 512).transpose(2, 1, 0, 3)
    a["w_gates"] = gates.reshape(KT, P, 16).transpose(1, 0, 2)
    a["gate_b"] = i["mlstm_gate_b"][0].T
    a["odd_w_in"] = i["odd_w_in"][0].reshape(KT, P, 7, 512).transpose(2, 1, 0, 3)
    for n in ("even_w_out", "odd_w_out"):
        a[n] = i[n][0].reshape(KT, P, D).transpose(1, 0, 2)
    for n in ("mlstm_norm_w", "hgrn_norm_w", "ret_norm_w", "hy_norm_w"):
        a[n] = np.broadcast_to(i[n][0][None], (P, 512))
    a["lb_cols"] = i["hgrn_lb"][0].reshape(HEADS, P).T
    a["hy_conv"] = np.broadcast_to(np.concatenate([i["hy_conv_w"][0], i["hy_conv_b"]], 0)[None], (P, 4, 3 * HYW))
    a["hy_w1"] = i["hy_f_w1"][0]
    a["hy_w23"] = np.stack([i["hy_f_w2"][0], i["hy_f_w3"][0]], 1)
    a["hy_cols"] = np.stack([i["hy_f_b1"][0], i["hy_f_b2"][0], i["hy_f_b3"][0], i["hy_f_freq"][0]], 1)
    a["hy_wout"] = i["hy_f_wout"][0].reshape(HYHID, 4, HYW)
    a["hy_skip"] = np.broadcast_to(i["hy_skip"][0][None], (P, 2, HYW))
    a["ret_lg"] = np.broadcast_to(i["ret_log_decay"][0][None], (P, 2, HEADS))
    a["router_w"] = i["router_w"].reshape(L, KT, P, EXPERTS).transpose(0, 2, 1, 3)
    a["router_b"] = np.broadcast_to(i["router_bias"][:, None], (L, P, EXPERTS))

    def expert_rows(w1, w3, w2):
        n = w1.shape[:-2]
        up = np.stack([w1.reshape(*n, D, 2, P), w3.reshape(*n, D, 2, P)], -2).reshape(*n, KT, P, 2 * HID).swapaxes(-3, -2).reshape(*n, P, W13)
        down = w2.reshape(*n, 2, P, D).swapaxes(-3, -2).reshape(*n, P, 2 * D)
        return np.concatenate([up, down], -1)
    routed = expert_rows(i["exp_w1"], i["exp_w3"], i["exp_w2"])
    shared = expert_rows(i["sh_w1"], i["sh_w3"], i["sh_w2"])[:, None]
    a["experts"] = np.concatenate([shared, routed, ], 1).reshape(L * (EXPERTS + 1), P, WEXP)
    return {k: np.ascontiguousarray(v) for k, v in a.items()}


def kernel(**inputs):
    import concourse.bacc as bacc
    from concourse.bass_utils import run_bass_kernel_spmd

    nc = bacc.Bacc("TRN2", target_bir_lowering=False, num_devices=1)
    arrays = {f"in_{k}": v for k, v in layout(inputs).items()}
    dram = {k[3:]: nc.dram_tensor(k, v.shape, F32, kind="ExternalInput").ap() for k, v in arrays.items()}
    out = nc.dram_tensor("out", (1, LAT, D), F32, kind="ExternalOutput").ap()
    build(nc, dram, out)
    return run_bass_kernel_spmd(nc, [arrays], core_ids=[0]).results[0]["out"]
```
